# Optimizing a Trainium2 kernel written in Bass

```python
import math
import jax, jax.numpy as jnp
from jax import lax
import numpy as np

D_MODEL = 1024
BATCH = 1
SEQ = 512
DEPTH = 2

N_MIXERS = 2
N_MLA_LAYERS = (DEPTH + N_MIXERS - 1) // N_MIXERS
N_HYENA_LAYERS = DEPTH // N_MIXERS

MLA_HEADS = 8
Q_LORA = 256
KV_LORA = 128
QK_NOPE = 128
QK_ROPE = 64
QK_HEAD = QK_NOPE + QK_ROPE
V_HEAD = 128
ROPE_HALF = QK_ROPE // 2
ROPE_THETA = 10000.0
Q_BLOCK = 128

HYENA_ORDER = 2
SHORT_CONV = 3
FILTER_EMB = 33
FILTER_BANDS = (FILTER_EMB - 1) // 2
FILTER_WIDTH = 64
FAST_DECAY = 0.3
SLOW_DECAY = 1.5
DECAY_TARGET = 1e-2

N_GROUPS = 4
EXPERTS_PER_GROUP = 4
N_EXPERTS = N_GROUPS * EXPERTS_PER_GROUP
TOP_K = 2
D_EXPERT = 256

EPS = 1e-6


def rms_norm(x, g):
    xf = x.astype(jnp.float32)
    y = xf * lax.rsqrt(jnp.mean(xf * xf, axis=-1, keepdims=True) + EPS)
    return (y * g.astype(jnp.float32)).astype(x.dtype)

def modulate(h, shift, scale):
    return h * (1 + scale[:, None, :]) + shift[:, None, :]

def rope_tables(positions):
    inv_freq = 1.0 / (ROPE_THETA ** (jnp.arange(0, QK_ROPE, 2, dtype=jnp.float32) / QK_ROPE))
    ang = positions.astype(jnp.float32)[..., None] * inv_freq
    return jnp.cos(ang), jnp.sin(ang)

def apply_rope(x, cos, sin):
    xf = x.astype(jnp.float32)
    x1, x2 = xf[..., :ROPE_HALF], xf[..., ROPE_HALF:]
    return jnp.concatenate([x1 * cos - x2 * sin, x1 * sin + x2 * cos], axis=-1).astype(x.dtype)

def mla_mixer(h, cos, sin, w_down, q_a_g, kv_a_g, w_uq, w_ukv, q_norm_g, k_norm_g, w_o):
    B, S, _ = h.shape
    lat = h @ w_down
    c_q = lat[..., :Q_LORA]
    c_kv = lat[..., Q_LORA:Q_LORA + KV_LORA]
    k_pe = lat[..., Q_LORA + KV_LORA:]
    q = (rms_norm(c_q, q_a_g) @ w_uq).reshape(B, S, MLA_HEADS, QK_HEAD)
    kv = (rms_norm(c_kv, kv_a_g) @ w_ukv).reshape(B, S, MLA_HEADS, QK_NOPE + V_HEAD)
    cos_h, sin_h = cos[:, :, None, :], sin[:, :, None, :]
    q_nope = rms_norm(q[..., :QK_NOPE], q_norm_g[:QK_NOPE])
    q_pe = apply_rope(rms_norm(q[..., QK_NOPE:], q_norm_g[QK_NOPE:]), cos_h, sin_h)
    k_nope = rms_norm(kv[..., :QK_NOPE], k_norm_g[:QK_NOPE])
    k_pe = apply_rope(rms_norm(k_pe, k_norm_g[QK_NOPE:]), cos, sin)
    v = kv[..., QK_NOPE:]
    q = jnp.concatenate([q_nope, q_pe], axis=-1)
    k = jnp.concatenate([k_nope, jnp.broadcast_to(k_pe[:, :, None, :], (B, S, MLA_HEADS, QK_ROPE))], axis=-1)
    scale = QK_HEAD ** -0.5
    n_blk = S // Q_BLOCK
    q_blocks = q.reshape(B, n_blk, Q_BLOCK, MLA_HEADS, QK_HEAD).transpose(1, 0, 2, 3, 4)

    def attend(q_blk):
        s = jnp.einsum('bqhd,bkhd->bhqk', q_blk, k, preferred_element_type=jnp.float32) * scale
        p = jax.nn.softmax(s, axis=-1).astype(v.dtype)
        return jnp.einsum('bhqk,bkhd->bqhd', p, v)

    o = lax.map(attend, q_blocks)
    o = o.transpose(1, 0, 2, 3, 4).reshape(B, S, MLA_HEADS * V_HEAD)
    return o @ w_o

def hyena_filters(L, w1, b1, f1, w2, b2, f2, w3, b3, f3, w4):
    f32 = jnp.float32
    t = jnp.linspace(0.0, 1.0, L, dtype=f32)[:, None]
    w = 2.0 * math.pi * jnp.arange(L, dtype=f32)[:, None] / L
    fr = jnp.linspace(1e-4, FILTER_BANDS - 1, FILTER_BANDS, dtype=f32)[None, :]
    z = jnp.concatenate([t, jnp.cos(fr * w), -jnp.sin(fr * w)], axis=-1)
    hdn = jnp.sin(f1.astype(f32) * (z @ w1.astype(f32) + b1.astype(f32)))
    hdn = jnp.sin(f2.astype(f32) * (hdn @ w2.astype(f32) + b2.astype(f32)))
    hdn = jnp.sin(f3.astype(f32) * (hdn @ w3.astype(f32) + b3.astype(f32)))
    h = (hdn @ w4.astype(f32)).reshape(L, HYENA_ORDER, 2, D_MODEL)
    deltas = jnp.abs(jnp.linspace(math.log(FAST_DECAY) / DECAY_TARGET,
                                  math.log(SLOW_DECAY) / DECAY_TARGET, D_MODEL, dtype=f32))
    decay = jnp.exp(-t * deltas)
    h = h * decay[:, None, None, :]
    return h / (jnp.sum(jnp.abs(h), axis=0, keepdims=True) + EPS)

def bidir_long_conv(u, h_fwd, h_bwd, bias):
    B, L, D = u.shape
    k2 = jnp.concatenate([h_fwd, jnp.zeros((1, D), jnp.float32), h_bwd[:0:-1]], axis=0)
    k_f = jnp.fft.rfft(k2, axis=0)
    u_f = jnp.fft.rfft(u.astype(jnp.float32), n=2 * L, axis=1)
    y = jnp.fft.irfft(u_f * k_f[None], n=2 * L, axis=1)[:, :L]
    return (y + u.astype(jnp.float32) * bias.astype(jnp.float32)).astype(u.dtype)

def hyena_mixer(h, w_in, b_in, conv_w, conv_b, f_w1, f_b1, f_freq1, f_w2, f_b2, f_freq2,
                f_w3, f_b3, f_freq3, f_w4, filt_bias, w_out):
    B, L, _ = h.shape
    C = 3 * D_MODEL
    u = h @ w_in + b_in
    u = lax.conv_general_dilated(u, conv_w[:, None, :].astype(u.dtype), window_strides=(1,),
                                 padding=((SHORT_CONV // 2, SHORT_CONV // 2),),
                                 dimension_numbers=('NWC', 'WIO', 'NWC'),
                                 feature_group_count=C) + conv_b
    x1, x2, v = jnp.split(u, 3, axis=-1)
    filt = hyena_filters(L, f_w1, f_b1, f_freq1, f_w2, f_b2, f_freq2, f_w3, f_b3, f_freq3, f_w4)
    z = v
    for o, gate in enumerate((x1, x2)):
        z = gate * bidir_long_conv(z, filt[:, o, 0], filt[:, o, 1], filt_bias[o])
    return z @ w_out

def hier_moe(h, wg, bg, we, be, w_gate, w_up, w_down):
    B, S, D = h.shape
    t = h.reshape(B * S, D)
    T = t.shape[0]
    g_prob = jax.nn.softmax((t @ wg).astype(jnp.float32) + bg.astype(jnp.float32), axis=-1)
    g_w, g_idx = lax.top_k(g_prob, 1)
    e_logits = ((t @ we).astype(jnp.float32) + be.astype(jnp.float32)).reshape(T, N_GROUPS, EXPERTS_PER_GROUP)
    e_logits = jnp.take_along_axis(e_logits, g_idx[:, :, None], axis=1)[:, 0]
    e_w, e_idx = lax.top_k(jax.nn.softmax(e_logits, axis=-1), TOP_K)
    weights = g_w * (e_w / jnp.sum(e_w, axis=-1, keepdims=True))
    expert = g_idx * EXPERTS_PER_GROUP + e_idx
    combine = jnp.sum(jax.nn.one_hot(expert, N_EXPERTS, dtype=jnp.float32) * weights[..., None], axis=1)
    combine = combine.astype(t.dtype)
    out = jnp.zeros_like(t)
    for e in range(N_EXPERTS):
        a = jax.nn.silu(t @ w_gate[e]) * (t @ w_up[e])
        out = out + combine[:, e:e + 1] * (a @ w_down[e])
    return out.reshape(B, S, D)

def first_inputs(seed: int = 0) -> dict:
    key = jax.random.key(seed)
    ks = iter(jax.random.split(key, 64))
    D = D_MODEL
    NA, NH = N_MLA_LAYERS, N_HYENA_LAYERS

    def nrm(shape, scale):
        return jax.random.normal(next(ks), shape, jnp.float32) * scale

    def gain(shape):
        return 1.0 + nrm(shape, 0.02)

    x = nrm((BATCH, SEQ, D), 1.0)
    c = nrm((BATCH, D), 1.0)
    offs = jax.random.randint(next(ks), (BATCH, 1), 0, 1024, dtype=jnp.int32)
    positions = offs + jnp.arange(SEQ, dtype=jnp.int32)[None, :]
    return {
        "x": x, "c": c, "positions": positions,
        "ada_w": nrm((DEPTH, D, 6 * D), 0.5 * D ** -0.5),
        "ada_b": nrm((DEPTH, 6 * D), 0.02),
        "norm_mix_g": gain((DEPTH, D)),
        "norm_ffn_g": gain((DEPTH, D)),
        "mla_w_down": nrm((NA, D, Q_LORA + KV_LORA + QK_ROPE), D ** -0.5),
        "mla_q_a_g": gain((NA, Q_LORA)),
        "mla_kv_a_g": gain((NA, KV_LORA)),
        "mla_w_uq": nrm((NA, Q_LORA, MLA_HEADS * QK_HEAD), Q_LORA ** -0.5),
        "mla_w_ukv": nrm((NA, KV_LORA, MLA_HEADS * (QK_NOPE + V_HEAD)), KV_LORA ** -0.5),
        "mla_q_norm_g": gain((NA, QK_HEAD)),
        "mla_k_norm_g": gain((NA, QK_HEAD)),
        "mla_w_o": nrm((NA, MLA_HEADS * V_HEAD, D), (MLA_HEADS * V_HEAD) ** -0.5),
        "hy_w_in": nrm((NH, D, 3 * D), D ** -0.5),
        "hy_b_in": nrm((NH, 3 * D), 0.02),
        "hy_conv_w": nrm((NH, SHORT_CONV, 3 * D), SHORT_CONV ** -0.5),
        "hy_conv_b": nrm((NH, 3 * D), 0.02),
        "hy_f_w1": nrm((NH, FILTER_EMB, FILTER_WIDTH), FILTER_EMB ** -0.5),
        "hy_f_b1": nrm((NH, FILTER_WIDTH), 0.1),
        "hy_f_freq1": gain((NH, FILTER_WIDTH)),
        "hy_f_w2": nrm((NH, FILTER_WIDTH, FILTER_WIDTH), FILTER_WIDTH ** -0.5),
        "hy_f_b2": nrm((NH, FILTER_WIDTH), 0.1),
        "hy_f_freq2": gain((NH, FILTER_WIDTH)),
        "hy_f_w3": nrm((NH, FILTER_WIDTH, FILTER_WIDTH), FILTER_WIDTH ** -0.5),
        "hy_f_b3": nrm((NH, FILTER_WIDTH), 0.1),
        "hy_f_freq3": gain((NH, FILTER_WIDTH)),
        "hy_f_w4": nrm((NH, FILTER_WIDTH, HYENA_ORDER * 2 * D), FILTER_WIDTH ** -0.5),
        "hy_filt_bias": nrm((NH, HYENA_ORDER, D), 1.0),
        "hy_w_out": nrm((NH, D, D), D ** -0.5),
        "moe_wg": nrm((DEPTH, D, N_GROUPS), D ** -0.5),
        "moe_bg": nrm((DEPTH, N_GROUPS), 0.01),
        "moe_we": nrm((DEPTH, D, N_EXPERTS), D ** -0.5),
        "moe_be": nrm((DEPTH, N_EXPERTS), 0.01),
        "moe_w_gate": nrm((DEPTH, N_EXPERTS, D, D_EXPERT), D ** -0.5),
        "moe_w_up": nrm((DEPTH, N_EXPERTS, D, D_EXPERT), D ** -0.5),
        "moe_w_down": nrm((DEPTH, N_EXPERTS, D_EXPERT, D), D_EXPERT ** -0.5),
    }

def first_block(x, c, positions, ada_w, ada_b, norm_mix_g, norm_ffn_g,
              mla_w_down, mla_q_a_g, mla_kv_a_g, mla_w_uq, mla_w_ukv, mla_q_norm_g, mla_k_norm_g, mla_w_o,
              hy_w_in, hy_b_in, hy_conv_w, hy_conv_b,
              hy_f_w1, hy_f_b1, hy_f_freq1, hy_f_w2, hy_f_b2, hy_f_freq2,
              hy_f_w3, hy_f_b3, hy_f_freq3, hy_f_w4, hy_filt_bias, hy_w_out,
              moe_wg, moe_bg, moe_we, moe_be, moe_w_gate, moe_w_up, moe_w_down):
    cos, sin = rope_tables(positions)
    c_act = jax.nn.silu(c.astype(jnp.float32))
    for i in range(DEPTH):
        mod = (c_act @ ada_w[i].astype(jnp.float32) + ada_b[i].astype(jnp.float32)).astype(x.dtype)
        sh1, sc1, g1, sh2, sc2, g2 = jnp.split(mod, 6, axis=-1)
        h = modulate(rms_norm(x, norm_mix_g[i]), sh1, sc1)
        j = i // N_MIXERS
        if i % N_MIXERS == 0:
            y = mla_mixer(h, cos, sin, mla_w_down[j], mla_q_a_g[j], mla_kv_a_g[j], mla_w_uq[j],
                          mla_w_ukv[j], mla_q_norm_g[j], mla_k_norm_g[j], mla_w_o[j])
        else:
            y = hyena_mixer(h, hy_w_in[j], hy_b_in[j], hy_conv_w[j], hy_conv_b[j],
                            hy_f_w1[j], hy_f_b1[j], hy_f_freq1[j], hy_f_w2[j], hy_f_b2[j], hy_f_freq2[j],
                            hy_f_w3[j], hy_f_b3[j], hy_f_freq3[j], hy_f_w4[j], hy_filt_bias[j], hy_w_out[j])
        x = x + g1[:, None, :] * y
        h = modulate(rms_norm(x, norm_ffn_g[i]), sh2, sc2)
        x = x + g2[:, None, :] * hier_moe(h, moe_wg[i], moe_bg[i], moe_we[i], moe_be[i],
                                          moe_w_gate[i], moe_w_up[i], moe_w_down[i])
    return x


MIX_WIDTH = D_MODEL // 2
RET_HEADS = 4
RET_V_DIM = MIX_WIDTH // RET_HEADS
RET_QK_DIM = RET_V_DIM // 2
RET_CHUNK = 128
SC_WIDTH = MIX_WIDTH
SC_KERNEL = 3
CF_WIDTH = MIX_WIDTH
CF_KERNEL = 31
N_BRANCH = 3
D_FF = int(round(8 * D_MODEL / 3 / 256)) * 256
FFN_KERNEL = 3
ROPE_BASE = 10000.0

IN_SIZES = [RET_HEADS * RET_QK_DIM, RET_HEADS * RET_QK_DIM, MIX_WIDTH, MIX_WIDTH,
            SC_WIDTH, SC_WIDTH, SC_WIDTH, CF_WIDTH, CF_WIDTH, N_BRANCH * D_MODEL]
IN_WIDTH = sum(IN_SIZES)


def rmsnorm(x, g):
    xf = x.astype(jnp.float32)
    y = xf * lax.rsqrt(jnp.mean(xf * xf, axis=-1, keepdims=True) + EPS)
    return (y * g.astype(jnp.float32)).astype(x.dtype)

def layernorm(x, g, b):
    xf = x.astype(jnp.float32)
    mu = jnp.mean(xf, axis=-1, keepdims=True)
    xc = xf - mu
    y = xc * lax.rsqrt(jnp.mean(xc * xc, axis=-1, keepdims=True) + EPS)
    return (y * g.astype(jnp.float32) + b.astype(jnp.float32)).astype(x.dtype)

def causal_dwconv(x, w, b=None):
    K, C = w.shape
    xp = jnp.pad(x, ((0, 0), (K - 1, 0), (0, 0)))
    y = lax.conv_general_dilated(xp, w.astype(x.dtype)[:, None, :], window_strides=(1,),
                                 padding='VALID', dimension_numbers=('NWC', 'WIO', 'NWC'),
                                 feature_group_count=C)
    if b is not None:
        y = y + b.astype(x.dtype)
    return y

def rotary(x, pos):
    half = x.shape[-1] // 2
    inv = ROPE_BASE ** (-jnp.arange(half, dtype=jnp.float32) / half)
    ang = pos.astype(jnp.float32)[:, None] * inv[None, :]
    cos = jnp.cos(ang)[None, :, None, :]
    sin = jnp.sin(ang)[None, :, None, :]
    x1, x2 = x[..., :half], x[..., half:]
    return jnp.concatenate([x1 * cos - x2 * sin, x2 * cos + x1 * sin], axis=-1)

def retention_chunkwise(q, k, v):
    B, S, H, dk = q.shape
    dv = v.shape[-1]
    C = RET_CHUNK
    N = S // C
    gamma = 1.0 - jnp.exp2(-5.0 - jnp.arange(H, dtype=jnp.float32))
    log_g = jnp.log(gamma)
    i = jnp.arange(C, dtype=jnp.float32)
    diff = i[:, None] - i[None, :]
    decay = jnp.where(diff[None] >= 0,
                      jnp.exp(jnp.maximum(diff, 0.0)[None] * log_g[:, None, None]), 0.0)
    zeta = jnp.exp((C - 1.0 - i)[None, :] * log_g[:, None])
    xi = jnp.exp((i + 1.0)[None, :] * log_g[:, None])
    chunk_decay = jnp.exp(C * log_g)

    def chunks(t):
        return t.reshape(B, N, C, H, t.shape[-1]).transpose(0, 3, 1, 2, 4)

    qc, kc, vc = chunks(q), chunks(k), chunks(v)
    scores = jnp.einsum('bhncd,bhnmd->bhncm', qc, kc) * decay[None, :, None]
    o_inner = jnp.einsum('bhncm,bhnme->bhnce', scores, vc)
    kv = jnp.einsum('bhnmd,bhnme->bhnde', kc * zeta[None, :, None, :, None], vc)

    def step(R, kv_n):
        return chunk_decay[None, :, None, None] * R + kv_n, R

    _, R_prev = lax.scan(step, jnp.zeros((B, H, dk, dv), jnp.float32), jnp.moveaxis(kv, 2, 0))
    R_prev = jnp.moveaxis(R_prev, 0, 2)
    o_cross = jnp.einsum('bhncd,bhnde->bhnce', qc, R_prev) * xi[None, :, None, :, None]
    return (o_inner + o_cross).transpose(0, 2, 3, 1, 4).reshape(B, S, H, dv)

def head_groupnorm(o):
    mu = jnp.mean(o, axis=-1, keepdims=True)
    oc = o - mu
    return oc * lax.rsqrt(jnp.mean(oc * oc, axis=-1, keepdims=True) + EPS)

def second_inputs(seed: int = 0) -> dict:
    key = jax.random.key(seed)
    ks = jax.random.split(key, 20)
    f32 = jnp.float32

    def w(k, shape, fan_in):
        return jax.random.normal(k, shape, f32) * (fan_in ** -0.5)

    def gain(k, shape):
        return 1.0 + 0.02 * jax.random.normal(k, shape, f32)

    def small(k, shape):
        return 0.01 * jax.random.normal(k, shape, f32)

    L = DEPTH
    return {
        "x": jax.random.normal(ks[0], (BATCH, SEQ, D_MODEL), f32),
        "norm_mix_pre": gain(ks[1], (L, D_MODEL)),
        "norm_mix_post": gain(ks[2], (L, D_MODEL)),
        "norm_ffn_pre": gain(ks[3], (L, D_MODEL)),
        "norm_ffn_post": gain(ks[4], (L, D_MODEL)),
        "w_in": w(ks[5], (L, D_MODEL, IN_WIDTH), D_MODEL),
        "w_ret_out": w(ks[6], (L, MIX_WIDTH, D_MODEL), MIX_WIDTH),
        "sc_conv_w": w(ks[7], (L, SC_KERNEL, SC_WIDTH), SC_KERNEL),
        "w_sc_out": w(ks[8], (L, SC_WIDTH, D_MODEL), SC_WIDTH),
        "cf_conv_w": w(ks[9], (L, CF_KERNEL, CF_WIDTH), CF_KERNEL),
        "cf_conv_b": small(ks[10], (L, CF_WIDTH)),
        "cf_ln_g": gain(ks[11], (L, CF_WIDTH)),
        "cf_ln_b": small(ks[12], (L, CF_WIDTH)),
        "w_cf_out": w(ks[13], (L, CF_WIDTH, D_MODEL), CF_WIDTH),
        "w_o": w(ks[14], (L, D_MODEL, D_MODEL), D_MODEL),
        "w_up": w(ks[15], (L, D_MODEL, 2 * D_FF), D_MODEL),
        "ffn_conv_w": w(ks[16], (L, FFN_KERNEL, 2 * D_FF), FFN_KERNEL),
        "w_down": w(ks[17], (L, D_FF, D_MODEL), D_FF),
    }

def second_block(x, norm_mix_pre, norm_mix_post, norm_ffn_pre, norm_ffn_post, w_in, w_ret_out,
              sc_conv_w, w_sc_out, cf_conv_w, cf_conv_b, cf_ln_g, cf_ln_b, w_cf_out, w_o,
              w_up, ffn_conv_w, w_down):
    B, S, D = x.shape
    dt = x.dtype
    pos = jnp.arange(S)
    split_idx = [int(c) for c in np.cumsum(IN_SIZES)[:-1]]
    for l in range(DEPTH):
        h = rmsnorm(x, norm_mix_pre[l])
        proj = h @ w_in[l].astype(dt)
        (q, k, v, g_ret, sc_b, sc_c, sc_x, cf_a, cf_b, gate_logits) = jnp.split(proj, split_idx, axis=-1)

        qh = rotary(q.astype(jnp.float32).reshape(B, S, RET_HEADS, RET_QK_DIM), pos)
        kh = rotary(k.astype(jnp.float32).reshape(B, S, RET_HEADS, RET_QK_DIM), pos) * (RET_QK_DIM ** -0.5)
        vh = v.astype(jnp.float32).reshape(B, S, RET_HEADS, RET_V_DIM)
        o = head_groupnorm(retention_chunkwise(qh, kh, vh)).reshape(B, S, MIX_WIDTH).astype(dt)
        y_ret = (jax.nn.silu(g_ret) * o) @ w_ret_out[l].astype(dt)

        u = causal_dwconv(sc_c * sc_x, sc_conv_w[l])
        y_sc = (sc_b * u) @ w_sc_out[l].astype(dt)

        glu = cf_a * jax.nn.sigmoid(cf_b)
        c = causal_dwconv(glu, cf_conv_w[l], cf_conv_b[l])
        c = jax.nn.silu(layernorm(c, cf_ln_g[l], cf_ln_b[l]))
        y_cf = c @ w_cf_out[l].astype(dt)

        gates = jax.nn.sigmoid(gate_logits).reshape(B, S, N_BRANCH, D)
        merged = gates[:, :, 0] * y_ret + gates[:, :, 1] * y_sc + gates[:, :, 2] * y_cf
        x = x + rmsnorm(merged @ w_o[l].astype(dt), norm_mix_post[l])

        h = rmsnorm(x, norm_ffn_pre[l])
        up = causal_dwconv(h @ w_up[l].astype(dt), ffn_conv_w[l])
        gate, val = jnp.split(up, 2, axis=-1)
        f = (jax.nn.silu(gate) * val) @ w_down[l].astype(dt)
        x = x + rmsnorm(f, norm_ffn_post[l])
    return x


def setup_inputs(seed=0):
    out = dict(first_inputs(seed))
    for name, value in second_inputs(seed + 1).items():
        if name != "x":
            out[name + "_2"] = value
    return out


def reference(
    x, c, positions, ada_w, ada_b, norm_mix_g, norm_ffn_g, mla_w_down, mla_q_a_g, mla_kv_a_g,
    mla_w_uq, mla_w_ukv, mla_q_norm_g, mla_k_norm_g, mla_w_o, hy_w_in, hy_b_in, hy_conv_w,
    hy_conv_b, hy_f_w1, hy_f_b1, hy_f_freq1, hy_f_w2, hy_f_b2, hy_f_freq2, hy_f_w3, hy_f_b3,
    hy_f_freq3, hy_f_w4, hy_filt_bias, hy_w_out, moe_wg, moe_bg, moe_we, moe_be, moe_w_gate,
    moe_w_up, moe_w_down, norm_mix_pre_2, norm_mix_post_2, norm_ffn_pre_2, norm_ffn_post_2,
    w_in_2, w_ret_out_2, sc_conv_w_2, w_sc_out_2, cf_conv_w_2, cf_conv_b_2, cf_ln_g_2,
    cf_ln_b_2, w_cf_out_2, w_o_2, w_up_2, ffn_conv_w_2, w_down_2,
):
    x = first_block(
        x, c, positions, ada_w, ada_b, norm_mix_g, norm_ffn_g, mla_w_down, mla_q_a_g,
        mla_kv_a_g, mla_w_uq, mla_w_ukv, mla_q_norm_g, mla_k_norm_g, mla_w_o, hy_w_in, hy_b_in,
        hy_conv_w, hy_conv_b, hy_f_w1, hy_f_b1, hy_f_freq1, hy_f_w2, hy_f_b2, hy_f_freq2,
        hy_f_w3, hy_f_b3, hy_f_freq3, hy_f_w4, hy_filt_bias, hy_w_out, moe_wg, moe_bg, moe_we,
        moe_be, moe_w_gate, moe_w_up, moe_w_down,
    )
    return second_block(
        x, norm_mix_pre_2, norm_mix_post_2, norm_ffn_pre_2, norm_ffn_post_2, w_in_2,
        w_ret_out_2, sc_conv_w_2, w_sc_out_2, cf_conv_w_2, cf_conv_b_2, cf_ln_g_2, cf_ln_b_2,
        w_cf_out_2, w_o_2, w_up_2, ffn_conv_w_2, w_down_2,
    )


_drawn_inputs = setup_inputs


def setup_inputs(seed=0):
    import zlib

    import numpy as np

    out = dict(_drawn_inputs(seed))
    spreads = {}
    factors = {'mla_q_a_g': 8.0,
     'mla_kv_a_g': 6.951,
     'mla_q_norm_g': 8.0,
     'mla_k_norm_g': 6.145,
     'hy_f_freq1': 3.88,
     'hy_f_freq2': 10.13,
     'hy_f_freq3': 19.4,
     'moe_bg': 16.129,
     'moe_be': 26.394,
     'norm_ffn_post_2': 15.849,
     'cf_conv_b_2': 28.592,
     'cf_ln_g_2': 130.392,
     'cf_ln_b_2': 200.0,
     'norm_ffn_g': 4.933,
     'hy_b_in': 5.626,
     'hy_conv_b': 5.457,
     'norm_mix_pre_2': 3.236,
     'norm_mix_post_2': 14.627,
     'norm_ffn_pre_2': 3.543}
    for name, (base, spread) in spreads.items():
        noise = np.random.default_rng([zlib.crc32(name.encode()), seed]).standard_normal(out[name].shape)
        drawn = base * np.exp(spread * noise) if base else spread * noise
        out[name] = __import__('jax').numpy.asarray(drawn.astype(out[name].dtype))
    for name, factor in factors.items():
        out[name] = (out[name] * factor).astype(out[name].dtype)
    return out
```

```python
import itertools
import math
from collections import namedtuple
from contextlib import ExitStack

import numpy as np

import concourse.bass as bass
from concourse import mybir

F32 = mybir.dt.float32
I32 = mybir.dt.int32
ALU = mybir.AluOpType
ACT = mybir.ActivationFunctionType
AX = mybir.AxisListType

P = 128
D = 1024
S = 512
DEPTH = 2
KC = D // P
TT = S // P
UNIT = 2048
SLOTS = 4
BANKS = 8

HEADS, Q_LORA, KV_LORA, NOPE, ROPE, V_HEAD = 8, 256, 128, 128, 64, 128
QK_HEAD = NOPE + ROPE
GROUPS, PER_GROUP, D_EXPERT = 4, 4, 256
EXPERTS = GROUPS * PER_GROUP
FILTER_EMB, FILTER_WIDTH = 33, 64
RET_HEADS, RET_QK, RET_V = 4, 64, 128
MIX = 512
D_FF = 2816
FF_TILES = D_FF // P
CF_K, SC_K, FFN_K = 31, 3, 3
EPS = 1e-6

PARAM_TILES = [
    ("c", KC), ("ada_b", DEPTH * 48), ("norm_mix_g", DEPTH * KC), ("norm_ffn_g", DEPTH * KC),
    ("q_a_g", 2), ("kv_a_g", 1), ("q_nope_g", 1), ("q_pe_g", 1), ("k_nope_g", 1), ("k_pe_g", 1),
    ("hy_b_in", 24), ("hy_conv_w", 72), ("hy_conv_b", 24), ("hy_filt_bias", 16),
    ("hy_fb", 3), ("hy_ff", 3),
    ("mix_pre", DEPTH * KC), ("mix_post", DEPTH * KC), ("ffn_pre", DEPTH * KC), ("ffn_post", DEPTH * KC),
    ("sc_w", DEPTH * SC_K * 4), ("cf_w", DEPTH * CF_K * 4), ("cf_b", DEPTH * 4),
    ("cf_g", DEPTH * 4), ("cf_lb", DEPTH * 4), ("ffn_w", DEPTH * FFN_K * 2 * FF_TILES),
]
PCOL, PCOLS = {}, 0
for _name, _n in PARAM_TILES:
    PCOL[_name] = PCOLS
    PCOLS += _n

CONST_TILES = [("ident", P), ("ones", P), ("ones64", P), ("rot", P), ("inv_freq", 1), ("eps", 1), ("zero", 1)]
CCOL, CCOLS = {}, 0
for _name, _n in CONST_TILES:
    CCOL[_name] = CCOLS
    CCOLS += _n

TWO_PI_A = 6.28125
TWO_PI_B = math.floor((2 * math.pi - TWO_PI_A) * 2.0 ** 21) / 2.0 ** 21
TWO_PI_C = float(np.float32(2 * math.pi - TWO_PI_A - TWO_PI_B))
PI_DOWN = 3.1415925
ROUND_MAGIC = 12582912.0


BUFFERS = itertools.count()


def on_chip(nc, ctx, name, shape, dtype):
    return ctx.enter_context(nc.sbuf_tensor(f"{name}_{next(BUFFERS)}", shape, dtype))


class Memory:
    pass


class Phases:

    POOL = 44

    def __init__(self, nc):
        self.nc = nc
        self.pools = [[nc.alloc_semaphore(f"phase{h}_{n}") for n in range(self.POOL)] for h in range(2)]
        self.turn = 0

    def open(self, ctx, *names):
        mine, other = self.pools[self.turn], self.pools[1 - self.turn]
        self.turn = 1 - self.turn
        assert len(names) <= self.POOL
        block = ctx.enter_context(self.nc.Block())
        stale = range(other[0].num, other[-1].num + 1)
        return block, namedtuple("Signals", names)(*mine[:len(names)]), stale


class Link:

    def __init__(self, eng, sem, start=0):
        self.eng, self.sem, self.start, self.n = eng, sem, start, 0

    def __call__(self, instruction):
        instruction.then_inc(self.sem, 1)
        self.n += 1
        self.eng.wait_ge(self.sem, self.start + self.n)


class Ring:

    def __init__(self, nc, ctx):
        self.buf = on_chip(nc, ctx, "weights", [P, SLOTS, UNIT], F32)
        self.loaded = [nc.alloc_semaphore(f"weights_loaded_{k}") for k in range(SLOTS)]
        self.used = nc.alloc_semaphore("weights_used")
        self.first = 0
        self.issued = 0

    def _load(self, sp, src):
        g = self.issued
        if g >= SLOTS:
            sp.wait_ge(self.used, g - SLOTS + 1)
        sp.dma_start(self.buf[:, g % SLOTS, :], src).then_inc(self.loaded[g % SLOTS], 16)
        self.issued += 1

    def stream(self, sp, src, n, following=None):
        while self.issued < self.first + n and self.issued < SLOTS:
            self._load(sp, src[self.issued - self.first, :, :])
        u = self.issued - self.first
        turns = (n - u) // SLOTS
        if turns > 1:
            g0 = self.issued
            with sp.Fori(0, turns) as i:
                for k in range(SLOTS):
                    sp.wait_ge(self.used, i * SLOTS + (g0 + k - SLOTS + 1))
                    sp.dma_start(self.buf[:, (g0 + k) % SLOTS, :],
                                 src[bass.ds(i * SLOTS + (u + k), 1), :, :].rearrange("a p n -> p (a n)"))\
                        .then_inc(self.loaded[(g0 + k) % SLOTS], 16)
            self.issued += turns * SLOTS
        while self.issued < self.first + n:
            self._load(sp, src[self.issued - self.first, :, :])
        if following is not None:
            for k in range(min(SLOTS, following.shape[0])):
                self._load(sp, following[k, :, :])

    def arrived(self, pe, u, turn=0):
        g = self.first + u
        pe.wait_ge(self.loaded[g % SLOTS], turn * 16 + 16 * (g // SLOTS + 1))
        return self.buf[:, g % SLOTS, :]

    def products(self, eng, u, turn=0, per=SLOTS):
        eng.wait_ge(self.used, turn * per + (self.first + u + 1))


def unit_products(nc, pe, ring, u, rhs, psum, kc=KC, tiles=2, turn=0, width=S, k_ready=None, banks=None):
    w = ring.arrived(pe, u, turn).rearrange("p (k m) -> p k m", k=kc)
    for j in range(tiles):
        b = banks[j] if banks else (tiles * u + j) % BANKS
        for k in range(kc):
            if k_ready is not None and j == 0:
                pe.wait_ge(k_ready, k + 1)
            mm = nc.tensor.matmul(psum[:, b, 0:width], w[:, k, j * P:(j + 1) * P], rhs[:, k, 0:width],
                                  start=(k == 0), stop=(k == kc - 1))
    mm.then_inc(ring.used, 1)


def streamed_products(nc, pe, ring, n, rhs, psum, read_out, width=S, k_ready=None):
    for u in range(min(n, SLOTS)):
        unit_products(nc, pe, ring, u, rhs, psum, width=width, k_ready=k_ready if u == 0 else None)
    turns = (n - SLOTS) // SLOTS
    if turns > 1:
        with pe.Fori(0, turns) as i:
            for k in range(SLOTS):
                pe.wait_ge(read_out, i * SLOTS + (k + 1))
                unit_products(nc, pe, ring, SLOTS + k, rhs, psum, width=width, turn=i)
    else:
        turns = 0
    for u in range(SLOTS * (turns + 1), n):
        pe.wait_ge(read_out, u - SLOTS + 1)
        unit_products(nc, pe, ring, u, rhs, psum, width=width)


def over_units(eng, n, body):
    turns = n // SLOTS
    if turns > 1:
        with eng.Fori(0, turns) as i:
            for k in range(SLOTS):
                body(k, i)
    else:
        turns = 0
    for u in range(SLOTS * turns, n):
        body(u, 0)


NORM_SEMS = ("squared", "summed", "root", "scaled", "h_ready")


def norm_act(nc, act, m, s, src, shift=None):
    for c in range(KC):
        nc.scalar.activation(m.H[:, c, :], src[:, c, :], ACT.Square).then_inc(s.squared, 1)
    act.wait_ge(s.summed, 1)
    nc.scalar.activation(m.root[:, :], m.psum[:, 7, :], ACT.Sqrt, bias=m.const("eps"), scale=1.0 / D)\
        .then_inc(s.root, 1)
    if shift is not None:
        for c in range(KC):
            act.wait_ge(s.scaled, c + 1)
            nc.scalar.activation(m.H[:, c, :], m.H[:, c, :], ACT.Identity, bias=shift[:, c:c + 1])\
                .then_inc(s.h_ready, 1)


def norm_pe(nc, pe, m, s):
    for c in range(KC):
        pe.wait_ge(s.squared, c + 1)
        mm = nc.tensor.matmul(m.psum[:, 7, :], m.const("ones"), m.H[:, c, :], start=(c == 0), stop=(c == KC - 1))
    mm.then_inc(s.summed, 1)


def norm_dve(nc, dve, m, s, link, src, gain, shifted):
    dve.wait_ge(s.root, 1)
    link(nc.vector.reciprocal(m.root[:, :], m.root[:, :]))
    for c in range(KC):
        nc.vector.scalar_tensor_tensor(m.H[:, c, :], src[:, c, :], gain[:, c:c + 1], m.root[:, :],
                                       ALU.mult, ALU.mult).then_inc(s.scaled if shifted else s.h_ready, 1)


def phase_load(nc, m, ph, ring, d):
    with ExitStack() as ctx:
        block, s, stale = ph.open(ctx, "here", "v", "a", "tables")
        pos = on_chip(nc, ctx, "pos_i", [P, S], I32)
        t0 = on_chip(nc, ctx, "angle", [P, S], F32)
        t1 = on_chip(nc, ctx, "turns", [P, S], F32)
        t2 = on_chip(nc, ctx, "angle2", [P, S], F32)

        @block.sync
        def _(sp):
            for dst, src in ((m.PT[:, :], d.params), (m.CT[:, :], d.consts), (pos[:, :], d.positions),
                             (m.X[:, :, :], d.x), (m.WR[:, :, :, :], d.router_w), (m.RB[:, :, :], d.router_b)):
                sp.dma_start(dst, src).then_inc(s.here, 16)
            ring.stream(sp, d.ada_w, 0, following=d.ada_w)
            sp.wait_ge(s.here, 96)

        @block.vector
        def _(dve):
            link = Link(dve, s.v)
            dve.wait_ge(s.here, 96)
            link(nc.vector.tensor_copy(t1[:, :], pos[:, :]))
            link(nc.vector.tensor_scalar(t0[:, :], t1[:, :], m.const("inv_freq"), None, ALU.mult))
            for table, quarter in ((m.sin, 0.0), (m.cos, math.pi / 2)):
                link(nc.vector.tensor_scalar(t1[:, :], t0[:, :], 1.0 / (2 * math.pi), quarter / (2 * math.pi),
                                             ALU.mult, ALU.add))
                link(nc.vector.tensor_scalar(t1[:, :], t1[:, :], ROUND_MAGIC, None, ALU.add))
                link(nc.vector.tensor_scalar(t1[:, :], t1[:, :], ROUND_MAGIC, None, ALU.subtract))
                link(nc.vector.scalar_tensor_tensor(t2[:, :], t1[:, :], -TWO_PI_A, t0[:, :], ALU.mult, ALU.add))
                if quarter:
                    link(nc.vector.tensor_scalar(t2[:, :], t2[:, :], quarter, None, ALU.add))
                link(nc.vector.scalar_tensor_tensor(t2[:, :], t1[:, :], -TWO_PI_B, t2[:, :], ALU.mult, ALU.add))
                link(nc.vector.scalar_tensor_tensor(t2[:, :], t1[:, :], -TWO_PI_C, t2[:, :], ALU.mult, ALU.add))
                nc.vector.tensor_scalar(table[:, :], t2[:, :], PI_DOWN, -PI_DOWN, ALU.min, ALU.max)\
                    .then_inc(s.tables, 1)

        @block.scalar
        def _(act):
            act.wait_ge(s.here, 96)
            nc.scalar.activation(m.c_act[:, :, 0], m.param("c", KC), ACT.Silu)
            for n, table in enumerate((m.sin, m.cos)):
                act.wait_ge(s.tables, n + 1)
                nc.scalar.activation(table[:, :], table[:, :], ACT.Sin)

        @block.gpsimd
        def _(pool):
            for k in range(4):
                nc.gpsimd.memset(m.priority[:, :, k:k + 1], 4.0 - k)


def phase_modulation(nc, m, ph, ring, d, following):
    n = DEPTH * 24
    with ExitStack() as ctx:
        block, s, stale = ph.open(ctx, "read_out", "v")

        @block.sync
        def _(sp):
            sp.sem_clear(stale)
            ring.stream(sp, d.ada_w, n, following)

        @block.tensor
        def _(pe):
            streamed_products(nc, pe, ring, n, m.c_act, m.psum, s.read_out, width=1)

        @block.vector
        def _(dve):
            def body(u, turn):
                ring.products(dve, u, turn)
                b = 2 * u % BANKS
                nc.vector.tensor_tensor(m.mod[:, bass.ds(turn * 8 + 2 * u, 2)], m.psum[:, b:b + 2, 0],
                                        m.PT[:, bass.ds(turn * 8 + (PCOL["ada_b"] + 2 * u), 2)], ALU.add)\
                    .then_inc(s.read_out, 1)
            over_units(dve, n, body)
            dve.wait_ge(s.read_out, n)
            link = Link(dve, s.v)
            for layer in range(DEPTH):
                for which, name, col in ((0, "norm_mix_g", 8), (1, "norm_ffn_g", 32)):
                    g = m.param(name, KC, layer * KC)
                    sc = m.mod[:, 48 * layer + col:48 * layer + col + KC]
                    nc.vector.scalar_tensor_tensor(m.gain[:, layer, which, :], sc, 1.0, g, ALU.add, ALU.mult)
        ring.first += n


def phase_latents(nc, m, ph, ring, d, following):
    n = 2
    with ExitStack() as ctx:
        block, s, stale = ph.open(ctx, *NORM_SEMS, "v", "raw", "raw_sq", "sums", "roots", "rdiv", "rot_in", "rot_out")

        @block.sync
        def _(sp):
            sp.sem_clear(stale)
            ring.stream(sp, d.mla_w_down, n, following)

        @block.scalar
        def _(act):
            norm_act(nc, act, m, s, m.X, shift=m.mod[:, 0:KC])
            ring.products(act, 1)
            nc.scalar.activation(m.lat[:, :, :], m.psum[:, 0:4, :], ACT.Copy).then_inc(s.raw, 1)
            act.wait_ge(s.raw, 1)
            nc.scalar.activation(m.sq4[:, :, :], m.psum[:, 0:4, :], ACT.Square).then_inc(s.raw_sq, 1)
            act.wait_ge(s.sums, 1)
            for b, width in ((0, Q_LORA), (1, KV_LORA), (2, ROPE)):
                nc.scalar.activation(m.r4[:, b, :], m.psum[:, 4 + b, :], ACT.Sqrt, bias=m.const("eps"),
                                     scale=1.0 / width).then_inc(s.roots, 1)

        @block.tensor
        def _(pe):
            norm_pe(nc, pe, m, s)
            unit_products(nc, pe, ring, 0, m.H, m.psum, k_ready=s.h_ready)
            unit_products(nc, pe, ring, 1, m.H, m.psum)
            pe.wait_ge(s.raw_sq, 1)
            nc.tensor.matmul(m.psum[:, 4, :], m.const("ones"), m.sq4[:, 0, :], start=True, stop=False)
            nc.tensor.matmul(m.psum[:, 4, :], m.const("ones"), m.sq4[:, 1, :], start=False, stop=True)
            nc.tensor.matmul(m.psum[:, 5, :], m.const("ones"), m.sq4[:, 2, :], start=True, stop=True)
            nc.tensor.matmul(m.psum[:, 6, :], m.const("ones64"), m.sq4[:, 3, :], start=True, stop=True)\
                .then_inc(s.sums, 1)
            pe.wait_ge(s.rot_in, 1)
            nc.tensor.matmul(m.psum[:, 0, :], m.const("rot"), m.lat[:, 3, :], start=True, stop=True)\
                .then_inc(s.rot_out, 1)

        @block.vector
        def _(dve):
            link = Link(dve, s.v)
            norm_dve(nc, dve, m, s, link, m.X, m.gain[:, 0, 0, :], True)
            dve.wait_ge(s.roots, 3)
            link(nc.vector.reciprocal(m.r4[:, 0:3, :], m.r4[:, 0:3, :]))
            for t, root, g in ((0, 0, m.param("q_a_g", 1, 0)), (1, 0, m.param("q_a_g", 1, 1)),
                               (2, 1, m.param("kv_a_g", 1))):
                nc.vector.scalar_tensor_tensor(m.lat[:, t, :], m.lat[:, t, :], g, m.r4[:, root, :],
                                               ALU.mult, ALU.mult)
            nc.vector.scalar_tensor_tensor(m.lat[:, 3, :], m.lat[:, 3, :], m.param("k_pe_g", 1), m.r4[:, 2, :],
                                           ALU.mult, ALU.mult).then_inc(s.rot_in, 1)
            dve.wait_ge(s.rot_in, 1)
            link(nc.vector.tensor_tensor(m.k_pe[:, :], m.lat[:, 3, :], m.cos[:, :], ALU.mult))
            dve.wait_ge(s.rot_out, 1)
            link(nc.vector.tensor_tensor(m.sq4[:, 0, :], m.psum[:, 0, :], m.sin[:, :], ALU.mult))
            nc.vector.tensor_tensor(m.k_pe[:, :], m.k_pe[:, :], m.sq4[:, 0, :], ALU.add)
        ring.first += n


def phase_heads(nc, m, ph, ring, d, following):
    with ExitStack() as ctx:
        block, s, stale = ph.open(ctx, "raw", "copied", "sq", "sums", "roots", "normed", "v", "rot", "rot_used", "vraw", "vcopied")
        dest = [m.qn[:, 0:4, :], m.qn[:, 4:8, :], m.kn[:, 0:4, :], m.kn[:, 4:8, :], m.qp[:, :, :]]
        gains = ["q_nope_g", "q_nope_g", "k_nope_g", "k_nope_g", "q_pe_g"]

        @block.sync
        def _(sp):
            sp.sem_clear(stale)
            ring.stream(sp, d.mla_w_heads, 3, following)

        @block.tensor
        def _(pe):
            uq0 = ring.arrived(pe, 0).rearrange("p (k m) -> p k m", k=2)
            uq1 = ring.arrived(pe, 1).rearrange("p (k m) -> p k m", k=2)
            ukv = ring.arrived(pe, 2)

            def raw(b):
                if b >= 1:
                    pe.wait_ge(s.sq, b)
                for j in range(4):
                    if b in (0, 1, 4):
                        w = uq1 if b == 4 else uq0
                        col = (j if b == 4 else 4 * b + j) * P
                        for k in range(2):
                            mm = nc.tensor.matmul(m.psum[:, j, :], w[:, k, col:col + P], m.lat[:, k, :],
                                                  start=(k == 0), stop=(k == 1))
                    else:
                        col = (4 * (b - 2) + j) * P
                        mm = nc.tensor.matmul(m.psum[:, j, :], ukv[:, col:col + P], m.lat[:, 2, :],
                                              start=True, stop=True)
                mm.then_inc(s.raw, 1)

            def sums(b):
                pe.wait_ge(s.sq, b + 1)
                if b >= 1:
                    pe.wait_ge(s.roots, b)
                for j in range(4):
                    mm = nc.tensor.matmul(m.psum[:, 4 + j, :], m.const("ones64" if b == 4 else "ones"),
                                          m.sq8[:, b % 2, j, :], start=True, stop=True)
                mm.then_inc(s.sums, 1)

            raw(0)
            for b in range(5):
                if b < 4:
                    raw(b + 1)
                sums(b)
            for half in range(2):
                if half == 0:
                    pe.wait_ge(s.sq, 5)
                else:
                    pe.wait_ge(s.roots, 5)
                for t in range(TT):
                    mm = nc.tensor.matmul(m.psum[:, 4 * half + t, :], m.lat[:, 2, t * P:(t + 1) * P],
                                          ukv[:, D + half * 512:D + half * 512 + 512], start=True, stop=True)
                mm.then_inc(s.vraw, 1)
            pe.wait_ge(s.normed, 5)
            pe.wait_ge(s.vcopied, 1)
            for j in range(4):
                mm = nc.tensor.matmul(m.psum[:, j, :], m.const("rot"), m.qp[:, j, :], start=True, stop=True)
            mm.then_inc(s.rot, 1)

        @block.scalar
        def _(act):
            def read(b):
                act.wait_ge(s.raw, b + 1)
                if b >= 2:
                    act.wait_ge(s.sums, b - 1)
                nc.scalar.activation(dest[b], m.psum[:, 0:4, :], ACT.Copy).then_inc(s.copied, 1)
                nc.scalar.activation(m.sq8[:, b % 2, :, :], m.psum[:, 0:4, :], ACT.Square).then_inc(s.sq, 1)

            def root(b):
                act.wait_ge(s.sums, b + 1)
                if b >= 2:
                    act.wait_ge(s.normed, b - 1)
                nc.scalar.activation(m.r8[:, b % 2, :, :], m.psum[:, 4:8, :], ACT.Sqrt, bias=m.const("eps"),
                                     scale=1.0 / (ROPE if b == 4 else P)).then_inc(s.roots, 1)

            read(0)
            for b in range(5):
                if b < 4:
                    read(b + 1)
                root(b)
            for half in range(2):
                act.wait_ge(s.vraw, half + 1)
                nc.scalar.activation(m.vt[:, :, half * 512:half * 512 + 512], m.psum[:, 4 * half:4 * half + 4, :],
                                     ACT.Copy).then_inc(s.vcopied, 1)

        @block.vector
        def _(dve):
            link = Link(dve, s.v)
            for b in range(5):
                dve.wait_ge(s.roots, b + 1)
                dve.wait_ge(s.copied, b + 1)
                link(nc.vector.reciprocal(m.r8[:, b % 2, :, :], m.r8[:, b % 2, :, :]))
                nc.vector.scalar_tensor_tensor(dest[b].rearrange("p t n -> p (t n)"), dest[b].rearrange("p t n -> p (t n)"),
                                               m.param(gains[b], 1),
                                               m.r8[:, b % 2, :, :].rearrange("p t n -> p (t n)"),
                                               ALU.mult, ALU.mult).then_inc(s.normed, 1)
            dve.wait_ge(s.rot, 1)
            for j in range(4):
                nc.vector.tensor_tensor(m.sq8[:, 0, j, :], m.psum[:, j, :], m.sin[:, :], ALU.mult)
                link(nc.vector.tensor_tensor(m.qp[:, j, :], m.qp[:, j, :], m.cos[:, :], ALU.mult))
            nc.vector.tensor_tensor(m.qp[:, :, :], m.qp[:, :, :], m.sq8[:, 0, :, :], ALU.add)

        @block.gpsimd
        def _(pool):
            pool.wait_ge(s.vraw, 2)
            pool.sem_inc(ring.used, 3)
        ring.first += 3


def phase_attention(nc, m, ph, ring, d):
    scale = QK_HEAD ** -0.5
    steps = HEADS * TT
    with ExitStack() as ctx:
        block, s, stale = ph.open(ctx, "scores", "v", "neg", "exped", "rsum", "probs", "flipped", "pt_ready", "pv", "pv_read")
        E = on_chip(nc, ctx, "probs", [P, 3, S], F32)
        pt = on_chip(nc, ctx, "probs_t", [P, 2, TT, S], F32)
        top = on_chip(nc, ctx, "top", [P, steps], F32)
        neg = on_chip(nc, ctx, "neg", [P, steps], F32)
        tot = on_chip(nc, ctx, "tot", [P, steps], F32)
        inv = on_chip(nc, ctx, "inv", [P, steps], F32)

        @block.sync
        def _(sp):
            sp.sem_clear(stale)

        @block.tensor
        def _(pe):
            def scores(i):
                h, q = divmod(i, TT)
                if i >= 3:
                    pe.wait_ge(s.exped, i - 2)
                half = ROPE * (h % 2)
                nc.tensor.matmul(m.psum[:, i % 3, :], m.qn[:, h, q * P:(q + 1) * P], m.kn[:, h, :],
                                 start=True, stop=False)
                nc.tensor.matmul(m.psum[:, i % 3, :], m.qp[half:half + ROPE, h // 2, q * P:(q + 1) * P],
                                 m.k_pe[half:half + ROPE, :], start=False, stop=True).then_inc(s.scores, 1)

            def flip(i):
                pe.wait_ge(s.probs, i + 1)
                if i >= 2:
                    pe.wait_ge(s.pt_ready, i - 1)
                for kt in range(TT):
                    mm = nc.tensor.transpose(m.psum[:, 3 + i % 2, kt * P:(kt + 1) * P],
                                             E[:, i % 3, kt * P:(kt + 1) * P], m.const("ident"))
                mm.then_inc(s.flipped, 1)

            def values(h):
                pe.wait_ge(s.pt_ready, TT * (h + 1))
                if h >= 2:
                    pe.wait_ge(s.pv_read, h - 1)
                for kt in range(TT):
                    mm = nc.tensor.matmul(m.psum[:, 5 + h % 2, :], m.vt[:, kt, h * P:(h + 1) * P],
                                          pt[:, h % 2, kt, :], start=(kt == 0), stop=(kt == TT - 1))
                mm.then_inc(s.pv, 1)

            for i in range(steps + 3):
                if i < steps:
                    scores(i)
                if 2 <= i < steps + 2:
                    flip(i - 2)
                if i >= 6 and (i - 6) % TT == 0:
                    values((i - 6) // TT)

        @block.vector
        def _(dve):
            link = Link(dve, s.v)
            for i in range(steps + 2):
                if i < steps:
                    dve.wait_ge(s.scores, i + 1)
                    link(nc.vector.tensor_reduce(top[:, i:i + 1], m.psum[:, i % 3, :], AX.X, ALU.max))
                    nc.vector.tensor_scalar(neg[:, i:i + 1], top[:, i:i + 1], -scale, None, ALU.mult).then_inc(s.neg, 1)
                if 1 <= i <= steps:
                    dve.wait_ge(s.exped, i)
                    nc.vector.reciprocal(inv[:, i - 1:i], tot[:, i - 1:i]).then_inc(s.rsum, 1)
                if i >= 2:
                    j = i - 2
                    h, q = divmod(j, TT)
                    dve.wait_ge(s.flipped, j + 1)
                    if h >= 2:
                        dve.wait_ge(s.pv, h - 1)
                    nc.vector.tensor_copy(pt[:, h % 2, :, q * P:(q + 1) * P],
                                          m.psum[:, 3 + j % 2, :].rearrange("p (k n) -> p k n", k=TT)).then_inc(s.pt_ready, 1)

        @block.scalar
        def _(act):
            def out(h):
                act.wait_ge(s.pv, h + 1)
                nc.scalar.activation(m.H[:, h, :], m.psum[:, 5 + h % 2, :], ACT.Copy).then_inc(s.pv_read, 1)

            for i in range(steps + 1):
                if i < steps:
                    act.wait_ge(s.neg, i + 1)
                    if i >= 3:
                        act.wait_ge(s.flipped, i - 2)
                    nc.scalar.activation(E[:, i % 3, :], m.psum[:, i % 3, :], ACT.Exp, bias=neg[:, i:i + 1],
                                         scale=scale, accum_out=tot[:, i:i + 1]).then_inc(s.exped, 1)
                if i >= 1:
                    act.wait_ge(s.rsum, i)
                    nc.scalar.activation(E[:, (i - 1) % 3, :], E[:, (i - 1) % 3, :], ACT.Copy,
                                         scale=inv[:, i - 1:i]).then_inc(s.probs, 1)
                if i >= 8 and (i - 8) % TT == 0:
                    out((i - 8) // TT)
            out(HEADS - 1)


def phase_residual(nc, m, ph, ring, w, gate, following, rhs=None, even_odd=False):
    n = 4
    with ExitStack() as ctx:
        block, s, stale = ph.open(ctx, "read_out")

        @block.sync
        def _(sp):
            sp.sem_clear(stale)
            ring.stream(sp, w, n, following)

        @block.tensor
        def _(pe):
            streamed_products(nc, pe, ring, n, m.H if rhs is None else rhs, m.psum, s.read_out)

        @block.vector
        def _(dve):
            for u in range(n):
                ring.products(dve, u)
                for j in range(2):
                    t = 2 * u + j
                    x, y = m.X[:, t, :], m.psum[:, t, :]
                    if even_odd:
                        x = x.rearrange("p (n two) -> p two n", two=2)
                        y = y.rearrange("p (two n) -> p two n", two=2)
                    nc.vector.scalar_tensor_tensor(x, y, gate[:, t:t + 1], x, ALU.mult, ALU.add)
        ring.first += n


def phase_router(nc, m, ph, ring, layer, shift, gain):
    with ExitStack() as ctx:
        block, s, stale = ph.open(ctx, *NORM_SEMS, "logits", "v", "m1", "e1", "m2", "e2", "diag", "spread", "spread_read")
        L = on_chip(nc, ctx, "logits", [P, TT, GROUPS + EXPERTS], F32)
        G = on_chip(nc, ctx, "group", [P, 4, TT, GROUPS], F32)
        C = on_chip(nc, ctx, "column", [P, 6, TT], F32)
        EL = on_chip(nc, ctx, "chosen", [P, 4, TT, PER_GROUP], F32)
        T16 = on_chip(nc, ctx, "masked", [P, 2, TT, GROUPS, PER_GROUP], F32)
        dg = on_chip(nc, ctx, "diagonals", [P, 4, TT, P], F32)

        def wide(col, n=4):
            return col.unsqueeze(2).broadcast_to([P, TT, n])

        @block.sync
        def _(sp):
            sp.sem_clear(stale)

        @block.scalar
        def _(act):
            norm_act(nc, act, m, s, m.X, shift=shift)
            act.wait_ge(s.m1, 1)
            nc.scalar.activation(G[:, 1, :, :], G[:, 1, :, :], ACT.Exp).then_inc(s.e1, 1)
            act.wait_ge(s.m2, 1)
            nc.scalar.activation(EL[:, 1, :, :], EL[:, 1, :, :], ACT.Exp).then_inc(s.e2, 1)
            for e in range(EXPERTS):
                act.wait_ge(s.spread, e + 1)
                nc.scalar.activation(m.cb[:, e, :], m.psum[:, e % 4, :], ACT.Copy).then_inc(s.spread_read, 1)

        @block.tensor
        def _(pe):
            norm_pe(nc, pe, m, s)
            pe.wait_ge(s.h_ready, KC)
            for t in range(TT):
                for k in range(KC):
                    mm = nc.tensor.matmul(m.psum[:, 6, t * 20:(t + 1) * 20], m.H[:, k, t * P:(t + 1) * P],
                                          m.WR[:, layer, k, :], start=(k == 0), stop=(k == KC - 1))
            mm.then_inc(s.logits, 1)
            for e in range(EXPERTS):
                pe.wait_ge(s.diag, e + 1)
                if e >= 4:
                    pe.wait_ge(s.spread_read, e - 3)
                nc.tensor.matmul(m.psum[:, e % 4, :], m.const("ones"), dg[:, e % 4, :, :].rearrange("p t n -> p (t n)"),
                                 start=True, stop=True).then_inc(s.spread, 1)

        @block.vector
        def _(dve):
            link = Link(dve, s.v)
            tt, red = nc.vector.tensor_tensor, nc.vector.tensor_reduce
            norm_dve(nc, dve, m, s, link, m.X, gain, True)

            def first_of(out, values, largest, scratch):
                link(tt(scratch, values, wide(largest), ALU.is_equal))
                link(tt(scratch, scratch, m.priority[:, :, :], ALU.mult))
                link(red(C[:, 5, :], scratch, AX.X, ALU.max))
                link(tt(out, scratch, wide(C[:, 5, :]), ALU.is_equal))

            dve.wait_ge(s.logits, 1)
            link(tt(L[:, :, :], m.psum[:, 6, 0:80].rearrange("p (t n) -> p t n", t=TT),
                    m.RB[:, layer, :].unsqueeze(1).broadcast_to([P, TT, 20]), ALU.add))
            lg = L[:, :, 0:GROUPS]
            le = L[:, :, GROUPS:].rearrange("p t (g e) -> p t g e", g=GROUPS)
            link(red(C[:, 0, :], lg, AX.X, ALU.max))
            tt(G[:, 1, :, :], lg, wide(C[:, 0, :]), ALU.subtract).then_inc(s.m1, 1)
            dve.wait_ge(s.e1, 1)
            link(red(C[:, 1, :], G[:, 1, :, :], AX.X, ALU.add))
            link(nc.vector.reciprocal(C[:, 1, :], C[:, 1, :]))
            link(tt(G[:, 1, :, :], G[:, 1, :, :], wide(C[:, 1, :]), ALU.mult))
            link(red(C[:, 2, :], G[:, 1, :, :], AX.X, ALU.max))
            first_of(G[:, 2, :, :], G[:, 1, :, :], C[:, 2, :], G[:, 3, :, :])
            chosen_g = G[:, 2, :, :]
            for t in range(TT):
                link(tt(T16[:, 0, t, :, :], le[:, t, :, :], chosen_g[:, t, :].unsqueeze(2).broadcast_to([P, GROUPS, PER_GROUP]),
                        ALU.mult))
            for t in range(TT):
                link(red(EL[:, 0, t, :], T16[:, 0, t, :, :].rearrange("p g e -> p e g"), AX.X, ALU.add))
            link(red(C[:, 0, :], EL[:, 0, :, :], AX.X, ALU.max))
            tt(EL[:, 1, :, :], EL[:, 0, :, :], wide(C[:, 0, :]), ALU.subtract).then_inc(s.m2, 1)
            dve.wait_ge(s.e2, 1)
            link(red(C[:, 0, :], EL[:, 1, :, :], AX.X, ALU.add))
            link(nc.vector.reciprocal(C[:, 0, :], C[:, 0, :]))
            link(tt(EL[:, 1, :, :], EL[:, 1, :, :], wide(C[:, 0, :]), ALU.mult))
            link(red(C[:, 0, :], EL[:, 1, :, :], AX.X, ALU.max))
            first_of(EL[:, 2, :, :], EL[:, 1, :, :], C[:, 0, :], EL[:, 0, :, :])
            link(nc.vector.scalar_tensor_tensor(EL[:, 0, :, :], EL[:, 2, :, :], -2.0, EL[:, 1, :, :], ALU.mult, ALU.add))
            link(red(C[:, 1, :], EL[:, 0, :, :], AX.X, ALU.max))
            first_of(EL[:, 3, :, :], EL[:, 0, :, :], C[:, 1, :], EL[:, 1, :, :])
            link(tt(C[:, 3, :], C[:, 0, :], C[:, 1, :], ALU.add))
            link(nc.vector.reciprocal(C[:, 3, :], C[:, 3, :]))
            link(tt(C[:, 3, :], C[:, 3, :], C[:, 2, :], ALU.mult))
            link(tt(C[:, 0, :], C[:, 0, :], C[:, 3, :], ALU.mult))
            link(tt(C[:, 1, :], C[:, 1, :], C[:, 3, :], ALU.mult))
            link(tt(EL[:, 2, :, :], EL[:, 2, :, :], wide(C[:, 0, :]), ALU.mult))
            link(tt(EL[:, 3, :, :], EL[:, 3, :, :], wide(C[:, 1, :]), ALU.mult))
            link(tt(EL[:, 2, :, :], EL[:, 2, :, :], EL[:, 3, :, :], ALU.add))
            for t in range(TT):
                link(tt(T16[:, 1, t, :, :], chosen_g[:, t, :].unsqueeze(2).broadcast_to([P, GROUPS, PER_GROUP]),
                        EL[:, 2, t, :].unsqueeze(1).broadcast_to([P, GROUPS, PER_GROUP]), ALU.mult))
            for e in range(EXPERTS):
                if e >= 4:
                    dve.wait_ge(s.spread, e - 3)
                w = T16[:, 1, :, e // PER_GROUP, e % PER_GROUP]
                tt(dg[:, e % 4, :, :], m.const("ident").unsqueeze(1).broadcast_to([P, TT, P]), wide(w, P), ALU.mult)\
                    .then_inc(s.diag, 1)


def phase_experts(nc, m, ph, ring, w, gate, following):
    per = 3 * PER_GROUP
    with ExitStack() as ctx:
        block, s, stale = ph.open(ctx, "gates_out", "ups_out", "a_ready", "downs_out")
        T = on_chip(nc, ctx, "silu", [P, PER_GROUP, 2, S], F32)
        A = on_chip(nc, ctx, "acts", [P, 2 * PER_GROUP, S], F32)

        @block.sync
        def _(sp):
            sp.sem_clear(stale)
            ring.stream(sp, w, per * GROUPS, following)

        @block.tensor
        def _(pe):
            pe.sem_inc(s.downs_out, 4)
            with pe.Fori(0, GROUPS) as g:
                for u in range(per):
                    if u < 4:
                        pe.wait_ge(s.downs_out, g * 4 + (u + 1))
                    elif u % 2 == 0:
                        pe.wait_ge(s.gates_out, g * 4 + (u // 2 - 1))
                    else:
                        pe.wait_ge(s.ups_out, g * 4 + (u // 2 - 1))
                    if u == 8:
                        pe.wait_ge(s.a_ready, g * 4 + 4)
                    unit_products(nc, pe, ring, u, m.H if u < 8 else A, m.psum, turn=g * 3)

        @block.scalar
        def _(act):
            with act.Fori(0, GROUPS) as g:
                for j in range(PER_GROUP):
                    ring.products(act, 2 * j, g, per)
                    b = 4 * j % BANKS
                    nc.scalar.activation(T[:, j, :, :], m.psum[:, b:b + 2, :], ACT.Silu).then_inc(s.gates_out, 1)

        @block.vector
        def _(dve):
            with dve.Fori(0, GROUPS) as g:
                for j in range(PER_GROUP):
                    ring.products(dve, 2 * j + 1, g, per)
                    dve.wait_ge(s.gates_out, g * 4 + (j + 1))
                    b = (4 * j + 2) % BANKS
                    nc.vector.tensor_tensor(T[:, j, :, :], T[:, j, :, :], m.psum[:, b:b + 2, :], ALU.mult)\
                        .then_inc(s.ups_out, 1)
                for u in range(4):
                    ring.products(dve, 8 + u, g, per)
                    for j in range(2):
                        t = 2 * u + j
                        last = nc.vector.scalar_tensor_tensor(m.X[:, t, :], m.psum[:, t, :], gate[:, t:t + 1],
                                                              m.X[:, t, :], ALU.mult, ALU.add)
                    last.then_inc(s.downs_out, 1)

        @block.gpsimd
        def _(pool):
            with pool.Fori(0, GROUPS) as g:
                for j in range(PER_GROUP):
                    pool.wait_ge(s.ups_out, g * 4 + (j + 1))
                    for i in range(2):
                        last = nc.gpsimd.tensor_tensor(A[:, 2 * j + i, :], T[:, j, i, :],
                                                       m.cb[:, bass.ds(g * PER_GROUP + j, 1), :].rearrange("p a n -> p (a n)"),
                                                       ALU.mult)
                    last.then_inc(s.a_ready, 1)
        ring.first += per * GROUPS


def phase_hyena_in(nc, m, ph, ring, d, following):
    n = 12
    with ExitStack() as ctx:
        block, s, stale = ph.open(ctx, *NORM_SEMS, "v", "read_out", "padded", "conv", "pads")
        U = on_chip(nc, ctx, "padded", [P, 2, 2, S + 2], F32)
        W = on_chip(nc, ctx, "conv", [P, 2, S], F32)

        @block.sync
        def _(sp):
            sp.sem_clear(stale)
            ring.stream(sp, d.hy_w_in, n, following)

        @block.gpsimd
        def _(pool):
            nc.gpsimd.memset(U[:, :, :, :], 0.0).then_inc(s.pads, 1)

        @block.tensor
        def _(pe):
            norm_pe(nc, pe, m, s)
            pe.wait_ge(s.root, 1)
            streamed_products(nc, pe, ring, n, m.H, m.psum, s.read_out, k_ready=s.h_ready)

        @block.scalar
        def _(act):
            norm_act(nc, act, m, s, m.X, shift=m.mod[:, 48:48 + KC])
            act.wait_ge(s.pads, 1)
            act.sem_inc(s.conv, 4)

            def body(u, turn):
                ring.products(act, u, turn)
                act.wait_ge(s.conv, turn * 8 + (2 * u + 2))
                for j in range(2):
                    b = (2 * u + j) % BANKS
                    last = nc.scalar.activation(
                        U[:, u % 2, j, 1:S + 1], m.psum[:, b, :], ACT.Identity,
                        bias=m.PT[:, bass.ds(turn * 8 + (PCOL["hy_b_in"] + 2 * u + j), 1)])
                last.then_inc(s.read_out, 1)
            over_units(act, n, body)

        @block.vector
        def _(dve):
            link = Link(dve, s.v)
            norm_dve(nc, dve, m, s, link, m.X, m.gain[:, 1, 0, :], True)
            base = link.n

            def col(name, k):
                return m.PT[:, bass.ds(k + PCOL[name], 1)]

            def body(u, turn):
                dve.wait_ge(s.read_out, turn * SLOTS + (u + 1))
                chain = Link(dve, s.v, turn * 16 + (base + 4 * u))
                for j in range(2):
                    t = turn * 8 + (2 * u + j)
                    src = U[:, u % 2, j, :]
                    chain(nc.vector.tensor_scalar(W[:, j, :], src[:, 1:S + 1], col("hy_conv_w", t + 24),
                                                  col("hy_conv_b", t), ALU.mult, ALU.add))
                    chain(nc.vector.scalar_tensor_tensor(W[:, j, :], src[:, 0:S], col("hy_conv_w", t), W[:, j, :],
                                                         ALU.mult, ALU.add))
                    out = m.xv[:, bass.ds(t, 1), :].rearrange("p a (two n) -> p n (a two)", two=2)
                    nc.vector.scalar_tensor_tensor(
                        out, src[:, 2:S + 2].rearrange("p (n two) -> p n two", two=2), col("hy_conv_w", t + 48),
                        W[:, j, :].rearrange("p (n two) -> p n two", two=2), ALU.mult, ALU.add).then_inc(s.conv, 1)
            over_units(dve, n, body)
        ring.first += n


def phase_filter_mlp(nc, m, ph, ring, d):
    with ExitStack() as ctx:
        block, s, stale = ph.open(ctx, "here", "v", "sum", "arg", "sine")
        zT = on_chip(nc, ctx, "zT", [FILTER_EMB, S], F32)
        w1 = on_chip(nc, ctx, "w1", [FILTER_EMB, FILTER_WIDTH], F32)
        w23 = on_chip(nc, ctx, "w23", [FILTER_WIDTH, 2, FILTER_WIDTH], F32)
        a = on_chip(nc, ctx, "arg", [FILTER_WIDTH, S], F32)
        k = on_chip(nc, ctx, "whole", [FILTER_WIDTH, S], F32)

        @block.sync
        def _(sp):
            sp.sem_clear(stale)
            for dst, src in ((zT[:, :], d.zT), (w1[:, :], d.hy_f_w1), (w23[:, 0, :], d.hy_f_w2), (w23[:, 1, :], d.hy_f_w3)):
                sp.dma_start(dst, src).then_inc(s.here, 16)
            sp.dma_start(m.fwd[:, :, :, :], d.dft_fwd).then_inc(s.here, 16)
            sp.dma_start(m.inv[:, :, :, :], d.dft_inv).then_inc(s.here, 16)
            sp.wait_ge(s.here, 96)

        @block.tensor
        def _(pe):
            pe.wait_ge(s.here, 96)
            for n in range(3):
                if n:
                    pe.wait_ge(s.sine, n)
                nc.tensor.matmul(m.psum[0:FILTER_WIDTH, 0, :], w1[:, :] if n == 0 else w23[:, n - 1, :],
                                 zT[:, :] if n == 0 else m.hdn[:, :], start=True, stop=True).then_inc(s.sum, 1)

        @block.vector
        def _(dve):
            link = Link(dve, s.v)
            for n in range(3):
                dve.wait_ge(s.sum, n + 1)
                link(nc.vector.tensor_scalar(a[:, :], m.psum[0:FILTER_WIDTH, 0, :], m.param("hy_fb", 1, n)[0:FILTER_WIDTH, :],
                                             m.param("hy_ff", 1, n)[0:FILTER_WIDTH, :], ALU.add, ALU.mult))
                link(nc.vector.tensor_scalar(k[:, :], a[:, :], 1.0 / (2 * math.pi), ROUND_MAGIC, ALU.mult, ALU.add))
                link(nc.vector.tensor_scalar(k[:, :], k[:, :], ROUND_MAGIC, None, ALU.subtract))
                for part in (TWO_PI_A, TWO_PI_B, TWO_PI_C):
                    link(nc.vector.scalar_tensor_tensor(a[:, :], k[:, :], -part, a[:, :], ALU.mult, ALU.add))
                nc.vector.tensor_scalar(a[:, :], a[:, :], PI_DOWN, -PI_DOWN, ALU.min, ALU.max).then_inc(s.arg, 1)

        @block.scalar
        def _(act):
            for n in range(3):
                act.wait_ge(s.arg, n + 1)
                nc.scalar.activation(m.hdn[:, :], a[:, :], ACT.Sin).then_inc(s.sine, 1)


def phase_long_conv(nc, m, ph, ring, d, order, half):
    with ExitStack() as ctx:
        block, s, stale = ph.open(ctx, "here", "raw", "decayed", "absed", "norms", "v", "ab", "z_flip", "z_out",
                                  "k_sums", "k_odd", "k_done", "u_sums", "u_odd", "pairs", "inverse")
        F = on_chip(nc, ctx, "filters_then_u", [P, 2, TT, 512], F32)
        A = on_chip(nc, ctx, "ab_then_y", [P, 2, TT, 512], F32)
        K = on_chip(nc, ctx, "k_spectrum", [P, 2, TT, 512], F32)
        O = on_chip(nc, ctx, "decay_then_odd", [P, TT, 512], F32)
        w4, rn = K[0:FILTER_WIDTH, 0, 0:2, :], K[:, 1, 0:2, :]
        vt = m.H[:, :, :].rearrange("p (j a) n -> p j (a n)", a=2)
        cols = slice(half * 512, half * 512 + 512)

        @block.sync
        def _(sp):
            sp.sem_clear(stale)
            sp.dma_start(w4, d.hy_f_w4[:, order, :, cols]).then_inc(s.here, 16)
            sp.dma_start(O[:, :, :], d.decay[:, :, cols]).then_inc(s.here, 16)
            sp.wait_ge(s.here, 32)

        def transform(src_cos, src_sin):
            for parity in range(2):
                for which, src in ((0, src_cos), (1, src_sin)):
                    for kt in range(2):
                        for c in range(2):
                            j = 2 * parity + c
                            mm = nc.tensor.matmul(m.psum[:, 4 * parity + 2 * which + kt, :],
                                                  m.fwd[:, which, j, kt * P:(kt + 1) * P], src[:, j, :],
                                                  start=(c == 0), stop=(c == 1))
            return mm

        @block.tensor
        def _(pe):
            pe.wait_ge(s.here, 32)
            for x in range(2):
                for j in range(TT):
                    mm = nc.tensor.matmul(m.psum[:, 4 * x + j, :], m.hdn[:, j * P:(j + 1) * P], w4[:, x, :],
                                          start=True, stop=True)
                mm.then_inc(s.raw, 1)
            for x in range(2):
                pe.wait_ge(s.absed, x + 1)
                for j in range(TT):
                    mm = nc.tensor.matmul(m.psum[:, x, :], m.const("ones"), A[:, x, j, :],
                                          start=(j == 0), stop=(j == TT - 1))
            mm.then_inc(s.norms, 1)
            for j in range(TT):
                for c in range(4):
                    mm = nc.tensor.transpose(m.psum[:, 4 + j, c * P:(c + 1) * P],
                                             m.xv[:, 16 + 4 * half + c, j * P:(j + 1) * P], m.const("ident"))
            mm.then_inc(s.z_flip, 1)
            pe.wait_ge(s.ab, 1)
            pe.wait_ge(s.z_out, 1)
            transform(A[:, 0, :, :], A[:, 1, :, :]).then_inc(s.k_sums, 1)
            pe.wait_ge(s.k_done, 1)
            transform(vt[:, :, cols], vt[:, :, cols]).then_inc(s.u_sums, 1)
            pe.wait_ge(s.pairs, 1)
            for c in range(4):
                for parity in range(2):
                    for n in range(4):
                        mm = nc.tensor.matmul(m.psum[:, c, parity * 256:(parity + 1) * 256],
                                              F[:, parity, n, c * P:(c + 1) * P], m.inv[:, parity, n, :],
                                              start=(n == 0), stop=(n == 3))
                mm.then_inc(s.inverse, 1)

        @block.scalar
        def _(act):
            for x in range(2):
                act.wait_ge(s.decayed, x + 1)
                nc.scalar.activation(A[:, x, :, :], F[:, x, :, :], ACT.Abs).then_inc(s.absed, 1)
            act.wait_ge(s.z_flip, 1)
            nc.scalar.activation(vt[:, :, cols], m.psum[:, 4:8, :], ACT.Copy).then_inc(s.z_out, 1)
            act.wait_ge(s.k_sums, 1)
            nc.scalar.activation(O[:, :, :], m.psum[:, 4:8, :], ACT.Copy).then_inc(s.k_odd, 1)
            act.wait_ge(s.u_sums, 1)
            nc.scalar.activation(O[:, :, :], m.psum[:, 4:8, :], ACT.Copy).then_inc(s.u_odd, 1)

        @block.vector
        def _(dve):
            link = Link(dve, s.v)
            tt = nc.vector.tensor_tensor

            def butterflies(out):
                even = m.psum
                tt(out[:, 0, 0:2, :], even[:, 0:2, :], O[:, 0:2, :], ALU.add)
                tt(out[:, 0, 2:4, :], even[:, 0:2, :], O[:, 0:2, :], ALU.subtract)
                tt(out[:, 1, 0:2, :], even[:, 2:4, :], O[:, 2:4, :], ALU.add)
                return tt(out[:, 1, 2:4, :], O[:, 2:4, :], even[:, 2:4, :], ALU.subtract)

            dve.wait_ge(s.here, 32)
            for x in range(2):
                dve.wait_ge(s.raw, x + 1)
                tt(F[:, x, :, :], m.psum[:, 4 * x:4 * x + 4, :], O[:, :, :], ALU.mult).then_inc(s.decayed, 1)
            dve.wait_ge(s.norms, 1)
            link(nc.vector.tensor_scalar(rn, m.psum[:, 0:2, :], EPS, None, ALU.add))
            link(nc.vector.reciprocal(rn, rn))
            for x in range(2):
                link(tt(F[:, x, :, :], F[:, x, :, :], rn[:, x, :].unsqueeze(1).broadcast_to([P, TT, 512]), ALU.mult))
            link(nc.vector.memset(F[0:1, 1, 0, :], 0.0))
            tt(A[:, 0, :, :], F[:, 0, :, :], F[:, 1, :, :], ALU.add)
            tt(A[:, 1, :, :], F[:, 0, :, :], F[:, 1, :, :], ALU.subtract).then_inc(s.ab, 1)
            dve.wait_ge(s.k_odd, 1)
            butterflies(K).then_inc(s.k_done, 1)
            dve.wait_ge(s.u_odd, 1)
            link(butterflies(F))
            link(tt(A[:, 0, :, :], F[:, 0, :, :], K[:, 0, :, :], ALU.mult))
            link(tt(O[:, :, :], F[:, 1, :, :], K[:, 1, :, :], ALU.mult))
            link(tt(A[:, 0, :, :], A[:, 0, :, :], O[:, :, :], ALU.subtract))
            link(tt(A[:, 1, :, :], F[:, 0, :, :], K[:, 1, :, :], ALU.mult))
            link(tt(O[:, :, :], F[:, 1, :, :], K[:, 0, :, :], ALU.mult))
            link(tt(A[:, 1, :, :], A[:, 1, :, :], O[:, :, :], ALU.add))
            tt(F[:, 0, 0:2, :], A[:, 0, 0:2, :], A[:, 0, 2:4, :], ALU.add)
            tt(F[:, 1, 0:2, :], A[:, 0, 0:2, :], A[:, 0, 2:4, :], ALU.subtract)
            tt(F[:, 0, 2:4, :], A[:, 1, 0:2, :], A[:, 1, 2:4, :], ALU.subtract)
            tt(F[:, 1, 2:4, :], A[:, 1, 0:2, :], A[:, 1, 2:4, :], ALU.add).then_inc(s.pairs, 1)
            for c in range(4):
                t = 4 * half + c
                dve.wait_ge(s.inverse, c + 1)
                link(nc.vector.scalar_tensor_tensor(O[:, c, :], m.xv[:, 16 + t, :], m.param("hy_filt_bias", 1, 8 * order + t),
                                                    m.psum[:, c, :], ALU.mult, ALU.add))
                tt(m.xv[:, 16 + t, :], O[:, c, :], m.xv[:, 8 * order + t, :], ALU.mult)


def phase_project(nc, m, ph, ring, d, layer, following):
    n = 16
    with ExitStack() as ctx:
        block, s, stale = ph.open(ctx, *NORM_SEMS, "v", "read_out")

        @block.sync
        def _(sp):
            sp.sem_clear(stale)
            ring.stream(sp, d.w_proj[layer], n, following)

        @block.tensor
        def _(pe):
            norm_pe(nc, pe, m, s)
            pe.wait_ge(s.root, 1)
            streamed_products(nc, pe, ring, 14, m.H, m.psum, s.read_out, k_ready=s.h_ready)
            for u in (14, 15):
                w = ring.arrived(pe, u).rearrange("p (k m) -> p k m", k=KC)
                pe.wait_ge(s.read_out, 14)
                for t in range(TT):
                    for k in range(KC):
                        mm = nc.tensor.matmul(m.psum[:, 4 * (u - 14) + t, 0:256], m.H[:, k, t * P:(t + 1) * P],
                                              w[:, k, :], start=(k == 0), stop=(k == KC - 1))
                mm.then_inc(ring.used, 1)

        @block.scalar
        def _(act):
            norm_act(nc, act, m, s, m.X)
            for u in range(14):
                ring.products(act, u)
                func = ACT.Silu if u in (2, 3) else ACT.Sigmoid if u >= 12 else ACT.Copy
                b = 2 * u % BANKS
                nc.scalar.activation(m.raw[:, 2 * u:2 * u + 2, :], m.psum[:, b:b + 2, :], func).then_inc(s.read_out, 1)
            for u in (14, 15):
                ring.products(act, u)
                nc.scalar.activation(m.vr[:, :, 256 * (u - 14):256 * (u - 13)],
                                     m.psum[:, 4 * (u - 14):4 * (u - 14) + 4, 0:256], ACT.Copy)

        @block.vector
        def _(dve):
            link = Link(dve, s.v)
            norm_dve(nc, dve, m, s, link, m.X, m.param("mix_pre", KC, layer * KC), False)
        ring.first += n


RAW_Q, RAW_K, RAW_G, RAW_SB, RAW_SC, RAW_SX, RAW_CA, RAW_CB = 0, 2, 4, 8, 12, 16, 20, 24


def phase_retention(nc, m, ph, ring, d):
    with ExitStack() as ctx:
        block, s, stale = ph.open(ctx, "here", "rot", "qk", "v", "scores", "decayed", "outs", "copied", "means", "centred",
                                  "squares", "variances", "root")
        dec = on_chip(nc, ctx, "ret_decay", [P, RET_HEADS, S], F32)
        tab = on_chip(nc, ctx, "rotary", [P, 2, S], F32)
        ST = on_chip(nc, ctx, "scores", [P, 2, TT, S], F32)
        OR = on_chip(nc, ctx, "head_out", [P, RET_HEADS, S], F32)
        qk = m.raw[:, RAW_Q:RAW_K + 2, :]

        @block.sync
        def _(sp):
            sp.sem_clear(stale)
            sp.dma_start(dec[:, :, :], d.ret_decay).then_inc(s.here, 16)
            sp.dma_start(tab[:, :, :], d.ret_rotary).then_inc(s.here, 16)
            sp.wait_ge(s.here, 32)

        @block.tensor
        def _(pe):
            for j in range(4):
                mm = nc.tensor.matmul(m.psum[:, j, :], m.const("rot"), qk[:, j, :], start=True, stop=True)
            mm.then_inc(s.rot, 1)
            pe.wait_ge(s.qk, 1)
            for h in range(RET_HEADS):
                rows, t = slice(64 * (h % 2), 64 * (h % 2) + 64), h // 2
                if h:
                    pe.wait_ge(s.decayed, TT * h)
                for i in range(TT):
                    nc.tensor.matmul(m.psum[:, 4 + i, 0:S - i * P], m.raw[rows, RAW_K + t, i * P:(i + 1) * P],
                                     m.raw[rows, RAW_Q + t, i * P:S], start=True, stop=True).then_inc(s.scores, 1)
                for i in range(TT):
                    pe.wait_ge(s.decayed, TT * h + i + 1)
                    mm = nc.tensor.matmul(m.psum[:, h, i * P:S], m.vr[:, i, h * P:(h + 1) * P],
                                          ST[:, h % 2, i, 0:S - i * P], start=(i == 0), stop=(i == TT - 1))
                mm.then_inc(s.outs, 1)
            pe.wait_ge(s.copied, RET_HEADS)
            for h in range(RET_HEADS):
                mm = nc.tensor.matmul(m.psum[:, h, :], m.const("ones"), OR[:, h, :], start=True, stop=True)
            mm.then_inc(s.means, 1)
            pe.wait_ge(s.squares, 1)
            for h in range(RET_HEADS):
                mm = nc.tensor.matmul(m.psum[:, 4 + h, :], m.const("ones"), ST[:, 0, h, :], start=True, stop=True)
            mm.then_inc(s.variances, 1)

        @block.vector
        def _(dve):
            link = Link(dve, s.v)
            tt = nc.vector.tensor_tensor
            wide = lambda x: x.unsqueeze(1).broadcast_to([P, 4, S])
            dve.wait_ge(s.here, 32)
            dve.wait_ge(s.rot, 1)
            tt(ST[:, 0, :, :], m.psum[:, 0:4, :], wide(tab[:, 1, :]), ALU.mult)
            link(tt(qk, qk, wide(tab[:, 0, :]), ALU.mult))
            tt(qk, qk, ST[:, 0, :, :], ALU.add).then_inc(s.qk, 1)
            dve.wait_ge(s.qk, 1)
            for h in range(RET_HEADS):
                for i in range(TT):
                    dve.wait_ge(s.scores, TT * h + i + 1)
                    if h >= 2 and i == 0:
                        dve.wait_ge(s.outs, h - 1)
                    tt(ST[:, h % 2, i, 0:S - i * P], m.psum[:, 4 + i, 0:S - i * P], dec[:, h, 0:S - i * P], ALU.mult)\
                        .then_inc(s.decayed, 1)
            dve.wait_ge(s.means, 1)
            nc.vector.scalar_tensor_tensor(flat(OR[:, :, :]), flat(m.psum[:, 0:4, :]), -1.0 / RET_V, flat(OR[:, :, :]),
                                           ALU.mult, ALU.add).then_inc(s.centred, 1)
            dve.wait_ge(s.root, 1)
            link(nc.vector.reciprocal(ST[:, 1, :, :], ST[:, 1, :, :]))
            link(tt(OR[:, :, :], OR[:, :, :], ST[:, 1, :, :], ALU.mult))
            tt(m.raw[:, RAW_G:RAW_G + 4, :], m.raw[:, RAW_G:RAW_G + 4, :], OR[:, :, :], ALU.mult)

        @block.scalar
        def _(act):
            for h in range(RET_HEADS):
                act.wait_ge(s.outs, h + 1)
                nc.scalar.activation(OR[:, h, :], m.psum[:, h, :], ACT.Copy).then_inc(s.copied, 1)
            act.wait_ge(s.centred, 1)
            nc.scalar.activation(ST[:, 0, :, :], OR[:, :, :], ACT.Square).then_inc(s.squares, 1)
            act.wait_ge(s.variances, 1)
            nc.scalar.activation(ST[:, 1, :, :], m.psum[:, 4:8, :], ACT.Sqrt, bias=m.const("eps"),
                                 scale=1.0 / RET_V).then_inc(s.root, 1)


def flat(x):
    return x.rearrange("p t n -> p (t n)")


def phase_gates(nc, m, ph, ring, d, layer, following):
    n = 12
    with ExitStack() as ctx:
        block, s, stale = ph.open(ctx, "read_out", "v", "pads", "conv", "means", "centred", "squares", "variances", "root",
                                  "scaled")
        PB = on_chip(nc, ctx, "short_in", [P, 4, S + SC_K - 1], F32)
        GP = on_chip(nc, ctx, "long_in", [P, 4, S + CF_K - 1], F32)
        sb, sc, sx = (m.raw[:, k:k + 4, :] for k in (RAW_SB, RAW_SC, RAW_SX))
        ca, cb = (m.raw[:, k:k + 4, :] for k in (RAW_CA, RAW_CB))
        c_sw, c_cw = PCOL["sc_w"] + layer * SC_K * 4, PCOL["cf_w"] + layer * CF_K * 4

        @block.sync
        def _(sp):
            sp.sem_clear(stale)
            ring.stream(sp, d.w_gates[layer], n, following)

        @block.gpsimd
        def _(pool):
            nc.gpsimd.memset(PB[:, :, 0:SC_K - 1], 0.0)
            nc.gpsimd.memset(GP[:, :, 0:CF_K - 1], 0.0).then_inc(s.pads, 1)

        @block.tensor
        def _(pe):
            streamed_products(nc, pe, ring, n, m.H, m.psum, s.read_out)
            pe.wait_ge(s.conv, 1)
            pe.wait_ge(s.read_out, n)
            for j in range(4):
                mm = nc.tensor.matmul(m.psum[:, 0, :], m.const("ones"), ca[:, j, :], start=(j == 0), stop=(j == 3))
            mm.then_inc(s.means, 1)
            pe.wait_ge(s.squares, 1)
            for j in range(4):
                mm = nc.tensor.matmul(m.psum[:, 1, :], m.const("ones"), cb[:, j, :], start=(j == 0), stop=(j == 3))
            mm.then_inc(s.variances, 1)

        @block.scalar
        def _(act):
            def body(u, turn):
                ring.products(act, u, turn)
                b = 2 * u % BANKS
                nc.scalar.activation(m.gates[:, bass.ds(turn * 8 + 2 * u, 2), :], m.psum[:, b:b + 2, :], ACT.Sigmoid)\
                    .then_inc(s.read_out, 1)
            over_units(act, n, body)
            act.wait_ge(s.centred, 1)
            nc.scalar.activation(cb, ca, ACT.Square).then_inc(s.squares, 1)
            act.wait_ge(s.variances, 1)
            nc.scalar.activation(m.root[:, :], m.psum[:, 1, :], ACT.Sqrt, bias=m.const("eps"), scale=1.0 / MIX)\
                .then_inc(s.root, 1)
            act.wait_ge(s.scaled, 1)
            for j in range(4):
                nc.scalar.activation(ca[:, j, :], ca[:, j, :], ACT.Silu, scale=m.param("cf_g", 1, 4 * layer + j),
                                     bias=m.param("cf_lb", 1, 4 * layer + j))

        @block.vector
        def _(dve):
            link = Link(dve, s.v)
            tt, stt = nc.vector.tensor_tensor, nc.vector.scalar_tensor_tensor
            dve.wait_ge(s.pads, 1)
            tt(GP[:, :, CF_K - 1:], ca, cb, ALU.mult)
            link(tt(PB[:, :, SC_K - 1:], sc, sx, ALU.mult))
            for j in range(4):
                nc.vector.tensor_scalar(sc[:, j, :], PB[:, j, 2:2 + S], m.PT[:, c_sw + 8 + j:c_sw + 9 + j], None, ALU.mult)
                link(nc.vector.tensor_scalar(ca[:, j, :], GP[:, j, CF_K - 1:], m.PT[:, c_cw + 120 + j:c_cw + 121 + j],
                                             m.param("cf_b", 1, 4 * layer + j), ALU.mult, ALU.add))
            for k in range(SC_K - 1):
                for j in range(4):
                    last = stt(sc[:, j, :], PB[:, j, k:k + S], m.PT[:, c_sw + 4 * k + j:c_sw + 4 * k + j + 1], sc[:, j, :],
                               ALU.mult, ALU.add)
                link(last)
            link(tt(sb, sb, sc, ALU.mult))
            base = link.n
            with dve.Fori(0, CF_K - 1) as k:
                chain = Link(dve, s.v, k + base)
                for j in range(4):
                    last = stt(ca[:, j, :], GP[:, j, bass.ds(k, S)], m.PT[:, bass.ds(k * 4 + (c_cw + j), 1)], ca[:, j, :],
                               ALU.mult, ALU.add)
                chain(last)
            link = Link(dve, s.v, base + CF_K - 1)
            nc.vector.memset(m.conv_end[:, :], 0.0).then_inc(s.conv, 1)
            dve.wait_ge(s.means, 1)
            link(nc.vector.tensor_scalar(m.root[:, :], m.psum[:, 0, :], -1.0 / MIX, None, ALU.mult))
            tt(ca, ca, m.root[:, :].unsqueeze(1).broadcast_to([P, 4, S]), ALU.add).then_inc(s.centred, 1)
            dve.wait_ge(s.root, 1)
            link(nc.vector.reciprocal(m.root[:, :], m.root[:, :]))
            tt(ca, ca, m.root[:, :].unsqueeze(1).broadcast_to([P, 4, S]), ALU.mult).then_inc(s.scaled, 1)
        ring.first += n


def phase_branches(nc, m, ph, ring, d, layer, following):
    n = 6
    with ExitStack() as ctx:
        block, s, stale = ph.open(ctx, "gated", "added")
        branch = [m.raw[:, k:k + 4, :] for k in (RAW_G, RAW_SB, RAW_CA)]

        @block.sync
        def _(sp):
            sp.sem_clear(stale)
            ring.stream(sp, d.w_branches[layer], n, following)

        @block.tensor
        def _(pe):
            for u in range(n):
                if u >= 2:
                    pe.wait_ge(s.gated, u - 1)
                unit_products(nc, pe, ring, u, branch[u // 2], m.psum, kc=4, tiles=4, banks=[4 * (u % 2) + j for j in range(4)])

        @block.vector
        def _(dve):
            for u in range(n):
                ring.products(dve, u)
                g = m.gates[:, 4 * u:4 * u + 4, :]
                b = 4 * (u % 2)
                nc.vector.tensor_tensor(g, g, m.psum[:, b:b + 4, :], ALU.mult).then_inc(s.gated, 1)

        @block.gpsimd
        def _(pool):
            for u in range(2, n):
                pool.wait_ge(s.gated, u + 1)
                if u >= 4:
                    pool.wait_ge(s.added, u - 3)
                t = 4 * (u % 2)
                nc.gpsimd.tensor_tensor(m.gates[:, t:t + 4, :], m.gates[:, t:t + 4, :], m.gates[:, 4 * u:4 * u + 4, :],
                                        ALU.add).then_inc(s.added, 1)
        ring.first += n


POST_SEMS = ("y_ready", "y_squared", "y_sum", "y_root")


def post_norm_pe(nc, pe, m, s, squares):
    pe.wait_ge(s.y_squared, 1)
    for c in range(KC):
        mm = nc.tensor.matmul(m.psum[:, 0, :], m.const("ones"), squares[:, c, :], start=(c == 0), stop=(c == KC - 1))
    mm.then_inc(s.y_sum, 1)


def post_norm_act(nc, act, m, s, squares):
    nc.scalar.activation(m.H[:, :, :], m.psum[:, :, :], ACT.Copy).then_inc(s.y_ready, 1)
    nc.scalar.activation(squares, m.psum[:, :, :], ACT.Square).then_inc(s.y_squared, 1)
    act.wait_ge(s.y_sum, 1)
    nc.scalar.activation(m.root[:, :], m.psum[:, 0, :], ACT.Sqrt, bias=m.const("eps"), scale=1.0 / D).then_inc(s.y_root, 1)


def post_norm_dve(nc, dve, m, s, gain):
    link = Link(dve, s.v)
    dve.wait_ge(s.y_root, 1)
    dve.wait_ge(s.y_ready, 1)
    link(nc.vector.reciprocal(m.root[:, :], m.root[:, :]))
    for c in range(KC):
        last = nc.vector.scalar_tensor_tensor(m.H[:, c, :], m.H[:, c, :], gain[:, c:c + 1], m.root[:, :], ALU.mult, ALU.mult)
    link(last)
    nc.vector.tensor_tensor(m.X[:, :, :], m.X[:, :, :], m.H[:, :, :], ALU.add)


def phase_mix_out(nc, m, ph, ring, d, layer, following):
    n = 4
    with ExitStack() as ctx:
        block, s, stale = ph.open(ctx, *POST_SEMS, "v")

        @block.sync
        def _(sp):
            sp.sem_clear(stale)
            ring.stream(sp, d.w_o_2[layer], n, following)

        @block.tensor
        def _(pe):
            for u in range(n):
                unit_products(nc, pe, ring, u, m.gates, m.psum)
            post_norm_pe(nc, pe, m, s, m.gates[:, 8:16, :])

        @block.scalar
        def _(act):
            ring.products(act, n - 1)
            post_norm_act(nc, act, m, s, m.gates[:, 8:16, :])

        @block.vector
        def _(dve):
            post_norm_dve(nc, dve, m, s, m.param("mix_post", KC, layer * KC))
        ring.first += n


def phase_ffn_up(nc, m, ph, ring, d, layer, following):
    n = FF_TILES
    with ExitStack() as ctx:
        block, s, stale = ph.open(ctx, *NORM_SEMS, "v", "last_tap", "read_out", "silu")
        T = on_chip(nc, ctx, "conv", [P, SLOTS, 2, S], F32)
        w0 = PCOL["ffn_w"] + layer * FFN_K * 2 * FF_TILES

        @block.sync
        def _(sp):
            sp.sem_clear(stale)
            ring.stream(sp, d.w_up[layer], n, following)

        @block.tensor
        def _(pe):
            norm_pe(nc, pe, m, s)
            pe.wait_ge(s.root, 1)
            streamed_products(nc, pe, ring, n, m.H, m.psum, s.read_out, k_ready=s.h_ready)

        def tap(u, turn, j, k):
            return m.PT[:, bass.ds(turn * SLOTS + (w0 + k * 2 * FF_TILES + j * FF_TILES + u), 1)]

        @block.scalar
        def _(act):
            norm_act(nc, act, m, s, m.X)

            def body(u, turn):
                ring.products(act, u, turn)
                for j in range(2):
                    b = (2 * u + j) % BANKS
                    last = nc.scalar.activation(T[:, u % SLOTS, j, :], m.psum[:, b, :], ACT.Copy, scale=tap(u, turn, j, 2))
                last.then_inc(s.last_tap, 1)
                act.wait_ge(s.read_out, turn * SLOTS + (u + 1))
                nc.scalar.activation(T[:, u % SLOTS, 0, :], T[:, u % SLOTS, 0, :], ACT.Silu).then_inc(s.silu, 1)
            over_units(act, n, body)

        @block.vector
        def _(dve):
            link = Link(dve, s.v)
            norm_dve(nc, dve, m, s, link, m.X, m.param("ffn_pre", KC, layer * KC), False)
            base = link.n

            def body(u, turn):
                dve.wait_ge(s.last_tap, turn * SLOTS + (u + 1))
                chain = Link(dve, s.v, turn * SLOTS + (base + u))
                t = T[:, u % SLOTS, :, :]
                for k in (1, 0):
                    for j in range(2):
                        b = (2 * u + j) % BANKS
                        lag = FFN_K - 1 - k
                        last = nc.vector.scalar_tensor_tensor(t[:, j, lag:], m.psum[:, b, 0:S - lag], tap(u, turn, j, k),
                                                              t[:, j, lag:], ALU.mult, ALU.add)
                    if k:
                        chain(last)
                last.then_inc(s.read_out, 1)
                dve.wait_ge(s.silu, turn * SLOTS + (u + 1))
                nc.vector.tensor_tensor(m.ff[:, bass.ds(turn * SLOTS + u, 1), :].rearrange("p a n -> p (a n)"),
                                        t[:, 0, :], t[:, 1, :], ALU.mult)
            over_units(dve, n, body)
        ring.first += n


def phase_ffn_down(nc, m, ph, ring, d, layer, following):
    n = FF_TILES // 2
    with ExitStack() as ctx:
        block, s, stale = ph.open(ctx, *POST_SEMS, "v")

        @block.sync
        def _(sp):
            sp.sem_clear(stale)
            ring.stream(sp, d.w_down[layer], n, following)

        @block.tensor
        def _(pe):
            def unit(u, turn):
                w = ring.arrived(pe, u, turn).rearrange("p (k m) -> p k m", k=2)
                for k in range(2):
                    rhs = m.ff[:, bass.ds(turn * 2 * SLOTS + (2 * u + k), 1), :].rearrange("p a n -> p (a n)")
                    for t in range(KC):
                        mm = nc.tensor.matmul(m.psum[:, t, :], w[:, k, t * P:(t + 1) * P], rhs,
                                              start=(u == 0 and k == 0), stop=(u == n - 1 and k == 1))
                mm.then_inc(ring.used, 1)

            unit(0, 0)
            turns = (n - 2) // SLOTS
            with pe.Fori(0, turns) as i:
                for k in range(SLOTS):
                    unit(1 + k, i)
            for u in range(1 + turns * SLOTS, n):
                unit(u, 0)
            post_norm_pe(nc, pe, m, s, m.ff[:, 0:8, :])

        @block.scalar
        def _(act):
            ring.products(act, n - 1)
            post_norm_act(nc, act, m, s, m.ff[:, 0:8, :])

        @block.vector
        def _(dve):
            post_norm_dve(nc, dve, m, s, m.param("ffn_post", KC, layer * KC))
        ring.first += n


def phase_store(nc, m, ph, ring, d):
    with ExitStack() as ctx:
        block, s, stale = ph.open(ctx, "stored")

        @block.sync
        def _(sp):
            sp.dma_start(d.out, m.X[:, :, :]).then_inc(s.stored, 16)
            sp.wait_ge(s.stored, 16)


def build(nc, d, upto=99):
    with ExitStack() as whole:
        def sb(ctx, name, shape, dtype=F32):
            return on_chip(nc, ctx, name, shape, dtype)

        m = Memory()
        m.X = sb(whole, "x", [P, KC, S])
        m.H = sb(whole, "h", [P, KC, S])
        m.PT = sb(whole, "params", [P, PCOLS])
        m.CT = sb(whole, "consts", [P, CCOLS])
        m.WR = sb(whole, "router_w", [P, DEPTH, KC, GROUPS + EXPERTS])
        m.RB = sb(whole, "router_b", [P, DEPTH, GROUPS + EXPERTS])
        m.mod = sb(whole, "mod", [P, DEPTH * 48])
        m.gain = sb(whole, "gain", [P, DEPTH, 2, KC])
        m.c_act = sb(whole, "c_act", [P, KC, 1])
        m.root = sb(whole, "root", [P, S])
        m.priority = sb(whole, "priority", [P, TT, 4])
        m.conv_end = sb(whole, "conv_end", [P, 1])
        m.psum = whole.enter_context(nc.psum_tensor("psum", [P, BANKS, S], F32))
        ring = Ring(nc, whole)
        ph = Phases(nc)
        m.const = lambda name: m.CT[:, CCOL[name]:CCOL[name] + dict(CONST_TILES)[name]]
        m.param = lambda name, n, at=0: m.PT[:, PCOL[name] + at:PCOL[name] + at + n]

        def mod(layer, k):
            return m.mod[:, 48 * layer + KC * k:48 * layer + KC * (k + 1)]

        def moe(layer, following):
            with ExitStack() as part:
                m.cb = sb(part, "expert_weights", [P, EXPERTS, S])
                phase_router(nc, m, ph, ring, layer, mod(layer, 3), m.gain[:, layer, 1, :])
                phase_experts(nc, m, ph, ring, d.moe[layer], mod(layer, 5), following)

        def finish():
            phase_store(nc, m, ph, ring, d)

        with ExitStack() as part:
            m.sin, m.cos = sb(part, "rope_sin", [P, S]), sb(part, "rope_cos", [P, S])
            phase_load(nc, m, ph, ring, d)
            phase_modulation(nc, m, ph, ring, d, d.mla_w_down)
            m.lat = sb(part, "latents", [P, 4, S])
            m.sq4 = sb(part, "sq4", [P, 4, S])
            m.r4 = sb(part, "r4", [P, 3, S])
            m.k_pe = sb(part, "k_pe", [P, S])
            m.qn, m.kn = sb(part, "q_nope", [P, HEADS, S]), sb(part, "k_nope", [P, HEADS, S])
            m.qp, m.vt = sb(part, "q_pe", [P, 4, S]), sb(part, "v_tok", [P, TT, D])
            phase_latents(nc, m, ph, ring, d, d.mla_w_heads)
            with ExitStack() as inner:
                m.sq8, m.r8 = sb(inner, "sq8", [P, 2, 4, S]), sb(inner, "r8", [P, 2, 4, S])
                phase_heads(nc, m, ph, ring, d, d.mla_w_o)
            phase_attention(nc, m, ph, ring, d)
            phase_residual(nc, m, ph, ring, d.mla_w_o, mod(0, 2), d.moe[0] if upto > 0 else None)
        if upto == 0:
            return finish()
        moe(0, d.hy_w_in if upto > 1 else None)
        if upto == 1:
            return finish()
        with ExitStack() as part:
            m.xv = sb(part, "x1_x2_v", [P, 24, S])
            phase_hyena_in(nc, m, ph, ring, d, d.hy_w_out)
            m.hdn = sb(part, "filter_hidden", [FILTER_WIDTH, S])
            m.fwd, m.inv = sb(part, "dft_fwd", [P, 2, TT, 256]), sb(part, "dft_inv", [P, 2, 4, 256])
            phase_filter_mlp(nc, m, ph, ring, d)
            for order in range(2):
                for half in range(2):
                    phase_long_conv(nc, m, ph, ring, d, order, half)
            phase_residual(nc, m, ph, ring, d.hy_w_out, mod(1, 2), d.moe[1] if upto > 2 else None,
                           rhs=m.xv[:, 16:24, :], even_odd=True)
        if upto == 2:
            return finish()
        moe(1, d.w_proj[0] if upto > 3 else None)
        if upto == 3:
            return finish()
        for layer in range(DEPTH):
            with ExitStack() as part:
                m.raw = sb(part, "projections", [P, 28, S])
                with ExitStack() as inner:
                    m.vr = sb(inner, "v_tok", [P, TT, MIX])
                    phase_project(nc, m, ph, ring, d, layer, d.w_gates[layer])
                    phase_retention(nc, m, ph, ring, d)
                m.gates = sb(part, "gates", [P, 24, S])
                phase_gates(nc, m, ph, ring, d, layer, d.w_branches[layer])
                phase_branches(nc, m, ph, ring, d, layer, d.w_o_2[layer])
                phase_mix_out(nc, m, ph, ring, d, layer, d.w_up[layer] if upto > 4 + 2 * layer else None)
            if upto == 4 + 2 * layer:
                return finish()
            with ExitStack() as part:
                m.ff = sb(part, "ff", [P, FF_TILES, S])
                phase_ffn_up(nc, m, ph, ring, d, layer, d.w_down[layer])
                phase_ffn_down(nc, m, ph, ring, d, layer, d.w_proj[1] if layer == 0 and upto > 5 else None)
            if upto == 5 + 2 * layer:
                return finish()
        finish()


def table_consts():
    f = np.float32
    parts = {"ident": np.eye(P), "ones": np.ones((P, P)), "ones64": np.kron(np.eye(2), np.ones((64, 64)))}
    rot = np.zeros((P, P))
    for b in (0, 64):
        for j in range(32):
            rot[b + 32 + j, b + j] = -1
            rot[b + j, b + 32 + j] = 1
    parts["rot"] = rot
    parts["inv_freq"] = (f(1) / (f(10000.0) ** (np.arange(0, 64, 2, dtype=f) / f(64))))[np.arange(P) % 32][:, None]
    parts["eps"] = np.full((P, 1), EPS)
    parts["zero"] = np.zeros((P, 1))
    consts = np.concatenate([parts[name].astype(f) for name, _ in CONST_TILES], axis=1)

    order = np.concatenate([np.arange(0, S, 2), np.arange(1, S, 2)])
    t = np.linspace(0.0, 1.0, S, dtype=f)[:, None]
    w = (f(2.0 * math.pi) * np.arange(S, dtype=f)[:, None] / f(S)).astype(f)
    fr = np.linspace(1e-4, 15, 16, dtype=f)[None, :]
    z = np.concatenate([t, np.cos(fr * w), -np.sin(fr * w)], axis=-1).astype(f)
    deltas = np.abs(np.linspace(math.log(0.3) / 1e-2, math.log(1.5) / 1e-2, D, dtype=f))
    decay = np.exp(-t * deltas).astype(f)[order].reshape(TT, P, D).transpose(1, 0, 2)
    k = np.arange(256)
    angle = math.pi * (2 * k[None, :] + 1) * order[:, None] / 1024.0
    fwd = np.stack([np.cos(angle), np.sin(angle)]).reshape(2, TT, P, 256).transpose(2, 0, 1, 3)
    back = np.stack([np.cos(angle).T, np.sin(angle).T]) / 512.0
    inv = back.reshape(2, 2, P, 2, 256).transpose(2, 3, 0, 1, 4).reshape(P, 2, 4, 256)

    gamma = 1.0 - np.exp2(-5.0 - np.arange(RET_HEADS))
    lag = np.arange(S)[None, :] - np.arange(P)[:, None]
    ret = np.where(lag[:, None, :] >= 0, gamma[None, :, None] ** np.maximum(lag, 0)[:, None, :], 0.0) / 8.0
    inv_r = f(10000.0) ** (-np.arange(32, dtype=f) / f(32))
    ang = (np.arange(S, dtype=f)[None, :] * inv_r[np.arange(P) % 32][:, None]).astype(f)
    rotary = np.stack([np.cos(ang), np.sin(ang)], axis=1)
    return {name: np.ascontiguousarray(a, dtype=f) for name, a in
            (("consts", consts), ("zT", z[order].T), ("decay", decay), ("dft_fwd", fwd), ("dft_inv", inv),
             ("ret_decay", ret), ("ret_rotary", rotary))}


def feature_tiles(a):
    return a.reshape(-1, P).T


def padded_rows(a):
    return np.concatenate([a.T, np.zeros_like(a.T)], axis=0)


def units(w, cols=256):
    k, n = w.shape[0] // P, w.shape[1] // cols
    return w.reshape(k, P, n, cols).transpose(2, 1, 0, 3).reshape(n, P, k * cols)


def layout(i):
    a = {k: np.asarray(v) for k, v in i.items()}
    out = table_consts()
    out["x"] = a["x"][0].T.reshape(KC, P, S).transpose(1, 0, 2)
    out["positions"] = np.broadcast_to(a["positions"].reshape(1, S), (P, S))
    twice = lambda v: np.concatenate([v, v])
    hy = lambda name: a[name][0]
    params = {
        "c": a["c"], "ada_b": a["ada_b"], "norm_mix_g": a["norm_mix_g"], "norm_ffn_g": a["norm_ffn_g"],
        "q_a_g": a["mla_q_a_g"], "kv_a_g": a["mla_kv_a_g"],
        "q_nope_g": a["mla_q_norm_g"][0, :NOPE], "q_pe_g": twice(a["mla_q_norm_g"][0, NOPE:]),
        "k_nope_g": a["mla_k_norm_g"][0, :NOPE], "k_pe_g": twice(a["mla_k_norm_g"][0, NOPE:]),
        "hy_b_in": hy("hy_b_in"), "hy_conv_w": hy("hy_conv_w"), "hy_conv_b": hy("hy_conv_b"),
        "hy_filt_bias": hy("hy_filt_bias"),
        "mix_pre": a["norm_mix_pre_2"], "mix_post": a["norm_mix_post_2"],
        "ffn_pre": a["norm_ffn_pre_2"], "ffn_post": a["norm_ffn_post_2"],
        "sc_w": a["sc_conv_w_2"], "cf_w": a["cf_conv_w_2"], "cf_b": a["cf_conv_b_2"],
        "cf_g": a["cf_ln_g_2"], "cf_lb": a["cf_ln_b_2"], "ffn_w": a["ffn_conv_w_2"],
    }
    cols = {name: feature_tiles(v) for name, v in params.items()}
    cols["hy_fb"] = padded_rows(np.concatenate([a["hy_f_b1"], a["hy_f_b2"], a["hy_f_b3"]]))
    cols["hy_ff"] = padded_rows(np.concatenate([a["hy_f_freq1"], a["hy_f_freq2"], a["hy_f_freq3"]]))
    out["params"] = np.concatenate([cols[name] for name, _ in PARAM_TILES], axis=1)
    assert out["params"].shape == (P, PCOLS)
    wr = np.concatenate([a["moe_wg"], a["moe_we"]], axis=2)
    out["router_w"] = wr.reshape(DEPTH, KC, P, GROUPS + EXPERTS).transpose(2, 0, 1, 3)
    out["router_b"] = np.broadcast_to(np.concatenate([a["moe_bg"], a["moe_be"]], axis=1)[None], (P, DEPTH, 20))

    out["ada_w"] = np.concatenate([units(a["ada_w"][l]) for l in range(DEPTH)])
    wd = a["mla_w_down"][0]
    out["mla_w_down"] = units(np.concatenate([wd, wd[:, -ROPE:]], axis=1))
    uq = a["mla_w_uq"][0].reshape(Q_LORA, HEADS, QK_HEAD)
    uq = np.concatenate([uq[:, :, :NOPE].reshape(Q_LORA, -1), uq[:, :, NOPE:].reshape(Q_LORA, -1)], axis=1)
    uq = np.concatenate([uq, np.zeros((Q_LORA, 512), uq.dtype)], axis=1)
    ukv = a["mla_w_ukv"][0].reshape(KV_LORA, HEADS, NOPE + V_HEAD)
    ukv = np.concatenate([ukv[:, :, :NOPE].reshape(KV_LORA, -1), ukv[:, :, NOPE:].reshape(KV_LORA, -1)], axis=1)
    out["mla_w_heads"] = np.concatenate([units(uq, 1024), ukv[None]])
    out["mla_w_o"] = units(a["mla_w_o"][0])
    for l in range(DEPTH):
        g = []
        for k in range(GROUPS):
            for e in range(k * PER_GROUP, (k + 1) * PER_GROUP):
                g += [units(a["moe_w_gate"][l, e]), units(a["moe_w_up"][l, e])]
            g.append(units(a["moe_w_down"][l, k * PER_GROUP:(k + 1) * PER_GROUP].reshape(PER_GROUP * D_EXPERT, D)))
        out[f"moe_{l}"] = np.concatenate(g)
        w = a["w_in_2"][l]
        q, v, r, g = w[:, :512], w[:, 512:1024], w[:, 1024:4096], w[:, 4096:]
        out[f"w_proj_{l}"] = units(np.concatenate([q, r, v], axis=1))
        out[f"w_gates_{l}"] = units(g)
        out[f"w_branches_{l}"] = np.concatenate([units(a[n][l], 512) for n in ("w_ret_out_2", "w_sc_out_2", "w_cf_out_2")])
        out[f"w_o_2_{l}"] = units(a["w_o_2"][l])
        up = a["w_up_2"][l].reshape(D, 2, FF_TILES, P).transpose(0, 2, 1, 3).reshape(D, -1)
        out[f"w_up_{l}"] = units(up)
        dn = a["w_down_2"][l].reshape(FF_TILES // 2, 2, P, D)
        out[f"w_down_{l}"] = dn.transpose(0, 2, 1, 3).reshape(FF_TILES // 2, P, 2 * D)
    out["hy_w_in"] = units(hy("hy_w_in"))
    out["hy_w_out"] = units(hy("hy_w_out"))
    out["hy_f_w1"], out["hy_f_w2"], out["hy_f_w3"] = hy("hy_f_w1"), hy("hy_f_w2"), hy("hy_f_w3")
    out["hy_f_w4"] = hy("hy_f_w4").reshape(FILTER_WIDTH, 2, 2, D)
    return {k: np.ascontiguousarray(v) for k, v in out.items()}


def declare(nc, arrays):
    found = {}
    for name, v in arrays.items():
        ap = nc.dram_tensor("in_" + name, list(v.shape), mybir.dt.from_np(v.dtype), kind="ExternalInput").ap()
        if name[-2:] in ("_0", "_1"):
            found.setdefault(name[:-2], []).append(ap)
        else:
            found[name] = ap
    found["out"] = nc.dram_tensor("out_x", [P, KC, S], F32, kind="ExternalOutput").ap()
    return namedtuple("Dram", found)(*found.values())


def kernel(**inputs):
    import concourse.bacc as bacc
    from concourse.bass_utils import run_bass_kernel_spmd

    arrays = layout(inputs)
    nc = bacc.Bacc("TRN2", target_bir_lowering=False, num_devices=1)
    build(nc, declare(nc, arrays))
    r = run_bass_kernel_spmd(nc, [{"in_" + k: v for k, v in arrays.items()}], core_ids=[0])
    out = np.asarray(r.results[0]["out_x"])
    return np.ascontiguousarray(out.transpose(1, 0, 2).reshape(D, S).T)[None]
```

```python
import itertools
import math
from collections import namedtuple
from contextlib import ExitStack

import numpy as np

import concourse.bass as bass
from concourse import mybir

F32 = mybir.dt.float32
F32R = mybir.dt.float32r
I32 = mybir.dt.int32
ALU = mybir.AluOpType
ACT = mybir.ActivationFunctionType
AX = mybir.AxisListType

P = 128
D = 1024
S = 512
DEPTH = 2
KC = D // P
TT = S // P
UNIT = 2048
TURN = 4
BANKS = 8

HEADS, Q_LORA, KV_LORA, NOPE, ROPE, V_HEAD = 8, 256, 128, 128, 64, 128
QK_HEAD = NOPE + ROPE
GROUPS, PER_GROUP, D_EXPERT = 4, 4, 256
EXPERTS = GROUPS * PER_GROUP
FILTER_EMB, FILTER_WIDTH = 33, 64
RET_HEADS, RET_QK, RET_V = 4, 64, 128
MIX = 512
D_FF = 2816
FF_TILES = D_FF // P
CF_K, SC_K, FFN_K = 31, 3, 3
EPS = 1e-6

PARAM_TILES = [
    ("ada_b", DEPTH * 48), ("norm_mix_g", DEPTH * KC), ("norm_ffn_g", DEPTH * KC),
    ("q_a_g", 2), ("kv_a_g", 1), ("q_nope_g", 1), ("q_pe_g", 1), ("k_nope_g", 1), ("k_pe_g", 1),
    ("hy_b_in", 24), ("hy_conv_w", 72), ("hy_conv_b", 24), ("hy_filt_bias", 16),
    ("hy_fb", 3), ("hy_ff", 3),
    ("mix_pre", DEPTH * KC), ("mix_post", DEPTH * KC), ("ffn_pre", DEPTH * KC), ("ffn_post", DEPTH * KC),
    ("sc_w", DEPTH * SC_K * 4), ("cf_w", DEPTH * CF_K * 4), ("cf_b", DEPTH * 4),
    ("cf_g", DEPTH * 4), ("cf_lb", DEPTH * 4), ("ffn_w", DEPTH * FFN_K * 2 * FF_TILES),
]
PCOL, PCOLS = {}, 0
for _name, _n in PARAM_TILES:
    PCOL[_name] = PCOLS
    PCOLS += _n

NORM_ROWS = (0, 4, 8, 16, 20, 24)
CONST_TILES = [("ident", P), ("ones", P), ("ones64", P), ("rot", P), ("pick_one", 2 * NORM_ROWS[-1] - 1),
               ("pick_two", 2 * NORM_ROWS[-1] - 1), ("inv_freq", 1), ("eps", 1), ("zero", 1)]
CCOL, CCOLS = {}, 0
for _name, _n in CONST_TILES:
    CCOL[_name] = CCOLS
    CCOLS += _n

TWO_PI_A = 6.28125
TWO_PI_B = math.floor((2 * math.pi - TWO_PI_A) * 2.0 ** 21) / 2.0 ** 21
TWO_PI_C = float(np.float32(2 * math.pi - TWO_PI_A - TWO_PI_B))
PI_DOWN = 3.1415925
ROUND_MAGIC = 12582912.0


BUFFERS = itertools.count()


def on_chip(nc, ctx, name, shape, dtype):
    return ctx.enter_context(nc.sbuf_tensor(f"{name}_{next(BUFFERS)}", shape, dtype))


class Memory:
    pass


class Phases:

    POOL = 44

    def __init__(self, nc):
        self.nc = nc
        self.pools = [[nc.alloc_semaphore(f"phase{h}_{n}") for n in range(self.POOL)] for h in range(2)]
        self.turn = 0

    def open(self, ctx, *names):
        mine, other = self.pools[self.turn], self.pools[1 - self.turn]
        self.turn = 1 - self.turn
        assert len(names) <= self.POOL
        block = ctx.enter_context(self.nc.Block())
        stale = range(other[0].num, other[-1].num + 1)
        return block, namedtuple("Signals", names)(*mine[:len(names)]), stale


class Link:

    def __init__(self, eng, sem, start=0):
        self.eng, self.sem, self.start, self.n = eng, sem, start, 0

    def __call__(self, instruction):
        instruction.then_inc(self.sem, 1)
        self.n += 1
        self.eng.wait_ge(self.sem, self.start + self.n)


class Ring:

    AHEAD = 2

    def __init__(self, nc, ctx):
        self.nc = nc
        self.raw = on_chip(nc, ctx, "weights_raw", [P, 2, UNIT], F32)
        self.high = on_chip(nc, ctx, "weights_high", [P, 2, UNIT], F32R)
        self.low = on_chip(nc, ctx, "weights_low", [P, 2, UNIT], F32R)
        self.loaded = [nc.alloc_semaphore(f"weights_loaded_{k}") for k in range(2)]
        self.high_done = nc.alloc_semaphore("weights_high_done")
        self.low_done = nc.alloc_semaphore("weights_low_done")
        self.used = nc.alloc_semaphore("weights_used")
        self.first = 0
        self.issued = 0
        self.lowered = 0

    def _load(self, sp, src):
        g = self.issued
        if g >= 2:
            sp.wait_ge(self.low_done, g - 1)
        sp.dma_start(self.raw[:, g % 2, :], src).then_inc(self.loaded[g % 2], 16)
        self.issued += 1

    def stream(self, sp, src, n, following=None):
        while self.issued < self.first + n and self.issued < 2:
            self._load(sp, src[self.issued - self.first, :, :])
        u = self.issued - self.first
        turns = (n - u) // TURN
        if turns > 1:
            g0 = self.issued
            with sp.Fori(0, turns) as i:
                for k in range(TURN):
                    sp.wait_ge(self.low_done, i * TURN + (g0 + k - 1))
                    sp.dma_start(self.raw[:, (g0 + k) % 2, :],
                                 src[bass.ds(i * TURN + (u + k), 1), :, :].rearrange("a p n -> p (a n)"))\
                        .then_inc(self.loaded[(g0 + k) % 2], 16)
            self.issued += turns * TURN
        while self.issued < self.first + n:
            self._load(sp, src[self.issued - self.first, :, :])
        if following is not None:
            for k in range(self.AHEAD):
                self._load(sp, following[k, :, :])

    def make_high(self, act, u, turn=0, per=4):
        g = self.first + u
        act.wait_ge(self.loaded[g % 2], turn * (8 * per) + 16 * (g // 2 + 1))
        if g >= 2:
            act.wait_ge(self.used, turn * per + (g - 1))
        self.nc.scalar.activation(self.high[:, g % 2, :], self.raw[:, g % 2, :], ACT.Copy).then_inc(self.high_done, 1)

    def _make_low(self, pool, g, turn=0):
        pool.wait_ge(self.high_done, turn * TURN + (g + 1))
        self.nc.gpsimd.tensor_tensor(self.low[:, g % 2, :], self.raw[:, g % 2, :], self.high[:, g % 2, :].bitcast(F32),
                                     ALU.subtract).then_inc(self.low_done, 1)

    def make_lows(self, pool, n, more=True):
        end = self.first + n + (self.AHEAD if more else 0)
        turns = (end - self.lowered) // TURN
        if turns > 1:
            with pool.Fori(0, turns) as i:
                for k in range(TURN):
                    self._make_low(pool, self.lowered + k, i)
            self.lowered += turns * TURN
        while self.lowered < end:
            self._make_low(pool, self.lowered)
            self.lowered += 1

    def parts(self, pe, u, turn=0, per=4):
        g = self.first + u
        pe.wait_ge(self.low_done, turn * per + (g + 1))
        return self.high[:, g % 2, :], self.low[:, g % 2, :]

    def products(self, eng, u, turn=0, per=4):
        eng.wait_ge(self.used, turn * per + (self.first + u + 1))


def split_matmul(nc, out, w, rhs, start, stop):
    nc.tensor.matmul(out, w[1], rhs[0], start=start, stop=False)
    nc.tensor.matmul(out, w[0], rhs[0], start=False, stop=False)
    return nc.tensor.matmul(out, w[0], rhs[1], start=False, stop=stop)


def unit_products(nc, pe, ring, u, rhs, psum, kc=KC, tiles=2, turn=0, per=4, k_ready=None, banks=None):
    w = [x.rearrange("p (k m) -> p k m", k=kc) for x in ring.parts(pe, u, turn, per)]
    order = [(j, k) for j in range(tiles) for k in range(kc)]
    if k_ready is not None:
        order = [(j, k) for k in range(kc) for j in range(tiles)]
    for j, k in order:
        b = banks[j] if banks else (tiles * u + j) % BANKS
        if k_ready is not None and j == 0:
            k_ready(k)
        mm = split_matmul(nc, psum[:, b, :], [x[:, k, j * P:(j + 1) * P] for x in w],
                          [x[:, k, :] for x in rhs], k == 0, k == kc - 1)
    mm.then_inc(ring.used, 1)


def streamed_products(nc, pe, ring, n, rhs, psum, read_out, k_ready=None):
    for u in range(min(n, TURN)):
        unit_products(nc, pe, ring, u, rhs, psum, k_ready=k_ready if u == 0 else None)
    turns = (n - TURN) // TURN
    if turns > 1:
        with pe.Fori(0, turns) as i:
            for k in range(TURN):
                pe.wait_ge(read_out, i * TURN + (k + 1))
                unit_products(nc, pe, ring, TURN + k, rhs, psum, turn=i)
    else:
        turns = 0
    for u in range(TURN * (turns + 1), n):
        pe.wait_ge(read_out, u - TURN + 1)
        unit_products(nc, pe, ring, u, rhs, psum)


def over_units(eng, n, body):
    turns = n // TURN
    if turns > 1:
        with eng.Fori(0, turns) as i:
            for k in range(TURN):
                body(k, i)
    else:
        turns = 0
    for u in range(TURN * turns, n):
        body(u, 0)


NORM_SEMS = ("squared", "summed", "root", "scaled", "h_high", "h_ready")


def norm_act(nc, act, m, s, src, shift=None):
    for c in range(KC):
        if c >= 4:
            act.wait_ge(s.summed, c - 3)
        nc.scalar.activation(m.F[:, c % 4, :], src[:, c, :], ACT.Square).then_inc(s.squared, 1)
    act.wait_ge(s.summed, KC)
    nc.scalar.activation(m.root[:, :], m.psum[:, 7, :], ACT.Sqrt, bias=m.const("eps"), scale=1.0 / D)\
        .then_inc(s.root, 1)
    for c in range(KC):
        act.wait_ge(s.scaled, c + 1)
        if shift is None:
            nc.scalar.activation(m.Hh[:, c, :], m.F[:, c % 4, :], ACT.Copy).then_inc(s.h_high, 1)
        else:
            nc.scalar.activation(m.Hh[:, c, :], m.F[:, c % 4, :], ACT.Identity, bias=shift[:, c:c + 1])
            nc.scalar.activation(m.F[:, c % 4, :], m.F[:, c % 4, :], ACT.Identity, bias=shift[:, c:c + 1])\
                .then_inc(s.h_high, 1)


def norm_pe(nc, pe, m, s):
    for c in range(KC):
        pe.wait_ge(s.squared, c + 1)
        nc.tensor.matmul(m.psum[:, 7, :], m.const("ones"), m.F[:, c % 4, :], start=(c == 0), stop=(c == KC - 1))\
            .then_inc(s.summed, 1)


def norm_dve(nc, dve, m, s, link, src, gain):
    dve.wait_ge(s.root, 1)
    link(nc.vector.reciprocal(m.root[:, :], m.root[:, :]))
    for c in range(KC + 2):
        if c < KC:
            if c >= 4:
                dve.wait_ge(s.h_ready, c - 3)
            nc.vector.scalar_tensor_tensor(m.F[:, c % 4, :], src[:, c, :], gain[:, c:c + 1], m.root[:, :],
                                           ALU.mult, ALU.mult).then_inc(s.scaled, 1)
        if c >= 2:
            dve.wait_ge(s.h_high, c - 1)
            low_part(nc, m.Hl[:, c - 2, :], m.F[:, (c - 2) % 4, :], m.Hh[:, c - 2, :]).then_inc(s.h_ready, 1)


def h_tiles(pe, s):
    return lambda k: pe.wait_ge(s.h_ready, k + 1)


def low_part(nc, low, value, high):
    return nc.vector.tensor_tensor(low, value, high.bitcast(F32), ALU.subtract)


def phase_load(nc, m, ph, ring, d):
    with ExitStack() as ctx:
        block, s, stale = ph.open(ctx, "here", "v", "c_ready", "tables", "router_high", "mod_read",
                                  *[f"mod_loaded_{k}" for k in range(MOD_SLOTS)])
        pos = on_chip(nc, ctx, "pos_i", [P, S], I32)
        t0 = on_chip(nc, ctx, "angle", [P, S], F32)
        t1 = on_chip(nc, ctx, "turns", [P, S], F32)
        t2 = on_chip(nc, ctx, "angle2", [P, S], F32)
        wr = on_chip(nc, ctx, "router_w", [P, DEPTH, KC, GROUPS + EXPERTS], F32)
        W = on_chip(nc, ctx, "mod_weights", [P, MOD_SLOTS, UNIT], F32)
        loaded = s[-MOD_SLOTS:]

        @block.sync
        def _(sp):
            sp.dma_start(m.c_act[:, :], d.c).then_inc(s.here, 16)
            sp.wait_ge(s.here, 16)
            for dst, src in ((m.PT[:, :], d.params), (m.CT[:, :], d.consts), (pos[:, :], d.positions),
                             (m.X[:, :, :], d.x), (wr[:, :, :, :], d.router_w), (m.RB[:, :, :], d.router_b)):
                sp.dma_start(dst, src).then_inc(s.here, 16)
            for u in range(MOD_FIRST):
                if u >= MOD_SLOTS:
                    sp.wait_ge(s.mod_read, u - MOD_SLOTS + 1)
                sp.dma_start(W[:, u % MOD_SLOTS, :], d.ada_w[u, :, :]).then_inc(loaded[u % MOD_SLOTS], 16)
            ring.stream(sp, None, 0, following=d.mla_w_down)
            sp.wait_ge(s.here, 112)

        @block.gpsimd
        def _(pool):
            for k in range(4):
                nc.gpsimd.memset(m.priority[:, :, k:k + 1], 4.0 - k)
            ring.make_lows(pool, 0)

        @block.vector
        def _(dve):
            dve.wait_ge(s.c_ready, 1)
            for u in range(MOD_FIRST):
                dve.wait_ge(loaded[u % MOD_SLOTS], 16 * (u // MOD_SLOTS + 1))
                modulation_unit(nc, m, W[:, u % MOD_SLOTS, :], m.mod, 2 * u).then_inc(s.mod_read, 1)
            link = Link(dve, s.v)
            dve.wait_ge(s.here, 112)
            dve.wait_ge(s.mod_read, MOD_FIRST)
            modulation_gains(nc, link, m, 0, 0, 2 * MOD_FIRST)
            dve.wait_ge(s.router_high, 1)
            nc.vector.tensor_tensor(m.WRl[:, :, :, :], wr[:, :, :, :], m.WRh[:, :, :, :].bitcast(F32), ALU.subtract)
            link(nc.vector.tensor_copy(t1[:, :], pos[:, :]))
            link(nc.vector.tensor_scalar(t0[:, :], t1[:, :], m.const("inv_freq"), None, ALU.mult))
            for table, quarter in ((m.sin, 0.0), (m.cos, math.pi / 2)):
                link(nc.vector.tensor_scalar(t1[:, :], t0[:, :], 1.0 / (2 * math.pi), quarter / (2 * math.pi),
                                             ALU.mult, ALU.add))
                link(nc.vector.tensor_scalar(t1[:, :], t1[:, :], ROUND_MAGIC, None, ALU.add))
                link(nc.vector.tensor_scalar(t1[:, :], t1[:, :], ROUND_MAGIC, None, ALU.subtract))
                link(nc.vector.scalar_tensor_tensor(t2[:, :], t1[:, :], -TWO_PI_A, t0[:, :], ALU.mult, ALU.add))
                if quarter:
                    link(nc.vector.tensor_scalar(t2[:, :], t2[:, :], quarter, None, ALU.add))
                link(nc.vector.scalar_tensor_tensor(t2[:, :], t1[:, :], -TWO_PI_B, t2[:, :], ALU.mult, ALU.add))
                link(nc.vector.scalar_tensor_tensor(t2[:, :], t1[:, :], -TWO_PI_C, t2[:, :], ALU.mult, ALU.add))
                nc.vector.tensor_scalar(table[:, :], t2[:, :], PI_DOWN, -PI_DOWN, ALU.min, ALU.max)\
                    .then_inc(s.tables, 1)

        @block.scalar
        def _(act):
            act.wait_ge(s.here, 16)
            nc.scalar.activation(m.c_act[:, :], m.c_act[:, :], ACT.Silu).then_inc(s.c_ready, 1)
            act.wait_ge(s.here, 112)
            nc.scalar.activation(m.WRh[:, :, :, :], wr[:, :, :, :], ACT.Copy).then_inc(s.router_high, 1)
            for u in range(Ring.AHEAD):
                ring.make_high(act, u)
            for n, table in enumerate((m.sin, m.cos)):
                act.wait_ge(s.tables, n + 1)
                nc.scalar.activation(table[:, :], table[:, :], ACT.Sin)


MOD_UNITS, MOD_SLOTS, MOD_TILES = 24, 4, 48
MOD_FIRST, MOD_HEADS = 8, 6
MOD_REST = MOD_UNITS - MOD_FIRST - MOD_HEADS


def modulation_unit(nc, m, w, out, t):
    for j in range(2):
        last = nc.vector.tensor_tensor_reduce(out=w[:, j * D:(j + 1) * D], in0=w[:, j * D:(j + 1) * D], in1=m.c_act[:, :],
                                              scale=1.0, scalar=0.0, op0=ALU.mult, op1=ALU.add,
                                              accum_out=out[:, t + j:t + j + 1])
    return last


def modulation_gains(nc, link, m, layer, first=0, end=MOD_TILES):
    at = MOD_TILES * layer
    part = m.mod[:, at + first:at + end]
    link(nc.vector.tensor_tensor(part, part, m.param("ada_b", end - first, at + first), ALU.add))
    for which, name, col in ((0, "norm_mix_g", KC), (1, "norm_ffn_g", 4 * KC)):
        if first <= col < end:
            nc.vector.scalar_tensor_tensor(m.gain[:, layer, which, :], m.mod[:, at + col:at + col + KC], 1.0,
                                           m.param(name, KC, layer * KC), ALU.add, ALU.mult)


BESIDE_SEMS = ("mod_read", "mod_loaded_0", "mod_loaded_1")


def load_beside(act, s, W, src, k):
    if k >= 2:
        act.wait_ge(s.mod_read, k - 1)
    act.dma_start(W[:, k % 2, :], src[k, :, :]).then_inc((s.mod_loaded_0, s.mod_loaded_1)[k % 2], 16)


def modulate_beside(nc, dve, m, s, W, k, tile):
    dve.wait_ge((s.mod_loaded_0, s.mod_loaded_1)[k % 2], 16 * (k // 2 + 1))
    modulation_unit(nc, m, W[:, k % 2, :], m.mod, tile).then_inc(s.mod_read, 1)


def phase_latents(nc, m, ph, ring, d, following):
    n = 2
    with ExitStack() as ctx:
        block, s, stale = ph.open(ctx, *NORM_SEMS, "v", "raw", "raw_sq", "sums", "roots", "rot_in", "rot_out",
                                  "normed", "lat_high")

        @block.sync
        def _(sp):
            sp.sem_clear(stale)
            ring.stream(sp, d.mla_w_down, n, following)

        @block.scalar
        def _(act):
            norm_act(nc, act, m, s, m.X, shift=m.mod[:, 0:KC])
            ring.make_high(act, 2)
            ring.products(act, 1)
            nc.scalar.activation(m.lat[:, :, :], m.psum[:, 0:4, :], ACT.Copy).then_inc(s.raw, 1)
            act.wait_ge(s.raw, 1)
            nc.scalar.activation(m.sq4[:, :, :], m.psum[:, 0:4, :], ACT.Square).then_inc(s.raw_sq, 1)
            act.wait_ge(s.sums, 1)
            for b, width in ((0, Q_LORA), (1, KV_LORA), (2, ROPE)):
                nc.scalar.activation(m.r4[:, b, :], m.psum[:, 4 + b, :], ACT.Sqrt, bias=m.const("eps"),
                                     scale=1.0 / width).then_inc(s.roots, 1)
            act.wait_ge(s.normed, 1)
            nc.scalar.activation(m.lat_h[:, :, :], m.lat[:, 0:3, :], ACT.Copy).then_inc(s.lat_high, 1)
            ring.make_high(act, 3)

        @block.tensor
        def _(pe):
            norm_pe(nc, pe, m, s)
            unit_products(nc, pe, ring, 0, m.Hs, m.psum, k_ready=h_tiles(pe, s))
            unit_products(nc, pe, ring, 1, m.Hs, m.psum)
            pe.wait_ge(s.raw_sq, 1)
            nc.tensor.matmul(m.psum[:, 4, :], m.const("ones"), m.sq4[:, 0, :], start=True, stop=False)
            nc.tensor.matmul(m.psum[:, 4, :], m.const("ones"), m.sq4[:, 1, :], start=False, stop=True)
            nc.tensor.matmul(m.psum[:, 5, :], m.const("ones"), m.sq4[:, 2, :], start=True, stop=True)
            nc.tensor.matmul(m.psum[:, 6, :], m.const("ones64"), m.sq4[:, 3, :], start=True, stop=True)\
                .then_inc(s.sums, 1)
            pe.wait_ge(s.rot_in, 1)
            nc.tensor.matmul(m.psum[:, 0, :], m.const("rot"), m.lat[:, 3, :], start=True, stop=True)\
                .then_inc(s.rot_out, 1)

        @block.vector
        def _(dve):
            link = Link(dve, s.v)
            norm_dve(nc, dve, m, s, link, m.X, m.gain[:, 0, 0, :])
            dve.wait_ge(s.roots, 3)
            link(nc.vector.reciprocal(m.r4[:, 0:3, :], m.r4[:, 0:3, :]))
            for t, root, g in ((0, 0, m.param("q_a_g", 1, 0)), (1, 0, m.param("q_a_g", 1, 1)),
                               (2, 1, m.param("kv_a_g", 1))):
                last = nc.vector.scalar_tensor_tensor(m.lat[:, t, :], m.lat[:, t, :], g, m.r4[:, root, :],
                                                      ALU.mult, ALU.mult)
            last.then_inc(s.normed, 1)
            nc.vector.scalar_tensor_tensor(m.lat[:, 3, :], m.lat[:, 3, :], m.param("k_pe_g", 1), m.r4[:, 2, :],
                                           ALU.mult, ALU.mult).then_inc(s.rot_in, 1)
            dve.wait_ge(s.rot_in, 1)
            link(nc.vector.tensor_tensor(m.k_pe[:, :], m.lat[:, 3, :], m.cos[:, :], ALU.mult))
            dve.wait_ge(s.rot_out, 1)
            link(nc.vector.tensor_tensor(m.sq4[:, 0, :], m.psum[:, 0, :], m.sin[:, :], ALU.mult))
            nc.vector.tensor_tensor(m.k_pe[:, :], m.k_pe[:, :], m.sq4[:, 0, :], ALU.add)
            dve.wait_ge(s.lat_high, 1)
            low_part(nc, m.lat_l[:, :, :], m.lat[:, 0:3, :], m.lat_h[:, :, :])

        @block.gpsimd
        def _(pool):
            ring.make_lows(pool, n)
        ring.first += n


def phase_heads(nc, m, ph, ring, d, following):
    with ExitStack() as ctx:
        block, s, stale = ph.open(ctx, "raw", "copied", "sq", "sums", "roots", "inv", "spread", "normed", "v", "rot",
                                  "rotated", "vraw", "vcopied", "here", *BESIDE_SEMS)
        W = on_chip(nc, ctx, "mod_weights", [P, 2, UNIT], F32)
        mod_units = d.ada_w[MOD_FIRST:MOD_FIRST + MOD_HEADS, :, :]
        dest = [m.qn[:, 0:4, :], m.qn[:, 4:8, :], m.qp[:, :, :], m.kn[:, 0:4, :], m.kn[:, 4:8, :]]
        gains = ["q_nope_g", "q_nope_g", "q_pe_g", "k_nope_g", "k_nope_g"]
        PE_BATCH = 2
        rows = m.root[0:NORM_ROWS[-1], :]
        pe_rows = on_chip(nc, ctx, "pe_rows", [NORM_ROWS[-1], 4 * P], F32)
        order = (PE_BATCH, 0, 1, 3, 4)

        @block.sync
        def _(sp):
            sp.sem_clear(stale)
            sp.dma_start(pe_rows[:, :], d.pe_rows).then_inc(s.here, 16)
            ring.stream(sp, d.mla_w_heads, 3, following)
            sp.wait_ge(s.here, 16)

        @block.gpsimd
        def _(pool):
            ring.make_lows(pool, 3)

        @block.tensor
        def _(pe):
            def raw(b):
                if b in (0, 2, 3):
                    unit[:] = ring.parts(pe, {0: 0, 2: 1, 3: 2}[b])
                if b >= 1:
                    pe.wait_ge(s.copied, b)
                for j in range(4):
                    if b <= PE_BATCH:
                        col = (j if b == PE_BATCH else 4 * b + j) * P
                        for k in range(2):
                            mm = split_matmul(nc, m.psum[:, j, :], [w[:, k * D + col:k * D + col + P] for w in unit],
                                              [x[:, k, :] for x in (m.lat_h, m.lat_l)], k == 0, k == 1)
                    else:
                        col = (4 * (b - 3) + j) * P
                        mm = split_matmul(nc, m.psum[:, j, :], [w[:, col:col + P] for w in unit],
                                          [x[:, 2, :] for x in (m.lat_h, m.lat_l)], True, True)
                mm.then_inc(s.raw, 1)

            def sums(b):
                pe.wait_ge(s.sq, b + 1)
                for j in range(4):
                    pick = m.const("pick_two" if b == PE_BATCH else "pick_one")
                    end = NORM_ROWS[-1]
                    row = NORM_ROWS[b] + (2 * j if b == PE_BATCH else j)
                    mm = nc.tensor.matmul(m.psum[0:end, 7, :], pick[:, end - 1 - row:2 * end - 1 - row],
                                          m.sq8[:, b % 2, j, :], start=(b == 0 and j == 0), stop=(b == 4 and j == 3))
                    if j == 0 and b in (0, 1):
                        mm.then_inc(ring.used, 1)
                mm.then_inc(s.sums, 1)

            def values(half):
                for t in range(TT):
                    mm = split_matmul(nc, m.psum[:, t, :], [x[:, 2, t * P:(t + 1) * P] for x in (m.lat_h, m.lat_l)],
                                      [w[:, D + half * 512:D + half * 512 + 512] for w in unit], True, True)
                mm.then_inc(s.vraw, 1)

            def spread(b, bank):
                for j in range(4):
                    row = NORM_ROWS[b] + j
                    if b == PE_BATCH:
                        sel = pe_rows[:, j * P:(j + 1) * P]
                    else:
                        sel = m.const("ident")[0:NORM_ROWS[-1], row:row + 1].broadcast_to([NORM_ROWS[-1], P])
                    mm = nc.tensor.matmul(m.psum[:, bank + j, :], sel, rows, start=True, stop=True)
                    if b == 0 and j == 0:
                        mm.then_inc(ring.used, 1)
                mm.then_inc(s.spread, 1)

            unit = [None, None]
            raw(0)
            for b in range(5):
                if b < 4:
                    raw(b + 1)
                sums(b)
            pe.wait_ge(s.copied, 5)
            values(0)
            pe.wait_ge(s.inv, 1)
            pe.wait_ge(s.here, 16)
            spread(PE_BATCH, 4)
            pe.wait_ge(s.vcopied, 1)
            values(1)
            pe.wait_ge(s.normed, 1)
            spread(0, 4)
            pe.wait_ge(s.vcopied, 2)
            spread(1, 0)
            pe.wait_ge(s.normed, 2)
            for j in range(4):
                mm = nc.tensor.matmul(m.psum[:, 4 + j, :], m.const("rot"), m.qp[:, j, :], start=True, stop=True)
            mm.then_inc(s.rot, 1)
            pe.wait_ge(s.normed, 3)
            spread(3, 0)
            pe.wait_ge(s.rotated, 4)
            spread(4, 4)

        @block.scalar
        def _(act):
            for k in range(2):
                load_beside(act, s, W, mod_units, k)
            for b in range(5):
                act.wait_ge(s.copied, b + 1)
                if b >= 2:
                    act.wait_ge(s.sums, b - 1)
                nc.scalar.activation(m.sq8[:, b % 2, :, :], dest[b], ACT.Square).then_inc(s.sq, 1)
                if 2 <= b + 1 < MOD_HEADS:
                    load_beside(act, s, W, mod_units, b + 1)
                if b in (1, 2):
                    ring.make_high(act, b + 1)
            act.wait_ge(s.sums, 5)
            nc.scalar.activation(rows, m.psum[0:NORM_ROWS[-1], 7, :], ACT.Sqrt,
                                 bias=m.const("eps")[0:NORM_ROWS[-1], :]).then_inc(s.roots, 1)
            for half in range(2):
                act.wait_ge(s.vraw, half + 1)
                nc.scalar.activation(m.vt[:, :, half * 512:half * 512 + 512], m.psum[:, 0:4, :],
                                     ACT.Copy).then_inc(s.vcopied, 1)
            ring.make_high(act, 4)

        @block.vector
        def _(dve):
            link = Link(dve, s.v)
            modulate_beside(nc, dve, m, s, W, 0, 2 * MOD_FIRST)
            for b in range(5):
                dve.wait_ge(s.raw, b + 1)
                nc.vector.tensor_copy(dest[b], m.psum[:, 0:4, :]).then_inc(s.copied, 1)
                if b + 1 < MOD_HEADS:
                    modulate_beside(nc, dve, m, s, W, b + 1, 2 * (MOD_FIRST + b + 1))
            dve.wait_ge(s.mod_read, MOD_HEADS)
            modulation_gains(nc, link, m, 0, 2 * KC, 3 * KC)
            dve.wait_ge(s.roots, 1)
            nc.vector.reciprocal(rows, rows).then_inc(s.inv, 1)
            dve.wait_ge(s.copied, 5)
            for n, b in enumerate(order):
                dve.wait_ge(s.spread, n + 1)
                bank = (4, 4, 0, 0, 4)[n]
                nc.vector.scalar_tensor_tensor(flat(dest[b]), flat(dest[b]), m.param(gains[b], 1),
                                               flat(m.psum[:, bank:bank + 4, :]), ALU.mult, ALU.mult).then_inc(s.normed, 1)
                if n == 2:
                    dve.wait_ge(s.normed, 1)
                    dve.wait_ge(s.rot, 1)
                    for j in range(4):
                        nc.vector.tensor_tensor(m.sq8[:, 0, j, :], m.psum[:, 4 + j, :], m.sin[:, :], ALU.mult)\
                            .then_inc(s.rotated, 1)
                        link(nc.vector.tensor_tensor(m.qp[:, j, :], m.qp[:, j, :], m.cos[:, :], ALU.mult))
                    dve.wait_ge(s.rotated, 4)
                    nc.vector.tensor_tensor(m.qp[:, :, :], m.qp[:, :, :], m.sq8[:, 0, :, :], ALU.add)
        ring.first += 3


def phase_attention(nc, m, ph, ring, d):
    scale = QK_HEAD ** -0.5
    steps = HEADS * TT
    with ExitStack() as ctx:
        block, s, stale = ph.open(ctx, "scores", "v", "neg", "exped", "rsum", "probs", "flipped", "pt_ready", "pv", "out_high", "out_low")
        E = on_chip(nc, ctx, "probs", [P, 3, S], F32)
        pt = on_chip(nc, ctx, "probs_t", [P, 2, TT, S], F32)
        top = on_chip(nc, ctx, "top", [P, steps], F32)
        neg = on_chip(nc, ctx, "neg", [P, steps], F32)
        tot = on_chip(nc, ctx, "tot", [P, steps], F32)
        inv = on_chip(nc, ctx, "inv", [P, steps], F32)

        @block.sync
        def _(sp):
            sp.sem_clear(stale)

        @block.tensor
        def _(pe):
            def scores(i):
                h, q = divmod(i, TT)
                if i >= 3:
                    pe.wait_ge(s.exped, i - 2)
                half = ROPE * (h % 2)
                nc.tensor.matmul(m.psum[:, i % 3, :], m.qn[:, h, q * P:(q + 1) * P], m.kn[:, h, :],
                                 start=True, stop=False)
                nc.tensor.matmul(m.psum[:, i % 3, :], m.qp[half:half + ROPE, h // 2, q * P:(q + 1) * P],
                                 m.k_pe[half:half + ROPE, :], start=False, stop=True).then_inc(s.scores, 1)

            def flip(i):
                pe.wait_ge(s.probs, i + 1)
                if i >= 2:
                    pe.wait_ge(s.pt_ready, i - 1)
                for kt in range(TT):
                    mm = nc.tensor.transpose(m.psum[:, 3 + i % 2, kt * P:(kt + 1) * P],
                                             E[:, i % 3, kt * P:(kt + 1) * P], m.const("ident"))
                mm.then_inc(s.flipped, 1)

            def values(h):
                pe.wait_ge(s.pt_ready, TT * (h + 1))
                if h >= 2:
                    pe.wait_ge(s.out_low, h - 1)
                for kt in range(TT):
                    mm = nc.tensor.matmul(m.psum[:, 5 + h % 2, :], m.vt[:, kt, h * P:(h + 1) * P],
                                          pt[:, h % 2, kt, :], start=(kt == 0), stop=(kt == TT - 1))
                mm.then_inc(s.pv, 1)

            for i in range(steps + 3):
                if i < steps:
                    scores(i)
                if 2 <= i < steps + 2:
                    flip(i - 2)
                if i >= 6 and (i - 6) % TT == 0:
                    values((i - 6) // TT)

        @block.vector
        def _(dve):
            link = Link(dve, s.v)

            def out(h):
                dve.wait_ge(s.out_high, h + 1)
                low_part(nc, m.Hl[:, h, :], m.psum[:, 5 + h % 2, :], m.Hh[:, h, :]).then_inc(s.out_low, 1)

            for i in range(steps + 2):
                if i < steps:
                    dve.wait_ge(s.scores, i + 1)
                    link(nc.vector.tensor_reduce(top[:, i:i + 1], m.psum[:, i % 3, :], AX.X, ALU.max))
                    nc.vector.tensor_scalar(neg[:, i:i + 1], top[:, i:i + 1], -scale, None, ALU.mult).then_inc(s.neg, 1)
                if 1 <= i <= steps:
                    dve.wait_ge(s.exped, i)
                    nc.vector.reciprocal(inv[:, i - 1:i], tot[:, i - 1:i]).then_inc(s.rsum, 1)
                if i >= 2:
                    j = i - 2
                    h, q = divmod(j, TT)
                    dve.wait_ge(s.flipped, j + 1)
                    if h >= 2:
                        dve.wait_ge(s.pv, h - 1)
                    nc.vector.tensor_copy(pt[:, h % 2, :, q * P:(q + 1) * P],
                                          m.psum[:, 3 + j % 2, :].rearrange("p (k n) -> p k n", k=TT)).then_inc(s.pt_ready, 1)
                if i >= 9 and (i - 9) % TT == 0:
                    out((i - 9) // TT)
            out(HEADS - 1)

        @block.scalar
        def _(act):
            def out(h):
                act.wait_ge(s.pv, h + 1)
                nc.scalar.activation(m.Hh[:, h, :], m.psum[:, 5 + h % 2, :], ACT.Copy).then_inc(s.out_high, 1)

            for i in range(steps + 1):
                if i < steps:
                    act.wait_ge(s.neg, i + 1)
                    if i >= 3:
                        act.wait_ge(s.flipped, i - 2)
                    nc.scalar.activation(E[:, i % 3, :], m.psum[:, i % 3, :], ACT.Exp, bias=neg[:, i:i + 1],
                                         scale=scale, accum_out=tot[:, i:i + 1]).then_inc(s.exped, 1)
                if i >= 1:
                    act.wait_ge(s.rsum, i)
                    nc.scalar.activation(E[:, (i - 1) % 3, :], E[:, (i - 1) % 3, :], ACT.Copy,
                                         scale=inv[:, i - 1:i]).then_inc(s.probs, 1)
                if i >= 8 and (i - 8) % TT == 0:
                    out((i - 8) // TT)
            out(HEADS - 1)


def phase_residual(nc, m, ph, ring, w, gate, following, z=None, mod_units=None):
    n = 4
    with ExitStack() as ctx:
        block, s, stale = ph.open(ctx, "read_out", "h_high", "h_ready", "v", *BESIDE_SEMS)
        if mod_units is not None:
            W = on_chip(nc, ctx, "mod_weights", [P, 2, UNIT], F32)

        @block.sync
        def _(sp):
            sp.sem_clear(stale)
            ring.stream(sp, w, n, following)

        @block.gpsimd
        def _(pool):
            ring.make_lows(pool, n, following is not None)

        @block.tensor
        def _(pe):
            streamed_products(nc, pe, ring, n, m.Hs, m.psum, s.read_out, k_ready=None if z is None else h_tiles(pe, s))

        @block.scalar
        def _(act):
            if z is not None:
                for c in range(KC):
                    nc.scalar.activation(m.Hh[:, c, :], z[:, c, :], ACT.Copy).then_inc(s.h_high, 1)
            if mod_units is not None:
                for k in range(2):
                    load_beside(act, s, W, mod_units, k)
            for u in range(n):
                if mod_units is not None:
                    for k in (2 * u + 2, 2 * u + 3):
                        load_beside(act, s, W, mod_units, k)
                ring.make_high(act, u + Ring.AHEAD)

        @block.vector
        def _(dve):
            def modulate(k):
                if mod_units is not None:
                    modulate_beside(nc, dve, m, s, W, k, MOD_TILES - 2 * MOD_REST + 2 * k)

            for k in range(2):
                modulate(k)
            if z is not None:
                for c in range(KC):
                    dve.wait_ge(s.h_high, c + 1)
                    low_part(nc, m.Hl[:, c, :], z[:, c, :], m.Hh[:, c, :]).then_inc(s.h_ready, 1)
            for u in range(n):
                ring.products(dve, u)
                for j in range(2):
                    t = 2 * u + j
                    x, y = m.X[:, t, :], m.psum[:, t, :]
                    if z is not None:
                        x = x.rearrange("p (n two) -> p two n", two=2)
                        y = y.rearrange("p (two n) -> p two n", two=2)
                    nc.vector.scalar_tensor_tensor(x, y, gate[:, t:t + 1], x, ALU.mult, ALU.add)
                for k in (2 * u + 2, 2 * u + 3):
                    modulate(k)
            if mod_units is not None:
                dve.wait_ge(s.mod_read, MOD_REST)
                modulation_gains(nc, Link(dve, s.v), m, 0, 3 * KC, MOD_TILES)
        ring.first += n


def phase_router(nc, m, ph, ring, layer, shift, gain):
    with ExitStack() as ctx:
        block, s, stale = ph.open(ctx, *NORM_SEMS, "logits", "v", "m1", "e1", "m2", "e2", "diag", "spread", "spread_read")
        L = on_chip(nc, ctx, "logits", [P, TT, GROUPS + EXPERTS], F32)
        G = on_chip(nc, ctx, "group", [P, 4, TT, GROUPS], F32)
        C = on_chip(nc, ctx, "column", [P, 6, TT], F32)
        EL = on_chip(nc, ctx, "chosen", [P, 4, TT, PER_GROUP], F32)
        T16 = on_chip(nc, ctx, "masked", [P, 2, TT, GROUPS, PER_GROUP], F32)
        dg = on_chip(nc, ctx, "diagonals", [P, 4, TT, P], F32)

        def wide(col, n=4):
            return col.unsqueeze(2).broadcast_to([P, TT, n])

        @block.sync
        def _(sp):
            sp.sem_clear(stale)

        @block.scalar
        def _(act):
            norm_act(nc, act, m, s, m.X, shift=shift)
            act.wait_ge(s.m1, 1)
            nc.scalar.activation(G[:, 1, :, :], G[:, 1, :, :], ACT.Exp).then_inc(s.e1, 1)
            act.wait_ge(s.m2, 1)
            nc.scalar.activation(EL[:, 1, :, :], EL[:, 1, :, :], ACT.Exp).then_inc(s.e2, 1)
            for e in range(EXPERTS):
                act.wait_ge(s.spread, e + 1)
                nc.scalar.activation(m.cb[:, e, :], m.psum[:, e % 4, :], ACT.Copy).then_inc(s.spread_read, 1)

        @block.tensor
        def _(pe):
            norm_pe(nc, pe, m, s)
            pe.wait_ge(s.h_ready, KC)
            for t in range(TT):
                for k in range(KC):
                    mm = split_matmul(nc, m.psum[:, 6, t * 20:(t + 1) * 20],
                                      [x[:, k, t * P:(t + 1) * P] for x in m.Hs],
                                      [x[:, layer, k, :] for x in (m.WRh, m.WRl)], k == 0, k == KC - 1)
            mm.then_inc(s.logits, 1)
            for e in range(EXPERTS):
                pe.wait_ge(s.diag, e + 1)
                if e >= 4:
                    pe.wait_ge(s.spread_read, e - 3)
                nc.tensor.matmul(m.psum[:, e % 4, :], m.const("ones"), dg[:, e % 4, :, :].rearrange("p t n -> p (t n)"),
                                 start=True, stop=True).then_inc(s.spread, 1)

        @block.vector
        def _(dve):
            link = Link(dve, s.v)
            tt, red = nc.vector.tensor_tensor, nc.vector.tensor_reduce
            norm_dve(nc, dve, m, s, link, m.X, gain)

            def first_of(out, values, largest, scratch):
                link(tt(scratch, values, wide(largest), ALU.is_equal))
                link(tt(scratch, scratch, m.priority[:, :, :], ALU.mult))
                link(red(C[:, 5, :], scratch, AX.X, ALU.max))
                link(tt(out, scratch, wide(C[:, 5, :]), ALU.is_equal))

            dve.wait_ge(s.logits, 1)
            link(tt(L[:, :, :], m.psum[:, 6, 0:80].rearrange("p (t n) -> p t n", t=TT),
                    m.RB[:, layer, :].unsqueeze(1).broadcast_to([P, TT, 20]), ALU.add))
            lg = L[:, :, 0:GROUPS]
            le = L[:, :, GROUPS:].rearrange("p t (g e) -> p t g e", g=GROUPS)
            link(red(C[:, 0, :], lg, AX.X, ALU.max))
            tt(G[:, 1, :, :], lg, wide(C[:, 0, :]), ALU.subtract).then_inc(s.m1, 1)
            dve.wait_ge(s.e1, 1)
            link(red(C[:, 1, :], G[:, 1, :, :], AX.X, ALU.add))
            link(nc.vector.reciprocal(C[:, 1, :], C[:, 1, :]))
            link(tt(G[:, 1, :, :], G[:, 1, :, :], wide(C[:, 1, :]), ALU.mult))
            link(red(C[:, 2, :], G[:, 1, :, :], AX.X, ALU.max))
            first_of(G[:, 2, :, :], G[:, 1, :, :], C[:, 2, :], G[:, 3, :, :])
            chosen_g = G[:, 2, :, :]
            for t in range(TT):
                link(tt(T16[:, 0, t, :, :], le[:, t, :, :], chosen_g[:, t, :].unsqueeze(2).broadcast_to([P, GROUPS, PER_GROUP]),
                        ALU.mult))
            for t in range(TT):
                link(red(EL[:, 0, t, :], T16[:, 0, t, :, :].rearrange("p g e -> p e g"), AX.X, ALU.add))
            link(red(C[:, 0, :], EL[:, 0, :, :], AX.X, ALU.max))
            tt(EL[:, 1, :, :], EL[:, 0, :, :], wide(C[:, 0, :]), ALU.subtract).then_inc(s.m2, 1)
            dve.wait_ge(s.e2, 1)
            link(red(C[:, 0, :], EL[:, 1, :, :], AX.X, ALU.add))
            link(nc.vector.reciprocal(C[:, 0, :], C[:, 0, :]))
            link(tt(EL[:, 1, :, :], EL[:, 1, :, :], wide(C[:, 0, :]), ALU.mult))
            link(red(C[:, 0, :], EL[:, 1, :, :], AX.X, ALU.max))
            first_of(EL[:, 2, :, :], EL[:, 1, :, :], C[:, 0, :], EL[:, 0, :, :])
            link(nc.vector.scalar_tensor_tensor(EL[:, 0, :, :], EL[:, 2, :, :], -2.0, EL[:, 1, :, :], ALU.mult, ALU.add))
            link(red(C[:, 1, :], EL[:, 0, :, :], AX.X, ALU.max))
            first_of(EL[:, 3, :, :], EL[:, 0, :, :], C[:, 1, :], EL[:, 1, :, :])
            link(tt(C[:, 3, :], C[:, 0, :], C[:, 1, :], ALU.add))
            link(nc.vector.reciprocal(C[:, 3, :], C[:, 3, :]))
            link(tt(C[:, 3, :], C[:, 3, :], C[:, 2, :], ALU.mult))
            link(tt(C[:, 0, :], C[:, 0, :], C[:, 3, :], ALU.mult))
            link(tt(C[:, 1, :], C[:, 1, :], C[:, 3, :], ALU.mult))
            link(tt(EL[:, 2, :, :], EL[:, 2, :, :], wide(C[:, 0, :]), ALU.mult))
            link(tt(EL[:, 3, :, :], EL[:, 3, :, :], wide(C[:, 1, :]), ALU.mult))
            link(tt(EL[:, 2, :, :], EL[:, 2, :, :], EL[:, 3, :, :], ALU.add))
            for t in range(TT):
                link(tt(T16[:, 1, t, :, :], chosen_g[:, t, :].unsqueeze(2).broadcast_to([P, GROUPS, PER_GROUP]),
                        EL[:, 2, t, :].unsqueeze(1).broadcast_to([P, GROUPS, PER_GROUP]), ALU.mult))
            for e in range(EXPERTS):
                if e >= 4:
                    dve.wait_ge(s.spread, e - 3)
                w = T16[:, 1, :, e // PER_GROUP, e % PER_GROUP]
                tt(dg[:, e % 4, :, :], m.const("ident").unsqueeze(1).broadcast_to([P, TT, P]), wide(w, P), ALU.mult)\
                    .then_inc(s.diag, 1)


def phase_experts(nc, m, ph, ring, w, gate, following, modulation=None):
    per = 3 * PER_GROUP
    extra = MOD_UNITS // GROUPS
    with ExitStack() as ctx:
        block, s, stale = ph.open(ctx, "gates_out", "ups_out", "weighted", "a_high", "a_ready", "downs_out", "v",
                                  "mod_read", "mod_kept", "mod_loaded_0", "mod_loaded_1")
        T = on_chip(nc, ctx, "silu", [P, 2, 2, S], F32)
        Ah = on_chip(nc, ctx, "acts_high", [P, 2 * PER_GROUP, S], F32R)
        Al = on_chip(nc, ctx, "acts_low", [P, 2 * PER_GROUP, S], F32R)
        if modulation is not None:
            W = on_chip(nc, ctx, "mod_weights", [P, 2, UNIT], F32)
            sums = on_chip(nc, ctx, "mod_sums", [P, 2 * extra], F32)
            mod_loaded = (s.mod_loaded_0, s.mod_loaded_1)

        @block.sync
        def _(sp):
            sp.sem_clear(stale)
            ring.stream(sp, w, per * GROUPS, following)

        @block.gpsimd
        def _(pool):
            ring.make_lows(pool, per * GROUPS, following is not None)

        @block.tensor
        def _(pe):
            pe.sem_inc(s.downs_out, 4)
            with pe.Fori(0, GROUPS) as g:
                for u in range(per):
                    if u < 4:
                        pe.wait_ge(s.downs_out, g * 4 + (u + 1))
                    elif u % 2 == 0:
                        pe.wait_ge(s.gates_out, g * 4 + (u // 2 - 1))
                    else:
                        pe.wait_ge(s.ups_out, g * 4 + (u // 2 - 1))
                    unit_products(nc, pe, ring, u, m.Hs if u < 8 else (Ah, Al), m.psum, turn=g, per=per,
                                  k_ready=(lambda k: pe.wait_ge(s.a_ready, g * 4 + (k // 2 + 1))) if u == 8 else None)

        @block.scalar
        def _(act):
            if modulation is not None:
                act.sem_inc(s.mod_read, 2)
            with act.Fori(0, GROUPS) as g:
                def load_modulation(k):
                    if modulation is None:
                        return
                    act.wait_ge(s.mod_read, g * extra + (k + 1))
                    act.dma_start(W[:, k % 2, :], modulation[bass.ds(g * extra + k, 1), :, :].rearrange("a p n -> (a p) n")
                                  ).then_inc(mod_loaded[k % 2], 16)

                for j in range(PER_GROUP):
                    load_modulation(j)
                    ring.products(act, 2 * j, g, per)
                    if j >= 2:
                        act.wait_ge(s.a_ready, g * 4 + (j - 1))
                    b = 4 * j % BANKS
                    nc.scalar.activation(T[:, j % 2, :, :], m.psum[:, b:b + 2, :], ACT.Silu).then_inc(s.gates_out, 1)
                    ring.make_high(act, 2 * j + 2, g, per)
                    act.wait_ge(s.weighted, g * 4 + (j + 1))
                    nc.scalar.activation(Ah[:, 2 * j:2 * j + 2, :], T[:, j % 2, :, :], ACT.Copy).then_inc(s.a_high, 1)
                    ring.make_high(act, 2 * j + 3, g, per)
                for u in range(8, per):
                    ring.make_high(act, u + 2, g, per)
                    if u in (8, 10):
                        load_modulation(u // 2)

        @block.vector
        def _(dve):
            if modulation is not None:
                dve.sem_inc(s.mod_kept, 1)
            with dve.Fori(0, GROUPS) as g:
                def modulate(k):
                    if modulation is None:
                        return
                    dve.wait_ge(mod_loaded[k % 2], g * (8 * extra) + 16 * (k // 2 + 1))
                    if k == 0:
                        dve.wait_ge(s.mod_kept, g + 1)
                    modulation_unit(nc, m, W[:, k % 2, :], sums, 2 * k).then_inc(s.mod_read, 1)

                for j in range(PER_GROUP):
                    ring.products(dve, 2 * j + 1, g, per)
                    dve.wait_ge(s.gates_out, g * 4 + (j + 1))
                    b = (4 * j + 2) % BANKS
                    t = T[:, j % 2, :, :]
                    mm = nc.vector.tensor_tensor(t, t, m.psum[:, b:b + 2, :], ALU.mult)
                    mm.then_inc(s.ups_out, 1)
                    dve.wait_ge(s.ups_out, g * 4 + (j + 1))
                    nc.vector.tensor_tensor(t, t, m.cb[:, bass.ds(g * PER_GROUP + j, 1), :].broadcast_to([P, 2, S]),
                                            ALU.mult).then_inc(s.weighted, 1)
                    dve.wait_ge(s.a_high, g * 4 + (j + 1))
                    low_part(nc, Al[:, 2 * j:2 * j + 2, :], t, Ah[:, 2 * j:2 * j + 2, :]).then_inc(s.a_ready, 1)
                    if j < 3:
                        modulate(j)
                for u in range(4):
                    ring.products(dve, 8 + u, g, per)
                    for j in range(2):
                        t = 2 * u + j
                        last = nc.vector.scalar_tensor_tensor(m.X[:, t, :], m.psum[:, t, :], gate[:, t:t + 1],
                                                              m.X[:, t, :], ALU.mult, ALU.add)
                    last.then_inc(s.downs_out, 1)
                    if u < 3:
                        modulate(3 + u)
                if modulation is not None:
                    dve.wait_ge(s.mod_read, g * extra + (extra + 2))
                    nc.vector.tensor_copy(m.mod[:, bass.ds(g * (2 * extra) + MOD_TILES, 2 * extra)],
                                          sums[:, :]).then_inc(s.mod_kept, 1)
            if modulation is not None:
                dve.wait_ge(s.mod_kept, GROUPS + 1)
                modulation_gains(nc, Link(dve, s.v, 0), m, 1)
        ring.first += per * GROUPS


def phase_hyena_in(nc, m, ph, ring, d, following):
    n = 12
    with ExitStack() as ctx:
        block, s, stale = ph.open(ctx, *NORM_SEMS, "v", "read_out", "padded", "conv", "pads")
        U = on_chip(nc, ctx, "padded", [P, 2, 2, S + 2], F32)
        W = on_chip(nc, ctx, "conv", [P, 2, S], F32)

        @block.sync
        def _(sp):
            sp.sem_clear(stale)
            ring.stream(sp, d.hy_w_in, n, following)

        @block.gpsimd
        def _(pool):
            nc.gpsimd.memset(U[:, :, :, :], 0.0).then_inc(s.pads, 1)
            ring.make_lows(pool, n)

        @block.tensor
        def _(pe):
            norm_pe(nc, pe, m, s)
            pe.wait_ge(s.root, 1)
            streamed_products(nc, pe, ring, n, m.Hs, m.psum, s.read_out, k_ready=h_tiles(pe, s))

        @block.scalar
        def _(act):
            norm_act(nc, act, m, s, m.X, shift=m.mod[:, 48:48 + KC])
            act.wait_ge(s.pads, 1)
            act.sem_inc(s.conv, 4)

            def body(u, turn):
                ring.products(act, u, turn)
                act.wait_ge(s.conv, turn * 8 + (2 * u + 2))
                for j in range(2):
                    b = (2 * u + j) % BANKS
                    last = nc.scalar.activation(
                        U[:, u % 2, j, 1:S + 1], m.psum[:, b, :], ACT.Identity,
                        bias=m.PT[:, bass.ds(turn * 8 + (PCOL["hy_b_in"] + 2 * u + j), 1)])
                last.then_inc(s.read_out, 1)
                ring.make_high(act, u + Ring.AHEAD, turn)
            over_units(act, n, body)

        @block.vector
        def _(dve):
            link = Link(dve, s.v)
            norm_dve(nc, dve, m, s, link, m.X, m.gain[:, 1, 0, :])
            base = link.n

            def col(name, k):
                return m.PT[:, bass.ds(k + PCOL[name], 1)]

            def body(u, turn):
                dve.wait_ge(s.read_out, turn * TURN + (u + 1))
                chain = Link(dve, s.v, turn * 16 + (base + 4 * u))
                for j in range(2):
                    t = turn * 8 + (2 * u + j)
                    src = U[:, u % 2, j, :]
                    chain(nc.vector.tensor_scalar(W[:, j, :], src[:, 1:S + 1], col("hy_conv_w", t + 24),
                                                  col("hy_conv_b", t), ALU.mult, ALU.add))
                    chain(nc.vector.scalar_tensor_tensor(W[:, j, :], src[:, 0:S], col("hy_conv_w", t), W[:, j, :],
                                                         ALU.mult, ALU.add))
                    out = m.xv[:, bass.ds(t, 1), :].rearrange("p a (two n) -> p n (a two)", two=2)
                    nc.vector.scalar_tensor_tensor(
                        out, src[:, 2:S + 2].rearrange("p (n two) -> p n two", two=2), col("hy_conv_w", t + 48),
                        W[:, j, :].rearrange("p (n two) -> p n two", two=2), ALU.mult, ALU.add).then_inc(s.conv, 1)
            over_units(dve, n, body)
        ring.first += n


def phase_filter_mlp(nc, m, ph, ring, d):
    with ExitStack() as ctx:
        block, s, stale = ph.open(ctx, "here", "tables", "v", "sum", "arg", "sine")
        zT = on_chip(nc, ctx, "zT", [FILTER_EMB, S], F32)
        w1 = on_chip(nc, ctx, "w1", [FILTER_EMB, FILTER_WIDTH], F32)
        w23 = on_chip(nc, ctx, "w23", [FILTER_WIDTH, 2, FILTER_WIDTH], F32)
        a = on_chip(nc, ctx, "arg", [FILTER_WIDTH, S], F32)
        k = on_chip(nc, ctx, "whole", [FILTER_WIDTH, S], F32)

        @block.sync
        def _(sp):
            sp.sem_clear(stale)
            for dst, src in ((zT[:, :], d.zT), (w1[:, :], d.hy_f_w1), (w23[:, 0, :], d.hy_f_w2), (w23[:, 1, :], d.hy_f_w3)):
                sp.dma_start(dst, src).then_inc(s.here, 16)
            sp.dma_start(m.fwd[:, :, :, :], d.dft_fwd).then_inc(s.tables, 16)
            sp.dma_start(m.inv[:, :, :, :], d.dft_inv).then_inc(s.tables, 16)
            sp.wait_ge(s.tables, 32)

        @block.tensor
        def _(pe):
            pe.wait_ge(s.here, 64)
            for n in range(3):
                if n:
                    pe.wait_ge(s.sine, n)
                nc.tensor.matmul(m.psum[0:FILTER_WIDTH, 0, :], w1[:, :] if n == 0 else w23[:, n - 1, :],
                                 zT[:, :] if n == 0 else m.hdn[:, :], start=True, stop=True).then_inc(s.sum, 1)

        @block.vector
        def _(dve):
            link = Link(dve, s.v)
            for n in range(3):
                dve.wait_ge(s.sum, n + 1)
                link(nc.vector.tensor_scalar(a[:, :], m.psum[0:FILTER_WIDTH, 0, :], m.param("hy_fb", 1, n)[0:FILTER_WIDTH, :],
                                             m.param("hy_ff", 1, n)[0:FILTER_WIDTH, :], ALU.add, ALU.mult))
                link(nc.vector.tensor_scalar(k[:, :], a[:, :], 1.0 / (2 * math.pi), ROUND_MAGIC, ALU.mult, ALU.add))
                link(nc.vector.tensor_scalar(k[:, :], k[:, :], ROUND_MAGIC, None, ALU.subtract))
                for part in (TWO_PI_A, TWO_PI_B, TWO_PI_C):
                    link(nc.vector.scalar_tensor_tensor(a[:, :], k[:, :], -part, a[:, :], ALU.mult, ALU.add))
                nc.vector.tensor_scalar(a[:, :], a[:, :], PI_DOWN, -PI_DOWN, ALU.min, ALU.max).then_inc(s.arg, 1)

        @block.scalar
        def _(act):
            for n in range(3):
                act.wait_ge(s.arg, n + 1)
                nc.scalar.activation(m.hdn[:, :], a[:, :], ACT.Sin).then_inc(s.sine, 1)


def phase_long_conv(nc, m, ph, ring, d, order, half):
    with ExitStack() as ctx:
        block, s, stale = ph.open(ctx, "here", "w4", "raw", "decayed", "absed", "added", "norms", "norms_out", "v", "ab",
                                  "z_flip", "z_out", "k_sums", "k_odd", "k_done", "u_sums", "u_odd", "u_done",
                                  "pairs", "inverse")
        F = on_chip(nc, ctx, "filters_then_u", [P, 2, TT, 512], F32)
        A = on_chip(nc, ctx, "ab_then_y", [P, 2, TT, 512], F32)
        K = on_chip(nc, ctx, "k_spectrum", [P, 2, TT, 512], F32)
        O = on_chip(nc, ctx, "decay_then_odd", [P, TT, 512], F32)
        w4, rn, added = K[0:FILTER_WIDTH, 0, 0:2, :], K[:, 1, 0:2, :], K[:, 1, 2:4, :]
        vt = on_chip(nc, ctx, "z_token_major", [P, TT, 512], F32)
        cols = slice(half * 512, half * 512 + 512)

        @block.sync
        def _(sp):
            sp.sem_clear(stale)
            sp.dma_start(w4, d.hy_f_w4[:, order, :, cols]).then_inc(s.w4, 16)
            sp.dma_start(O[:, :, :], d.decay[:, :, cols]).then_inc(s.here, 16)
            sp.wait_ge(s.here, 16)

        def transform(src_cos, src_sin, done):
            for which, src in ((0, src_cos), (1, src_sin)):
                for parity in range(2):
                    for kt in range(2):
                        for c in range(2):
                            j = 2 * parity + c
                            mm = nc.tensor.matmul(m.psum[:, 4 * parity + 2 * which + kt, :],
                                                  m.fwd[:, which, j, kt * P:(kt + 1) * P], src[:, j, :],
                                                  start=(c == 0), stop=(c == 1))
                mm.then_inc(done, 1)

        @block.tensor
        def _(pe):
            pe.wait_ge(s.w4, 16)
            for x in range(2):
                for j in range(TT):
                    mm = nc.tensor.matmul(m.psum[:, 4 * x + j, :], m.hdn[:, j * P:(j + 1) * P], w4[:, x, :],
                                          start=True, stop=True)
                mm.then_inc(s.raw, 1)
            pe.wait_ge(s.decayed, 1)
            for j in range(TT):
                for c in range(4):
                    mm = nc.tensor.transpose(m.psum[:, j, c * P:(c + 1) * P],
                                             m.xv[:, 16 + 4 * half + c, j * P:(j + 1) * P], m.const("ident"))
            mm.then_inc(s.z_flip, 1)
            for x in range(2):
                pe.wait_ge(s.added, x + 1)
                nc.tensor.matmul(m.psum[:, 4 + x, :], m.const("ones"), added[:, x, :],
                                 start=True, stop=True).then_inc(s.norms, 1)
            pe.wait_ge(s.z_out, 1)
            pe.wait_ge(s.norms_out, 1)
            transform(vt, vt, s.u_sums)
            pe.wait_ge(s.ab, 1)
            pe.wait_ge(s.u_done, 2)
            transform(A[:, 0, :, :], A[:, 1, :, :], s.k_sums)
            for parity in range(2):
                pe.wait_ge(s.pairs, parity + 1)
                for c in range(4):
                    for n in range(4):
                        mm = nc.tensor.matmul(m.psum[:, c, parity * 256:(parity + 1) * 256],
                                              F[:, parity, n, c * P:(c + 1) * P], m.inv[:, parity, n, :],
                                              start=(n == 0), stop=(n == 3))
                    if parity:
                        mm.then_inc(s.inverse, 1)

        @block.scalar
        def _(act):
            for x in range(2):
                act.wait_ge(s.decayed, x + 1)
                nc.scalar.activation(A[:, x, :, :], F[:, x, :, :], ACT.Abs).then_inc(s.absed, 1)
            act.wait_ge(s.z_flip, 1)
            nc.scalar.activation(vt[:, :, :], m.psum[:, 0:4, :], ACT.Copy).then_inc(s.z_out, 1)
            for w in range(2):
                act.wait_ge(s.u_sums, w + 1)
                nc.scalar.activation(O[:, 2 * w:2 * w + 2, :], m.psum[:, 4 + 2 * w:6 + 2 * w, :], ACT.Copy)\
                    .then_inc(s.u_odd, 1)
            for w in range(2):
                act.wait_ge(s.k_sums, w + 1)
                nc.scalar.activation(O[:, 2 * w:2 * w + 2, :], m.psum[:, 4 + 2 * w:6 + 2 * w, :], ACT.Copy)\
                    .then_inc(s.k_odd, 1)

        @block.vector
        def _(dve):
            link = Link(dve, s.v)
            tt = nc.vector.tensor_tensor

            def butterflies(out, which, done):
                at = 2 * which
                even, odd = m.psum[:, at:at + 2, :], O[:, at:at + 2, :]
                tt(out[:, which, 0:2, :], even, odd, ALU.add)
                mirror = (odd, even) if which else (even, odd)
                return tt(out[:, which, 2:4, :], mirror[0], mirror[1], ALU.subtract).then_inc(done, 1)

            dve.wait_ge(s.here, 16)
            for x in range(2):
                dve.wait_ge(s.raw, x + 1)
                tt(F[:, x, :, :], m.psum[:, 4 * x:4 * x + 4, :], O[:, :, :], ALU.mult).then_inc(s.decayed, 1)
            for x in range(2):
                dve.wait_ge(s.absed, x + 1)
                link(tt(A[:, x, 0:2, :], A[:, x, 0:2, :], A[:, x, 2:4, :], ALU.add))
                tt(added[:, x, :], A[:, x, 0, :], A[:, x, 1, :], ALU.add).then_inc(s.added, 1)
            dve.wait_ge(s.norms, 2)
            nc.vector.tensor_scalar(rn, m.psum[:, 4:6, :], EPS, None, ALU.add).then_inc(s.norms_out, 1)
            dve.wait_ge(s.norms_out, 1)
            link(nc.vector.reciprocal(rn, rn))
            for x in range(2):
                link(tt(F[:, x, :, :], F[:, x, :, :], rn[:, x, :].unsqueeze(1).broadcast_to([P, TT, 512]), ALU.mult))
            link(nc.vector.memset(F[0:1, 1, 0, :], 0.0))
            tt(A[:, 0, :, :], F[:, 0, :, :], F[:, 1, :, :], ALU.add)
            tt(A[:, 1, :, :], F[:, 0, :, :], F[:, 1, :, :], ALU.subtract).then_inc(s.ab, 1)
            dve.wait_ge(s.ab, 1)
            for w in range(2):
                dve.wait_ge(s.u_odd, w + 1)
                butterflies(F, w, s.u_done)
            for w in range(2):
                dve.wait_ge(s.k_odd, w + 1)
                butterflies(K, w, s.k_done)
            dve.wait_ge(s.k_done, 2)
            link(tt(A[:, 0, :, :], F[:, 0, :, :], K[:, 0, :, :], ALU.mult))
            link(tt(O[:, :, :], F[:, 1, :, :], K[:, 1, :, :], ALU.mult))
            link(tt(A[:, 0, :, :], A[:, 0, :, :], O[:, :, :], ALU.subtract))
            link(tt(A[:, 1, :, :], F[:, 0, :, :], K[:, 1, :, :], ALU.mult))
            link(tt(O[:, :, :], F[:, 1, :, :], K[:, 0, :, :], ALU.mult))
            link(tt(A[:, 1, :, :], A[:, 1, :, :], O[:, :, :], ALU.add))
            tt(F[:, 0, 0:2, :], A[:, 0, 0:2, :], A[:, 0, 2:4, :], ALU.add)
            tt(F[:, 0, 2:4, :], A[:, 1, 0:2, :], A[:, 1, 2:4, :], ALU.subtract).then_inc(s.pairs, 1)
            tt(F[:, 1, 0:2, :], A[:, 0, 0:2, :], A[:, 0, 2:4, :], ALU.subtract)
            tt(F[:, 1, 2:4, :], A[:, 1, 0:2, :], A[:, 1, 2:4, :], ALU.add).then_inc(s.pairs, 1)
            for c in range(4):
                t = 4 * half + c
                dve.wait_ge(s.inverse, c + 1)
                link(nc.vector.scalar_tensor_tensor(O[:, c, :], m.xv[:, 16 + t, :], m.param("hy_filt_bias", 1, 8 * order + t),
                                                    m.psum[:, c, :], ALU.mult, ALU.add))
                tt(m.xv[:, 16 + t, :], O[:, c, :], m.xv[:, 8 * order + t, :], ALU.mult)


def phase_project(nc, m, ph, ring, d, layer, following):
    n = 16
    with ExitStack() as ctx:
        block, s, stale = ph.open(ctx, *NORM_SEMS, "v", "read_out")
        m.F = on_chip(nc, ctx, "norm_tiles", [P, 4, S], F32)

        @block.sync
        def _(sp):
            sp.sem_clear(stale)
            ring.stream(sp, d.w_proj[layer], n, following)

        @block.gpsimd
        def _(pool):
            ring.make_lows(pool, n)

        @block.tensor
        def _(pe):
            norm_pe(nc, pe, m, s)
            pe.wait_ge(s.root, 1)
            streamed_products(nc, pe, ring, 14, m.Hs, m.psum, s.read_out, k_ready=h_tiles(pe, s))
            for u in (14, 15):
                w = [x.rearrange("p (k m) -> p k m", k=KC) for x in ring.parts(pe, u)]
                pe.wait_ge(s.read_out, 14)
                for t in range(TT):
                    for k in range(KC):
                        mm = split_matmul(nc, m.psum[:, 4 * (u - 14) + t, 0:256], [x[:, k, t * P:(t + 1) * P] for x in m.Hs],
                                          [x[:, k, :] for x in w], k == 0, k == KC - 1)
                mm.then_inc(ring.used, 1)

        @block.scalar
        def _(act):
            norm_act(nc, act, m, s, m.X)
            for u in range(14):
                ring.products(act, u)
                func = ACT.Silu if u in (2, 3) else ACT.Sigmoid if u >= 12 else ACT.Copy
                b = 2 * u % BANKS
                nc.scalar.activation(m.raw[:, 2 * u:2 * u + 2, :], m.psum[:, b:b + 2, :], func).then_inc(s.read_out, 1)
                ring.make_high(act, u + 2)
            for u in (14, 15):
                ring.products(act, u)
                nc.scalar.activation(m.vr[:, :, 256 * (u - 14):256 * (u - 13)],
                                     m.psum[:, 4 * (u - 14):4 * (u - 14) + 4, 0:256], ACT.Copy)
                ring.make_high(act, u + 2)

        @block.vector
        def _(dve):
            link = Link(dve, s.v)
            norm_dve(nc, dve, m, s, link, m.X, m.param("mix_pre", KC, layer * KC))
        ring.first += n


RAW_Q, RAW_K, RAW_G, RAW_SB, RAW_SC, RAW_SX, RAW_CA, RAW_CB = 0, 2, 4, 8, 12, 16, 20, 24


def phase_retention(nc, m, ph, ring, d):
    with ExitStack() as ctx:
        block, s, stale = ph.open(ctx, "here", "rot", "qk", "v", "scores", "decayed", "outs", "copied", "means", "centred",
                                  "squares", "variances", "root")
        dec = on_chip(nc, ctx, "ret_decay", [P, RET_HEADS, S], F32)
        ST = on_chip(nc, ctx, "scores", [P, 2, TT, S], F32)
        OR = on_chip(nc, ctx, "head_out", [P, RET_HEADS, S], F32)
        tab = OR[:, 0:2, :]
        qk = m.raw[:, RAW_Q:RAW_K + 2, :]

        @block.sync
        def _(sp):
            sp.sem_clear(stale)
            sp.dma_start(dec[:, :, :], d.ret_decay).then_inc(s.here, 16)
            sp.dma_start(tab[:, :, :], d.ret_rotary).then_inc(s.here, 16)
            sp.wait_ge(s.here, 32)

        @block.tensor
        def _(pe):
            for j in range(4):
                mm = nc.tensor.matmul(m.psum[:, j, :], m.const("rot"), qk[:, j, :], start=True, stop=True)
            mm.then_inc(s.rot, 1)
            pe.wait_ge(s.qk, 1)
            for h in range(RET_HEADS):
                rows, t = slice(64 * (h % 2), 64 * (h % 2) + 64), h // 2
                if h:
                    pe.wait_ge(s.decayed, TT * h)
                for i in range(TT):
                    nc.tensor.matmul(m.psum[:, 4 + i, 0:S - i * P], m.raw[rows, RAW_K + t, i * P:(i + 1) * P],
                                     m.raw[rows, RAW_Q + t, i * P:S], start=True, stop=True).then_inc(s.scores, 1)
                for i in range(TT):
                    pe.wait_ge(s.decayed, TT * h + i + 1)
                    mm = nc.tensor.matmul(m.psum[:, h, i * P:S], m.vr[:, i, h * P:(h + 1) * P],
                                          ST[:, h % 2, i, 0:S - i * P], start=(i == 0), stop=(i == TT - 1))
                mm.then_inc(s.outs, 1)
            pe.wait_ge(s.copied, RET_HEADS)
            for h in range(RET_HEADS):
                mm = nc.tensor.matmul(m.psum[:, h, :], m.const("ones"), OR[:, h, :], start=True, stop=True)
            mm.then_inc(s.means, 1)
            pe.wait_ge(s.squares, 1)
            for h in range(RET_HEADS):
                mm = nc.tensor.matmul(m.psum[:, 4 + h, :], m.const("ones"), ST[:, 0, h, :], start=True, stop=True)
            mm.then_inc(s.variances, 1)

        @block.vector
        def _(dve):
            link = Link(dve, s.v)
            tt = nc.vector.tensor_tensor
            wide = lambda x: x.unsqueeze(1).broadcast_to([P, 4, S])
            dve.wait_ge(s.here, 32)
            dve.wait_ge(s.rot, 1)
            tt(ST[:, 0, :, :], m.psum[:, 0:4, :], wide(tab[:, 1, :]), ALU.mult)
            link(tt(qk, qk, wide(tab[:, 0, :]), ALU.mult))
            tt(qk, qk, ST[:, 0, :, :], ALU.add).then_inc(s.qk, 1)
            dve.wait_ge(s.qk, 1)
            for h in range(RET_HEADS):
                for i in range(TT):
                    dve.wait_ge(s.scores, TT * h + i + 1)
                    if h >= 2 and i == 0:
                        dve.wait_ge(s.outs, h - 1)
                    tt(ST[:, h % 2, i, 0:S - i * P], m.psum[:, 4 + i, 0:S - i * P], dec[:, h, 0:S - i * P], ALU.mult)\
                        .then_inc(s.decayed, 1)
            dve.wait_ge(s.means, 1)
            nc.vector.scalar_tensor_tensor(flat(OR[:, :, :]), flat(m.psum[:, 0:4, :]), -1.0 / RET_V, flat(OR[:, :, :]),
                                           ALU.mult, ALU.add).then_inc(s.centred, 1)
            dve.wait_ge(s.root, 1)
            link(nc.vector.reciprocal(ST[:, 1, :, :], ST[:, 1, :, :]))
            link(tt(OR[:, :, :], OR[:, :, :], ST[:, 1, :, :], ALU.mult))
            tt(m.raw[:, RAW_G:RAW_G + 4, :], m.raw[:, RAW_G:RAW_G + 4, :], OR[:, :, :], ALU.mult)

        @block.scalar
        def _(act):
            for h in range(RET_HEADS):
                act.wait_ge(s.outs, h + 1)
                nc.scalar.activation(OR[:, h, :], m.psum[:, h, :], ACT.Copy).then_inc(s.copied, 1)
            act.wait_ge(s.centred, 1)
            nc.scalar.activation(ST[:, 0, :, :], OR[:, :, :], ACT.Square).then_inc(s.squares, 1)
            act.wait_ge(s.variances, 1)
            nc.scalar.activation(ST[:, 1, :, :], m.psum[:, 4:8, :], ACT.Sqrt, bias=m.const("eps"),
                                 scale=1.0 / RET_V).then_inc(s.root, 1)


def flat(x):
    return x.rearrange("p t n -> p (t n)")


def phase_branches(nc, m, ph, ring, d, layer, following):
    steps = 6
    n = 3 * steps
    with ExitStack() as ctx:
        block, s, stale = ph.open(ctx, "pads", "glu", "v", "sigmoids", "merged", "b_value", "b_high", "b_ready",
                                  "conv", "means", "centred", "squares", "variances", "root", "scaled")
        GP = on_chip(nc, ctx, "long_in", [P, 4, S + CF_K - 1], F32)
        Bh = on_chip(nc, ctx, "branch_high", [P, 4, S], F32R)
        Bl = on_chip(nc, ctx, "branch_low", [P, 4, S], F32R)
        sg, sb, sc, sx, ca, cb = (m.raw[:, k:k + 4, :] for k in (RAW_G, RAW_SB, RAW_SC, RAW_SX, RAW_CA, RAW_CB))
        gate = cb
        branch = (sg, sb, ca)
        c_sw, c_cw = PCOL["sc_w"] + layer * SC_K * 4, PCOL["cf_w"] + layer * CF_K * 4
        chunk = (CF_K - 1) // 3

        @block.sync
        def _(sp):
            sp.sem_clear(stale)
            ring.stream(sp, d.w_branches[layer], n, following)

        @block.gpsimd
        def _(pool):
            nc.gpsimd.memset(GP[:, :, 0:CF_K - 1], 0.0).then_inc(s.pads, 1)
            ring.make_lows(pool, n)

        @block.tensor
        def _(pe):
            for i in range(steps):
                for j in range(2):
                    if i:
                        pe.wait_ge(s.sigmoids, 2 * (i - 1) + j + 1)
                    unit_products(nc, pe, ring, 3 * i + j, m.Hs, m.psum, banks=(2 * j, 2 * j + 1))
                    if i == 4 and j == 0:
                        pe.wait_ge(s.squares, 1)
                        for c in range(4):
                            mm = nc.tensor.matmul(m.psum[:, 5, :], m.const("ones"), sc[:, c, :], start=(c == 0), stop=(c == 3))
                        mm.then_inc(s.variances, 1)
                if i % 2 == 0:
                    pe.wait_ge(s.b_ready, i // 2 + 1)
                if i:
                    pe.wait_ge(s.merged, i)
                if i == 4:
                    pe.wait_ge(s.root, 1)
                unit_products(nc, pe, ring, 3 * i + 2, (Bh, Bl), m.psum, kc=4, tiles=4, banks=(4, 5, 6, 7))
                if i == 3:
                    pe.wait_ge(s.conv, 1)
                    pe.wait_ge(s.merged, 4)
                    for c in range(4):
                        mm = nc.tensor.matmul(m.psum[:, 4, :], m.const("ones"), ca[:, c, :], start=(c == 0), stop=(c == 3))
                    mm.then_inc(s.means, 1)

        @block.scalar
        def _(act):
            def high(b):
                act.wait_ge(s.b_value, b + 1)
                if b:
                    ring.products(act, 6 * b - 1)
                nc.scalar.activation(Bh[:, :, :], branch[b], ACT.Copy).then_inc(s.b_high, 1)

            high(0)
            act.wait_ge(s.glu, 1)
            for i in range(steps):
                for j in range(2):
                    u = 3 * i + j
                    ring.products(act, u)
                    if i and j == 0:
                        act.wait_ge(s.merged, i)
                    nc.scalar.activation(gate[:, 2 * j:2 * j + 2, :], m.psum[:, 2 * j:2 * j + 2, :], ACT.Sigmoid)\
                        .then_inc(s.sigmoids, 1)
                    ring.make_high(act, u + 2)
                    if i == 4 and j == 0:
                        act.wait_ge(s.variances, 1)
                        nc.scalar.activation(m.root[:, :], m.psum[:, 5, :], ACT.Sqrt, bias=m.const("eps"), scale=1.0 / MIX)\
                            .then_inc(s.root, 1)
                        act.wait_ge(s.scaled, 1)
                        for c in range(4):
                            nc.scalar.activation(ca[:, c, :], ca[:, c, :], ACT.Silu, scale=m.param("cf_g", 1, 4 * layer + c),
                                                 bias=m.param("cf_lb", 1, 4 * layer + c)).then_inc(s.b_value, 1)
                        act.wait_ge(s.b_value, 6)
                        ring.products(act, 11)
                        nc.scalar.activation(Bh[:, :, :], ca, ACT.Copy).then_inc(s.b_high, 1)
                if i == 1:
                    ring.products(act, 5)
                    high(1)
                if i == 3:
                    act.wait_ge(s.centred, 1)
                    nc.scalar.activation(sc, ca, ACT.Square).then_inc(s.squares, 1)
                ring.make_high(act, 3 * i + 4)

        @block.vector
        def _(dve):
            link = Link(dve, s.v)
            tt, stt = nc.vector.tensor_tensor, nc.vector.scalar_tensor_tensor
            col = lambda c: m.PT[:, bass.ds(c, 1)]

            def low(b):
                dve.wait_ge(s.b_high, b + 1)
                low_part(nc, Bl[:, :, :], branch[b], Bh[:, :, :]).then_inc(s.b_ready, 1)

            def merge(i):
                dve.wait_ge(s.sigmoids, 2 * i + 2)
                ring.products(dve, 3 * i + 2)
                out = m.merged[:, 4 * (i % 2):4 * (i % 2) + 4, :]
                if i < 2:
                    tt(out, gate, m.psum[:, 4:8, :], ALU.mult).then_inc(s.merged, 1)
                else:
                    link(tt(gate, gate, m.psum[:, 4:8, :], ALU.mult))
                    tt(out, out, gate, ALU.add).then_inc(s.merged, 1)

            def taps(first):
                base = link.n
                with dve.Fori(0, chunk) as k:
                    chain = Link(dve, s.v, k + base)
                    for j in range(4):
                        last = stt(ca[:, j, :], GP[:, j, bass.ds(k + first, S)], col(k * 4 + (c_cw + 4 * first + j)),
                                   ca[:, j, :], ALU.mult, ALU.add)
                    chain(last)
                link.n += chunk

            nc.vector.memset(m.conv_end[:, :], 0.0).then_inc(s.b_value, 1)
            dve.wait_ge(s.pads, 1)
            link(tt(GP[:, :, CF_K - 1:], ca, cb, ALU.mult))
            nc.vector.memset(m.conv_end[:, :], 0.0).then_inc(s.glu, 1)
            low(0)
            link(tt(sx, sc, sx, ALU.mult))
            for j in range(4):
                nc.vector.tensor_scalar(sc[:, j, :], sx[:, j, :], col(c_sw + 8 + j), None, ALU.mult)
                link(nc.vector.tensor_scalar(ca[:, j, :], GP[:, j, CF_K - 1:], col(c_cw + 120 + j),
                                             m.param("cf_b", 1, 4 * layer + j), ALU.mult, ALU.add))
            for k in (1, 0):
                lag = SC_K - 1 - k
                for j in range(4):
                    last = stt(sc[:, j, lag:], sx[:, j, 0:S - lag], col(c_sw + 4 * k + j), sc[:, j, lag:], ALU.mult, ALU.add)
                link(last)
            tt(sb, sb, sc, ALU.mult).then_inc(s.b_value, 1)
            for i in range(steps):
                merge(i)
                if i < 3:
                    taps(i * chunk)
                if i == 1:
                    low(1)
                if i == 2:
                    nc.vector.memset(m.conv_end[:, :], 0.0).then_inc(s.conv, 1)
                if i == 3:
                    dve.wait_ge(s.means, 1)
                    link(nc.vector.tensor_scalar(m.root[:, :], m.psum[:, 4, :], -1.0 / MIX, None, ALU.mult))
                    tt(ca, ca, m.root[:, :].unsqueeze(1).broadcast_to([P, 4, S]), ALU.add).then_inc(s.centred, 1)
                    dve.wait_ge(s.root, 1)
                    link(nc.vector.reciprocal(m.root[:, :], m.root[:, :]))
                    tt(ca, ca, m.root[:, :].unsqueeze(1).broadcast_to([P, 4, S]), ALU.mult).then_inc(s.scaled, 1)
                    low(2)
        ring.first += n


POST_SEMS = ("y_ready", "y_squared", "y_sum", "y_root")


def post_norm_pe(nc, pe, m, s, squares):
    pe.wait_ge(s.y_squared, 1)
    for c in range(KC):
        mm = nc.tensor.matmul(m.psum[:, 0, :], m.const("ones"), squares[:, c, :], start=(c == 0), stop=(c == KC - 1))
    mm.then_inc(s.y_sum, 1)


def post_norm_act(nc, act, m, s, y, squares):
    nc.scalar.activation(y, m.psum[:, :, :], ACT.Copy).then_inc(s.y_ready, 1)
    nc.scalar.activation(squares, m.psum[:, :, :], ACT.Square).then_inc(s.y_squared, 1)
    act.wait_ge(s.y_sum, 1)
    nc.scalar.activation(m.root[:, :], m.psum[:, 0, :], ACT.Sqrt, bias=m.const("eps"), scale=1.0 / D).then_inc(s.y_root, 1)


def post_norm_dve(nc, dve, m, s, y, gain):
    link = Link(dve, s.v)
    dve.wait_ge(s.y_root, 1)
    dve.wait_ge(s.y_ready, 1)
    link(nc.vector.reciprocal(m.root[:, :], m.root[:, :]))
    for c in range(KC):
        last = nc.vector.scalar_tensor_tensor(y[:, c, :], y[:, c, :], gain[:, c:c + 1], m.root[:, :], ALU.mult, ALU.mult)
    link(last)
    nc.vector.tensor_tensor(m.X[:, :, :], m.X[:, :, :], y, ALU.add)


def phase_mix_out(nc, m, ph, ring, d, layer, following):
    n = 4
    with ExitStack() as ctx:
        block, s, stale = ph.open(ctx, *POST_SEMS, "v", "h_high", "h_ready")

        @block.sync
        def _(sp):
            sp.sem_clear(stale)
            ring.stream(sp, d.w_o_2[layer], n, following)

        @block.gpsimd
        def _(pool):
            ring.make_lows(pool, n, following is not None)

        @block.tensor
        def _(pe):
            for u in range(n):
                unit_products(nc, pe, ring, u, m.Hs, m.psum, k_ready=h_tiles(pe, s) if u == 0 else None)
            post_norm_pe(nc, pe, m, s, m.raw[:, 0:8, :])

        @block.scalar
        def _(act):
            for c in range(KC):
                nc.scalar.activation(m.Hh[:, c, :], m.merged[:, c, :], ACT.Copy).then_inc(s.h_high, 1)
            for u in range(n if following is not None else n - Ring.AHEAD):
                ring.make_high(act, u + Ring.AHEAD)
            ring.products(act, n - 1)
            post_norm_act(nc, act, m, s, m.merged[:, :, :], m.raw[:, 0:8, :])

        @block.vector
        def _(dve):
            for c in range(KC):
                dve.wait_ge(s.h_high, c + 1)
                low_part(nc, m.Hl[:, c, :], m.merged[:, c, :], m.Hh[:, c, :]).then_inc(s.h_ready, 1)
            post_norm_dve(nc, dve, m, s, m.merged[:, :, :], m.param("mix_post", KC, layer * KC))
        ring.first += n


def phase_ffn_up(nc, m, ph, ring, d, layer, following):
    n = FF_TILES
    with ExitStack() as ctx:
        block, s, stale = ph.open(ctx, *NORM_SEMS, "v", "last_tap", "read_out", "silu", "f_value", "f_high", "f_low")
        T = m.F[:, :, :].rearrange("p (a j) n -> p a j n", a=2)
        w0 = PCOL["ffn_w"] + layer * FFN_K * 2 * FF_TILES

        def tile_of(x, u, turn):
            return x[:, bass.ds(turn * TURN + u, 1), :].rearrange("p a n -> p (a n)")

        @block.sync
        def _(sp):
            sp.sem_clear(stale)
            ring.stream(sp, d.w_up[layer], n, following)

        @block.gpsimd
        def _(pool):
            ring.make_lows(pool, n)

        @block.tensor
        def _(pe):
            norm_pe(nc, pe, m, s)
            pe.wait_ge(s.root, 1)
            streamed_products(nc, pe, ring, n, m.Hs, m.psum, s.read_out, k_ready=h_tiles(pe, s))

        def tap(u, turn, j, k):
            return m.PT[:, bass.ds(turn * TURN + (w0 + k * 2 * FF_TILES + j * FF_TILES + u), 1)]

        @block.scalar
        def _(act):
            norm_act(nc, act, m, s, m.X)
            act.sem_inc(s.f_low, 2)

            def body(u, turn):
                ring.products(act, u, turn)
                act.wait_ge(s.f_low, turn * TURN + (u + 1))
                for j in range(2):
                    b = (2 * u + j) % BANKS
                    last = nc.scalar.activation(T[:, u % 2, j, :], m.psum[:, b, :], ACT.Copy, scale=tap(u, turn, j, 2))
                last.then_inc(s.last_tap, 1)
                ring.make_high(act, u + Ring.AHEAD, turn)
                act.wait_ge(s.read_out, turn * TURN + (u + 1))
                nc.scalar.activation(T[:, u % 2, 0, :], T[:, u % 2, 0, :], ACT.Silu).then_inc(s.silu, 1)
                act.wait_ge(s.f_value, turn * TURN + (u + 1))
                nc.scalar.activation(tile_of(m.ffs[0], u, turn), T[:, u % 2, 1, :], ACT.Copy).then_inc(s.f_high, 1)
            over_units(act, n, body)

        @block.vector
        def _(dve):
            link = Link(dve, s.v)
            norm_dve(nc, dve, m, s, link, m.X, m.param("ffn_pre", KC, layer * KC))
            base = link.n

            def body(u, turn):
                dve.wait_ge(s.last_tap, turn * TURN + (u + 1))
                chain = Link(dve, s.v, turn * TURN + (base + u))
                t = T[:, u % 2, :, :]
                for k in (1, 0):
                    for j in range(2):
                        b = (2 * u + j) % BANKS
                        lag = FFN_K - 1 - k
                        last = nc.vector.scalar_tensor_tensor(t[:, j, lag:], m.psum[:, b, 0:S - lag], tap(u, turn, j, k),
                                                              t[:, j, lag:], ALU.mult, ALU.add)
                    if k:
                        chain(last)
                last.then_inc(s.read_out, 1)
                dve.wait_ge(s.silu, turn * TURN + (u + 1))
                nc.vector.tensor_tensor(t[:, 1, :], t[:, 0, :], t[:, 1, :], ALU.mult).then_inc(s.f_value, 1)
                dve.wait_ge(s.f_high, turn * TURN + (u + 1))
                low_part(nc, tile_of(m.ffs[1], u, turn), t[:, 1, :], tile_of(m.ffs[0], u, turn)).then_inc(s.f_low, 1)
            over_units(dve, n, body)
        ring.first += n


def phase_ffn_down(nc, m, ph, ring, d, layer, following):
    n = FF_TILES // 2
    with ExitStack() as ctx:
        block, s, stale = ph.open(ctx, *POST_SEMS, "v")
        y = on_chip(nc, ctx, "y", [P, KC, S], F32)
        squares = on_chip(nc, ctx, "y_squares", [P, KC, S], F32)

        @block.sync
        def _(sp):
            sp.sem_clear(stale)
            ring.stream(sp, d.w_down[layer], n, following)

        @block.gpsimd
        def _(pool):
            ring.make_lows(pool, n, following is not None)

        @block.tensor
        def _(pe):
            def unit(u, turn):
                w = [x.rearrange("p (k m) -> p k m", k=2) for x in ring.parts(pe, u, turn)]
                for k in range(2):
                    rhs = [x[:, bass.ds(turn * 2 * TURN + (2 * u + k), 1), :].rearrange("p a n -> p (a n)") for x in m.ffs]
                    for t in range(KC):
                        mm = split_matmul(nc, m.psum[:, t, :], [x[:, k, t * P:(t + 1) * P] for x in w], rhs,
                                          u == 0 and k == 0, u == n - 1 and k == 1)
                mm.then_inc(ring.used, 1)

            unit(0, 0)
            turns = (n - 2) // TURN
            with pe.Fori(0, turns) as i:
                for k in range(TURN):
                    unit(1 + k, i)
            for u in range(1 + turns * TURN, n):
                unit(u, 0)
            post_norm_pe(nc, pe, m, s, squares)

        @block.scalar
        def _(act):
            end = n if following is not None else n - Ring.AHEAD
            over_units(act, end, lambda u, turn: ring.make_high(act, u + Ring.AHEAD, turn))
            ring.products(act, n - 1)
            post_norm_act(nc, act, m, s, y[:, :, :], squares[:, :, :])

        @block.vector
        def _(dve):
            post_norm_dve(nc, dve, m, s, y[:, :, :], m.param("ffn_post", KC, layer * KC))
        ring.first += n


def phase_store(nc, m, ph, ring, d):
    with ExitStack() as ctx:
        block, s, stale = ph.open(ctx, "stored")

        @block.sync
        def _(sp):
            sp.dma_start(d.out, m.X[:, :, :]).then_inc(s.stored, 16)
            sp.wait_ge(s.stored, 16)


def build(nc, d, upto=99):
    with ExitStack() as whole:
        def sb(ctx, name, shape, dtype=F32):
            return on_chip(nc, ctx, name, shape, dtype)

        m = Memory()
        m.X = sb(whole, "x", [P, KC, S])
        m.PT = sb(whole, "params", [P, PCOLS])
        m.CT = sb(whole, "consts", [P, CCOLS])
        m.WRh = sb(whole, "router_high", [P, DEPTH, KC, GROUPS + EXPERTS], F32R)
        m.WRl = sb(whole, "router_low", [P, DEPTH, KC, GROUPS + EXPERTS], F32R)
        m.RB = sb(whole, "router_b", [P, DEPTH, GROUPS + EXPERTS])
        m.mod = sb(whole, "mod", [P, DEPTH * 48])
        m.gain = sb(whole, "gain", [P, DEPTH, 2, KC])
        m.root = sb(whole, "root", [P, S])
        m.priority = sb(whole, "priority", [P, TT, 4])
        m.conv_end = sb(whole, "conv_end", [P, 1])
        m.psum = whole.enter_context(nc.psum_tensor("psum", [P, BANKS, S], F32))
        ring = Ring(nc, whole)
        ph = Phases(nc)
        m.const = lambda name: m.CT[:, CCOL[name]:CCOL[name] + dict(CONST_TILES)[name]]
        m.param = lambda name, n, at=0: m.PT[:, PCOL[name] + at:PCOL[name] + at + n]

        def mod(layer, k):
            return m.mod[:, 48 * layer + KC * k:48 * layer + KC * (k + 1)]

        def operand(ctx, name, tiles):
            return sb(ctx, name + "_high", [P, tiles, S], F32R), sb(ctx, name + "_low", [P, tiles, S], F32R)

        def give_h(ctx):
            m.Hs = m.Hh, m.Hl = operand(ctx, "h", KC)

        def moe(layer, following, modulation=None):
            with ExitStack() as part:
                give_h(part)
                m.cb = sb(part, "expert_weights", [P, EXPERTS, S])
                with ExitStack() as inner:
                    m.F = sb(inner, "norm_tiles", [P, 4, S])
                    phase_router(nc, m, ph, ring, layer, mod(layer, 3), m.gain[:, layer, 1, :])
                phase_experts(nc, m, ph, ring, d.moe[layer], mod(layer, 5), following, modulation)

        def finish():
            phase_store(nc, m, ph, ring, d)

        with ExitStack() as early:
            m.c_act = sb(early, "c_act", [P, D])
            with ExitStack() as part:
                m.sin, m.cos = sb(part, "rope_sin", [P, S]), sb(part, "rope_cos", [P, S])
                phase_load(nc, m, ph, ring, d)
                m.k_pe = sb(part, "k_pe", [P, S])
                m.qn, m.kn = sb(part, "q_nope", [P, HEADS, S]), sb(part, "k_nope", [P, HEADS, S])
                m.qp, m.vt = sb(part, "q_pe", [P, 4, S]), sb(part, "v_tok", [P, TT, D])
                with ExitStack() as inner:
                    m.lat = sb(inner, "latents", [P, 4, S])
                    m.lat_h, m.lat_l = operand(inner, "latents", 3)
                    with ExitStack() as narrow:
                        give_h(narrow)
                        m.F = m.sq4 = sb(narrow, "norm_tiles", [P, 4, S])
                        m.r4 = sb(narrow, "r4", [P, 3, S])
                        phase_latents(nc, m, ph, ring, d, d.mla_w_heads)
                    m.sq8 = sb(inner, "sq8", [P, 2, 4, S])
                    phase_heads(nc, m, ph, ring, d, d.mla_w_o)
                give_h(part)
                phase_attention(nc, m, ph, ring, d)
                phase_residual(nc, m, ph, ring, d.mla_w_o, mod(0, 2), d.moe[0],
                               mod_units=d.ada_w[MOD_UNITS - MOD_REST:MOD_UNITS, :, :])
            if upto == 0:
                return finish()
            moe(0, d.hy_w_in, d.ada_w[MOD_UNITS:2 * MOD_UNITS, :, :])
        if upto == 1:
            return finish()
        with ExitStack() as part:
            m.xv = sb(part, "x1_x2_v", [P, 24, S])
            with ExitStack() as inner:
                give_h(inner)
                m.F = sb(inner, "norm_tiles", [P, 4, S])
                phase_hyena_in(nc, m, ph, ring, d, d.hy_w_out)
            with ExitStack() as inner:
                m.hdn = sb(inner, "filter_hidden", [FILTER_WIDTH, S])
                m.fwd, m.inv = sb(inner, "dft_fwd", [P, 2, TT, 256]), sb(inner, "dft_inv", [P, 2, 4, 256])
                phase_filter_mlp(nc, m, ph, ring, d)
                for order in range(2):
                    for half in range(2):
                        phase_long_conv(nc, m, ph, ring, d, order, half)
            give_h(part)
            phase_residual(nc, m, ph, ring, d.hy_w_out, mod(1, 2), d.moe[1], z=m.xv[:, 16:24, :])
        if upto == 2:
            return finish()
        moe(1, d.w_proj[0])
        if upto == 3:
            return finish()
        for layer in range(DEPTH):
            with ExitStack() as part:
                give_h(part)
                m.raw = sb(part, "projections", [P, 28, S])
                with ExitStack() as inner:
                    m.vr = sb(inner, "v_tok", [P, TT, MIX])
                    phase_project(nc, m, ph, ring, d, layer, d.w_branches[layer])
                    phase_retention(nc, m, ph, ring, d)
                m.merged = sb(part, "merged", [P, KC, S])
                phase_branches(nc, m, ph, ring, d, layer, d.w_o_2[layer])
                phase_mix_out(nc, m, ph, ring, d, layer, d.w_up[layer])
            if upto == 4 + 2 * layer:
                return finish()
            with ExitStack() as part:
                m.ffs = operand(part, "ff", FF_TILES)
                with ExitStack() as inner:
                    give_h(inner)
                    m.F = sb(inner, "norm_tiles", [P, 4, S])
                    phase_ffn_up(nc, m, ph, ring, d, layer, d.w_down[layer])
                phase_ffn_down(nc, m, ph, ring, d, layer, d.w_proj[1] if layer == 0 else None)
            if upto == 5 + 2 * layer:
                return finish()
        finish()


def table_consts():
    f = np.float32
    parts = {"ident": np.eye(P), "ones": np.ones((P, P)), "ones64": np.kron(np.eye(2), np.ones((64, 64)))}
    rot = np.zeros((P, P))
    for b in (0, 64):
        for j in range(32):
            rot[b + 32 + j, b + j] = -1
            rot[b + j, b + 32 + j] = 1
    parts["rot"] = rot
    middle = NORM_ROWS[-1] - 1
    parts["pick_one"], parts["pick_two"] = np.zeros((P, 2 * middle + 1)), np.zeros((P, 2 * middle + 1))
    pe_rows = np.zeros((NORM_ROWS[-1], 4 * P))
    pe_rows[NORM_ROWS[2] + np.arange(4 * P) // ROPE, np.arange(4 * P)] = 1
    parts["pick_one"][:, middle] = 1.0 / NOPE
    parts["pick_two"][:ROPE, middle] = parts["pick_two"][ROPE:, middle + 1] = 1.0 / ROPE
    parts["inv_freq"] = (f(1) / (f(10000.0) ** (np.arange(0, 64, 2, dtype=f) / f(64))))[np.arange(P) % 32][:, None]
    parts["eps"] = np.full((P, 1), EPS)
    parts["zero"] = np.zeros((P, 1))
    consts = np.concatenate([parts[name].astype(f) for name, _ in CONST_TILES], axis=1)

    order = np.concatenate([np.arange(0, S, 2), np.arange(1, S, 2)])
    t = np.linspace(0.0, 1.0, S, dtype=f)[:, None]
    w = (f(2.0 * math.pi) * np.arange(S, dtype=f)[:, None] / f(S)).astype(f)
    fr = np.linspace(1e-4, 15, 16, dtype=f)[None, :]
    z = np.concatenate([t, np.cos(fr * w), -np.sin(fr * w)], axis=-1).astype(f)
    deltas = np.abs(np.linspace(math.log(0.3) / 1e-2, math.log(1.5) / 1e-2, D, dtype=f))
    decay = np.exp(-t * deltas).astype(f)[order].reshape(TT, P, D).transpose(1, 0, 2)
    k = np.arange(256)
    angle = math.pi * (2 * k[None, :] + 1) * order[:, None] / 1024.0
    fwd = np.stack([np.cos(angle), np.sin(angle)]).reshape(2, TT, P, 256).transpose(2, 0, 1, 3)
    back = np.stack([np.cos(angle).T, np.sin(angle).T]) / 512.0
    inv = back.reshape(2, 2, P, 2, 256).transpose(2, 3, 0, 1, 4).reshape(P, 2, 4, 256)

    gamma = 1.0 - np.exp2(-5.0 - np.arange(RET_HEADS))
    lag = np.arange(S)[None, :] - np.arange(P)[:, None]
    ret = np.where(lag[:, None, :] >= 0, gamma[None, :, None] ** np.maximum(lag, 0)[:, None, :], 0.0) / 8.0
    inv_r = f(10000.0) ** (-np.arange(32, dtype=f) / f(32))
    ang = (np.arange(S, dtype=f)[None, :] * inv_r[np.arange(P) % 32][:, None]).astype(f)
    rotary = np.stack([np.cos(ang), np.sin(ang)], axis=1)
    return {name: np.ascontiguousarray(a, dtype=f) for name, a in
            (("consts", consts), ("pe_rows", pe_rows), ("zT", z[order].T), ("decay", decay), ("dft_fwd", fwd), ("dft_inv", inv),
             ("ret_decay", ret), ("ret_rotary", rotary))}


def feature_tiles(a):
    return a.reshape(-1, P).T


def padded_rows(a):
    return np.concatenate([a.T, np.zeros_like(a.T)], axis=0)


def units(w, cols=256):
    k, n = w.shape[0] // P, w.shape[1] // cols
    return w.reshape(k, P, n, cols).transpose(2, 1, 0, 3).reshape(n, P, k * cols)


def layout(i):
    a = {k: np.asarray(v) for k, v in i.items()}
    out = table_consts()
    out["x"] = a["x"][0].T.reshape(KC, P, S).transpose(1, 0, 2)
    out["positions"] = np.broadcast_to(a["positions"].reshape(1, S), (P, S))
    twice = lambda v: np.concatenate([v, v])
    hy = lambda name: a[name][0]
    params = {
        "ada_b": a["ada_b"], "norm_mix_g": a["norm_mix_g"], "norm_ffn_g": a["norm_ffn_g"],
        "q_a_g": a["mla_q_a_g"], "kv_a_g": a["mla_kv_a_g"],
        "q_nope_g": a["mla_q_norm_g"][0, :NOPE], "q_pe_g": twice(a["mla_q_norm_g"][0, NOPE:]),
        "k_nope_g": a["mla_k_norm_g"][0, :NOPE], "k_pe_g": twice(a["mla_k_norm_g"][0, NOPE:]),
        "hy_b_in": hy("hy_b_in"), "hy_conv_w": hy("hy_conv_w"), "hy_conv_b": hy("hy_conv_b"),
        "hy_filt_bias": hy("hy_filt_bias"),
        "mix_pre": a["norm_mix_pre_2"], "mix_post": a["norm_mix_post_2"],
        "ffn_pre": a["norm_ffn_pre_2"], "ffn_post": a["norm_ffn_post_2"],
        "sc_w": a["sc_conv_w_2"], "cf_w": a["cf_conv_w_2"], "cf_b": a["cf_conv_b_2"],
        "cf_g": a["cf_ln_g_2"], "cf_lb": a["cf_ln_b_2"], "ffn_w": a["ffn_conv_w_2"],
    }
    cols = {name: feature_tiles(v) for name, v in params.items()}
    cols["hy_fb"] = padded_rows(np.concatenate([a["hy_f_b1"], a["hy_f_b2"], a["hy_f_b3"]]))
    cols["hy_ff"] = padded_rows(np.concatenate([a["hy_f_freq1"], a["hy_f_freq2"], a["hy_f_freq3"]]))
    out["params"] = np.concatenate([cols[name] for name, _ in PARAM_TILES], axis=1)
    assert out["params"].shape == (P, PCOLS)
    wr = np.concatenate([a["moe_wg"], a["moe_we"]], axis=2)
    out["router_w"] = wr.reshape(DEPTH, KC, P, GROUPS + EXPERTS).transpose(2, 0, 1, 3)
    out["router_b"] = np.broadcast_to(np.concatenate([a["moe_bg"], a["moe_be"]], axis=1)[None], (P, DEPTH, 20))

    out["c"] = np.broadcast_to(a["c"].reshape(1, D), (P, D))
    out["ada_w"] = a["ada_w"].transpose(0, 2, 1).reshape(DEPTH * 24, 2, P, D).transpose(0, 2, 1, 3).reshape(-1, P, 2 * D)
    wd = a["mla_w_down"][0]
    out["mla_w_down"] = units(np.concatenate([wd, wd[:, -ROPE:]], axis=1))
    uq = a["mla_w_uq"][0].reshape(Q_LORA, HEADS, QK_HEAD)
    uq = np.concatenate([uq[:, :, :NOPE].reshape(Q_LORA, -1), uq[:, :, NOPE:].reshape(Q_LORA, -1)], axis=1)
    uq = np.concatenate([uq, np.zeros((Q_LORA, 512), uq.dtype)], axis=1)
    ukv = a["mla_w_ukv"][0].reshape(KV_LORA, HEADS, NOPE + V_HEAD)
    ukv = np.concatenate([ukv[:, :, :NOPE].reshape(KV_LORA, -1), ukv[:, :, NOPE:].reshape(KV_LORA, -1)], axis=1)
    out["mla_w_heads"] = np.concatenate([units(uq, 1024), ukv[None]])
    out["mla_w_o"] = units(a["mla_w_o"][0])
    for l in range(DEPTH):
        g = []
        for k in range(GROUPS):
            for e in range(k * PER_GROUP, (k + 1) * PER_GROUP):
                g += [units(a["moe_w_gate"][l, e]), units(a["moe_w_up"][l, e])]
            g.append(units(a["moe_w_down"][l, k * PER_GROUP:(k + 1) * PER_GROUP].reshape(PER_GROUP * D_EXPERT, D)))
        out[f"moe_{l}"] = np.concatenate(g)
        w = a["w_in_2"][l]
        q, v, r, g = w[:, :512], w[:, 512:1024], w[:, 1024:4096], w[:, 4096:]
        out[f"w_proj_{l}"] = units(np.concatenate([q, r, v], axis=1))
        outs = [units(a[n][l], 512) for n in ("w_ret_out_2", "w_sc_out_2", "w_cf_out_2")]
        g = units(g)
        out[f"w_branches_{l}"] = np.concatenate(
            [x for i in range(6) for x in (g[2 * i:2 * i + 2], outs[i // 2][i % 2:i % 2 + 1])])
        out[f"w_o_2_{l}"] = units(a["w_o_2"][l])
        up = a["w_up_2"][l].reshape(D, 2, FF_TILES, P).transpose(0, 2, 1, 3).reshape(D, -1)
        out[f"w_up_{l}"] = units(up)
        dn = a["w_down_2"][l].reshape(FF_TILES // 2, 2, P, D)
        out[f"w_down_{l}"] = dn.transpose(0, 2, 1, 3).reshape(FF_TILES // 2, P, 2 * D)
    out["hy_w_in"] = units(hy("hy_w_in"))
    out["hy_w_out"] = units(hy("hy_w_out"))
    out["hy_f_w1"], out["hy_f_w2"], out["hy_f_w3"] = hy("hy_f_w1"), hy("hy_f_w2"), hy("hy_f_w3")
    out["hy_f_w4"] = hy("hy_f_w4").reshape(FILTER_WIDTH, 2, 2, D)
    return {k: np.ascontiguousarray(v) for k, v in out.items()}


def declare(nc, arrays):
    found = {}
    for name, v in arrays.items():
        ap = nc.dram_tensor("in_" + name, list(v.shape), mybir.dt.from_np(v.dtype), kind="ExternalInput").ap()
        if name[-2:] in ("_0", "_1"):
            found.setdefault(name[:-2], []).append(ap)
        else:
            found[name] = ap
    found["out"] = nc.dram_tensor("out_x", [P, KC, S], F32, kind="ExternalOutput").ap()
    return namedtuple("Dram", found)(*found.values())


def kernel(**inputs):
    import concourse.bacc as bacc
    from concourse.bass_utils import run_bass_kernel_spmd

    arrays = layout(inputs)
    nc = bacc.Bacc("TRN2", target_bir_lowering=False, num_devices=1)
    build(nc, declare(nc, arrays))
    r = run_bass_kernel_spmd(nc, [{"in_" + k: v for k, v in arrays.items()}], core_ids=[0])
    out = np.asarray(r.results[0]["out_x"])
    return np.ascontiguousarray(out.transpose(1, 0, 2).reshape(D, S).T)[None]
```

```python
import itertools
import math
from collections import namedtuple
from contextlib import ExitStack

import numpy as np

import concourse.bass as bass
from concourse import mybir

F32 = mybir.dt.float32
F32R = mybir.dt.float32r
I32 = mybir.dt.int32
ALU = mybir.AluOpType
ACT = mybir.ActivationFunctionType
AX = mybir.AxisListType

P = 128
D = 1024
S = 512
DEPTH = 2
KC = D // P
TT = S // P
UNIT = 2048
TURN = 4
BANKS = 8

HEADS, Q_LORA, KV_LORA, NOPE, ROPE, V_HEAD = 8, 256, 128, 128, 64, 128
QK_HEAD = NOPE + ROPE
GROUPS, PER_GROUP, D_EXPERT = 4, 4, 256
EXPERTS = GROUPS * PER_GROUP
FILTER_EMB, FILTER_WIDTH = 33, 64
RET_HEADS, RET_QK, RET_V = 4, 64, 128
MIX = 512
D_FF = 2816
FF_TILES = D_FF // P
CF_K, SC_K, FFN_K = 31, 3, 3
EPS = 1e-6

PARAM_TILES = [
    ("ada_b", DEPTH * 48), ("norm_mix_g", DEPTH * KC), ("norm_ffn_g", DEPTH * KC),
    ("q_a_g", 2), ("kv_a_g", 1), ("q_nope_g", 1), ("q_pe_g", 1), ("k_nope_g", 1), ("k_pe_g", 1),
    ("hy_b_in", 24), ("hy_conv_w", 72), ("hy_conv_b", 24), ("hy_filt_bias", 16),
    ("hy_fb", 3), ("hy_ff", 3),
    ("mix_pre", DEPTH * KC), ("mix_post", DEPTH * KC), ("ffn_pre", DEPTH * KC), ("ffn_post", DEPTH * KC),
    ("sc_w", DEPTH * SC_K * 4), ("cf_w", DEPTH * CF_K * 4), ("cf_b", DEPTH * 4),
    ("cf_g", DEPTH * 4), ("cf_lb", DEPTH * 4), ("ffn_w", DEPTH * FFN_K * 2 * FF_TILES),
]
PCOL, PCOLS = {}, 0
for _name, _n in PARAM_TILES:
    PCOL[_name] = PCOLS
    PCOLS += _n

NORM_ROWS = (0, 4, 8, 16, 20, 24)
CONST_TILES = [("ident", P), ("ones", P), ("ones64", P), ("rot", P), ("pick_one", 2 * NORM_ROWS[-1] - 1),
               ("pick_two", 2 * NORM_ROWS[-1] - 1), ("inv_freq", 1), ("eps", 1), ("zero", 1)]
CCOL, CCOLS = {}, 0
for _name, _n in CONST_TILES:
    CCOL[_name] = CCOLS
    CCOLS += _n

TWO_PI_A = 6.28125
TWO_PI_B = math.floor((2 * math.pi - TWO_PI_A) * 2.0 ** 21) / 2.0 ** 21
TWO_PI_C = float(np.float32(2 * math.pi - TWO_PI_A - TWO_PI_B))
PI_DOWN = 3.1415925
ROUND_MAGIC = 12582912.0


BUFFERS = itertools.count()


def on_chip(nc, ctx, name, shape, dtype):
    return ctx.enter_context(nc.sbuf_tensor(f"{name}_{next(BUFFERS)}", shape, dtype))


class Memory:
    pass


class Phases:

    POOL = 44

    def __init__(self, nc):
        self.nc = nc
        self.pools = [[nc.alloc_semaphore(f"phase{h}_{n}") for n in range(self.POOL)] for h in range(2)]
        self.turn = 0

    def open(self, ctx, *names):
        mine, other = self.pools[self.turn], self.pools[1 - self.turn]
        self.turn = 1 - self.turn
        assert len(names) <= self.POOL
        block = ctx.enter_context(self.nc.Block())
        stale = range(other[0].num, other[-1].num + 1)
        return block, namedtuple("Signals", names)(*mine[:len(names)]), stale


class Link:

    def __init__(self, eng, sem, start=0):
        self.eng, self.sem, self.start, self.n = eng, sem, start, 0

    def __call__(self, instruction):
        instruction.then_inc(self.sem, 1)
        self.n += 1
        self.eng.wait_ge(self.sem, self.start + self.n)


class Ring:

    def __init__(self, nc, ctx):
        self.nc = nc
        self.raw = on_chip(nc, ctx, "weights_raw", [P, 2, UNIT], F32)
        self.high = on_chip(nc, ctx, "weights_high", [P, 2, UNIT], F32R)
        self.low = on_chip(nc, ctx, "weights_low", [P, 2, UNIT], F32R)
        self.loaded = [nc.alloc_semaphore(f"weights_loaded_{k}") for k in range(2)]
        self.high_done = nc.alloc_semaphore("weights_high_done")
        self.low_done = nc.alloc_semaphore("weights_low_done")
        self.used = nc.alloc_semaphore("weights_used")
        self.first = 0
        self.issued = 0
        self.lowered = 0

    def _load(self, sp, src):
        g = self.issued
        if g >= 2:
            sp.wait_ge(self.low_done, g - 1)
        sp.dma_start(self.raw[:, g % 2, :], src).then_inc(self.loaded[g % 2], 16)
        self.issued += 1

    def stream(self, sp, src, n, following=None):
        while self.issued < self.first + n and self.issued < 2:
            self._load(sp, src[self.issued - self.first, :, :])
        u = self.issued - self.first
        turns = (n - u) // TURN
        if turns > 1:
            g0 = self.issued
            with sp.Fori(0, turns) as i:
                for k in range(TURN):
                    sp.wait_ge(self.low_done, i * TURN + (g0 + k - 1))
                    sp.dma_start(self.raw[:, (g0 + k) % 2, :],
                                 src[bass.ds(i * TURN + (u + k), 1), :, :].rearrange("a p n -> p (a n)"))\
                        .then_inc(self.loaded[(g0 + k) % 2], 16)
            self.issued += turns * TURN
        while self.issued < self.first + n:
            self._load(sp, src[self.issued - self.first, :, :])
        if following is not None:
            for k in range(2):
                self._load(sp, following[k, :, :])

    def make_high(self, act, u, turn=0, per=4):
        g = self.first + u
        act.wait_ge(self.loaded[g % 2], turn * (8 * per) + 16 * (g // 2 + 1))
        if g >= 2:
            act.wait_ge(self.used, turn * per + (g - 1))
        self.nc.scalar.activation(self.high[:, g % 2, :], self.raw[:, g % 2, :], ACT.Copy).then_inc(self.high_done, 1)

    def _make_low(self, pool, g, turn=0):
        pool.wait_ge(self.high_done, turn * TURN + (g + 1))
        self.nc.gpsimd.tensor_tensor(self.low[:, g % 2, :], self.raw[:, g % 2, :], self.high[:, g % 2, :].bitcast(F32),
                                     ALU.subtract).then_inc(self.low_done, 1)

    def make_lows(self, pool, n, more=True):
        end = self.first + n + (1 if more else 0)
        turns = (end - self.lowered) // TURN
        if turns > 1:
            with pool.Fori(0, turns) as i:
                for k in range(TURN):
                    self._make_low(pool, self.lowered + k, i)
            self.lowered += turns * TURN
        while self.lowered < end:
            self._make_low(pool, self.lowered)
            self.lowered += 1

    def parts(self, pe, u, turn=0, per=4):
        g = self.first + u
        pe.wait_ge(self.low_done, turn * per + (g + 1))
        return self.high[:, g % 2, :], self.low[:, g % 2, :]

    def products(self, eng, u, turn=0, per=4):
        eng.wait_ge(self.used, turn * per + (self.first + u + 1))


def split_matmul(nc, out, w, rhs, start, stop):
    nc.tensor.matmul(out, w[1], rhs[0], start=start, stop=False)
    nc.tensor.matmul(out, w[0], rhs[0], start=False, stop=False)
    return nc.tensor.matmul(out, w[0], rhs[1], start=False, stop=stop)


def unit_products(nc, pe, ring, u, rhs, psum, kc=KC, tiles=2, turn=0, per=4, k_ready=None, banks=None):
    w = [x.rearrange("p (k m) -> p k m", k=kc) for x in ring.parts(pe, u, turn, per)]
    order = [(j, k) for j in range(tiles) for k in range(kc)]
    if k_ready is not None:
        order = [(j, k) for k in range(kc) for j in range(tiles)]
    for j, k in order:
        b = banks[j] if banks else (tiles * u + j) % BANKS
        if k_ready is not None and j == 0:
            k_ready(k)
        mm = split_matmul(nc, psum[:, b, :], [x[:, k, j * P:(j + 1) * P] for x in w],
                          [x[:, k, :] for x in rhs], k == 0, k == kc - 1)
    mm.then_inc(ring.used, 1)


def streamed_products(nc, pe, ring, n, rhs, psum, read_out, k_ready=None, after=None):
    for u in range(min(n, TURN)):
        unit_products(nc, pe, ring, u, rhs, psum, k_ready=k_ready if u == 0 else None)
        if after is not None:
            after(u)
    turns = (n - TURN) // TURN
    if turns > 1:
        with pe.Fori(0, turns) as i:
            for k in range(TURN):
                pe.wait_ge(read_out, i * TURN + (k + 1))
                unit_products(nc, pe, ring, TURN + k, rhs, psum, turn=i)
    else:
        turns = 0
    for u in range(TURN * (turns + 1), n):
        pe.wait_ge(read_out, u - TURN + 1)
        unit_products(nc, pe, ring, u, rhs, psum)


def over_units(eng, n, body, first=0, after=None):
    turns = (n - 1) // TURN if not first else 0
    if turns > 1:
        with eng.Fori(0, turns) as i:
            for k in range(TURN):
                body(k, i)
    else:
        turns = 0
    for u in range(TURN * turns, n):
        body(u, 0)
        if u < first:
            after(u)


NORM_SEMS = ("squared", "added", "summed", "root", "scaled", "h_high", "h_ready")


def norm_act(nc, act, m, s, src, shift=None, ring=None):
    for c in range(KC):
        if c >= 4:
            act.wait_ge(s.added, max(c - 4, 1))
        nc.scalar.activation(m.F[:, c % 4, :], src[:, c, :], ACT.Square).then_inc(s.squared, 1)
    if ring is not None:
        ring.make_high(act, 1)
    act.wait_ge(s.summed, 1)
    nc.scalar.activation(m.root[:, :], m.psum[:, 7, :], ACT.Sqrt, bias=m.const("eps"), scale=1.0 / D)\
        .then_inc(s.root, 1)
    for c in range(KC):
        act.wait_ge(s.scaled, c + 1)
        if shift is None:
            nc.scalar.activation(m.Hh[:, c, :], m.F[:, c % 4, :], ACT.Copy).then_inc(s.h_high, 1)
        else:
            nc.scalar.activation(m.Hh[:, c, :], m.F[:, c % 4, :], ACT.Identity, bias=shift[:, c:c + 1])
            nc.scalar.activation(m.F[:, c % 4, :], m.F[:, c % 4, :], ACT.Identity, bias=shift[:, c:c + 1])\
                .then_inc(s.h_high, 1)


def norm_pe(nc, pe, m, s):
    pe.wait_ge(s.added, KC - 1)
    nc.tensor.matmul(m.psum[:, 7, :], m.const("ones"), m.root[:, :], start=True, stop=True).then_inc(s.summed, 1)


def norm_dve(nc, dve, m, s, link, src, gain):
    for c in range(1, KC):
        dve.wait_ge(s.squared, c + 1)
        if c >= 2:
            dve.wait_ge(s.added, c - 1)
        nc.vector.tensor_tensor(m.root[:, :], m.F[:, 0, :] if c == 1 else m.root[:, :], m.F[:, c % 4, :], ALU.add)\
            .then_inc(s.added, 1)
    dve.wait_ge(s.root, 1)
    link(nc.vector.reciprocal(m.root[:, :], m.root[:, :]))
    for c in range(KC + 2):
        if c < KC:
            if c >= 4:
                dve.wait_ge(s.h_ready, c - 3)
            nc.vector.scalar_tensor_tensor(m.F[:, c % 4, :], src[:, c, :], gain[:, c:c + 1], m.root[:, :],
                                           ALU.mult, ALU.mult).then_inc(s.scaled, 1)
        if c >= 2:
            dve.wait_ge(s.h_high, c - 1)
            low_part(nc, m.Hl[:, c - 2, :], m.F[:, (c - 2) % 4, :], m.Hh[:, c - 2, :]).then_inc(s.h_ready, 1)


def h_tiles(pe, s):
    return lambda k: pe.wait_ge(s.h_ready, k + 1)


def low_part(nc, low, value, high):
    return nc.vector.tensor_tensor(low, value, high.bitcast(F32), ALU.subtract)


def phase_load(nc, m, ph, ring, d):
    with ExitStack() as ctx:
        block, s, stale = ph.open(ctx, "here", "v", "c_ready", "router_high", "mod_read",
                                  *[f"mod_loaded_{k}" for k in range(MOD_SLOTS)])
        pos = on_chip(nc, ctx, "positions", [P, S], I32)
        wr = on_chip(nc, ctx, "router_w", [P, DEPTH, KC, GROUPS + EXPERTS], F32)
        W = on_chip(nc, ctx, "mod_weights", [P, MOD_SLOTS, UNIT], F32)
        loaded = s[-MOD_SLOTS:]

        @block.sync
        def _(sp):
            sp.dma_start(m.c_act[:, :], d.c).then_inc(s.here, 16)
            sp.wait_ge(s.here, 16)
            for u in range(MOD_FIRST):
                if u >= MOD_SLOTS:
                    sp.wait_ge(s.mod_read, u - MOD_SLOTS + 1)
                sp.dma_start(W[:, u % MOD_SLOTS, :], d.ada_w[u, :, :]).then_inc(loaded[u % MOD_SLOTS], 16)
                if u == MOD_SLOTS - 1:
                    for dst, src in ((wr[:, :, :, :], d.router_w), (m.RB[:, :, :], d.router_b), (m.PT[:, :], d.params),
                                     (m.CT[:, :], d.consts), (pos[:, :], d.positions), (m.X[:, :, :], d.x)):
                        sp.dma_start(dst, src).then_inc(s.here, 16)
                    ring.stream(sp, None, 0, following=d.mla_w_down)
            sp.wait_ge(s.here, 112)

        @block.gpsimd
        def _(pool):
            for k in range(4):
                nc.gpsimd.memset(m.priority[:, :, k:k + 1], 4.0 - k)
            ring.make_lows(pool, 0)

        @block.vector
        def _(dve):
            dve.wait_ge(s.c_ready, 1)
            for u in range(MOD_FIRST):
                dve.wait_ge(loaded[u % MOD_SLOTS], 16 * (u // MOD_SLOTS + 1))
                modulation_unit(nc, m, W[:, u % MOD_SLOTS, :], m.mod, 2 * u).then_inc(s.mod_read, 1)
            link = Link(dve, s.v)
            dve.wait_ge(s.here, 112)
            dve.wait_ge(s.mod_read, MOD_FIRST)
            modulation_gains(nc, link, m, 0, 0, 2 * MOD_FIRST)
            nc.vector.tensor_copy(m.qn[:, 1, :], pos[:, :])
            dve.wait_ge(s.router_high, 1)
            nc.vector.tensor_tensor(m.WRl[:, :, :, :], wr[:, :, :, :], m.WRh[:, :, :, :].bitcast(F32), ALU.subtract)

        @block.scalar
        def _(act):
            act.wait_ge(s.here, 16)
            nc.scalar.activation(m.c_act[:, :], m.c_act[:, :], ACT.Silu).then_inc(s.c_ready, 1)
            act.wait_ge(s.here, 112)
            nc.scalar.activation(m.WRh[:, :, :, :], wr[:, :, :, :], ACT.Copy).then_inc(s.router_high, 1)
            ring.make_high(act, 0)


MOD_UNITS, MOD_SLOTS, MOD_TILES = 24, 4, 48
MOD_FIRST, MOD_HEADS = 8, 6
MOD_REST = MOD_UNITS - MOD_FIRST - MOD_HEADS


def modulation_unit(nc, m, w, out, t):
    for j in range(2):
        last = nc.vector.tensor_tensor_reduce(out=w[:, j * D:(j + 1) * D], in0=w[:, j * D:(j + 1) * D], in1=m.c_act[:, :],
                                              scale=1.0, scalar=0.0, op0=ALU.mult, op1=ALU.add,
                                              accum_out=out[:, t + j:t + j + 1])
    return last


def modulation_gains(nc, link, m, layer, first=0, end=MOD_TILES):
    at = MOD_TILES * layer
    part = m.mod[:, at + first:at + end]
    link(nc.vector.tensor_tensor(part, part, m.param("ada_b", end - first, at + first), ALU.add))
    for which, name, col in ((0, "norm_mix_g", KC), (1, "norm_ffn_g", 4 * KC)):
        if first <= col < end:
            nc.vector.scalar_tensor_tensor(m.gain[:, layer, which, :], m.mod[:, at + col:at + col + KC], 1.0,
                                           m.param(name, KC, layer * KC), ALU.add, ALU.mult)


BESIDE_SEMS = ("mod_read", "mod_loaded_0", "mod_loaded_1")


def load_beside(act, s, W, src, k):
    if k >= 2:
        act.wait_ge(s.mod_read, k - 1)
    act.dma_start(W[:, k % 2, :], src[k, :, :]).then_inc((s.mod_loaded_0, s.mod_loaded_1)[k % 2], 16)


def modulate_beside(nc, dve, m, s, W, k, tile):
    dve.wait_ge((s.mod_loaded_0, s.mod_loaded_1)[k % 2], 16 * (k // 2 + 1))
    modulation_unit(nc, m, W[:, k % 2, :], m.mod, tile).then_inc(s.mod_read, 1)


def phase_latents(nc, m, ph, ring, d, following):
    n = 2
    with ExitStack() as ctx:
        block, s, stale = ph.open(ctx, *NORM_SEMS, "v", "raw", "raw_sq", "sums", "roots", "rot_in", "rot_out",
                                  "normed", "lat_high", "tables", "tables_done",
                                  "angles_v")
        t0, t1, t2 = (m.qn[:, k, :] for k in range(3))

        @block.sync
        def _(sp):
            sp.sem_clear(stale)
            ring.stream(sp, d.mla_w_down, n, following)

        @block.scalar
        def _(act):
            norm_act(nc, act, m, s, m.X, shift=m.mod[:, 0:KC], ring=ring)
            ring.make_high(act, 2)
            for k, table in enumerate((m.sin, m.cos)):
                act.wait_ge(s.tables, k + 1)
                nc.scalar.activation(table[:, :], table[:, :], ACT.Sin).then_inc(s.tables_done, 1)
            ring.products(act, 1)
            nc.scalar.activation(m.lat[:, :, :], m.psum[:, 0:4, :], ACT.Copy).then_inc(s.raw, 1)
            act.wait_ge(s.raw, 1)
            nc.scalar.activation(m.sq4[:, :, :], m.psum[:, 0:4, :], ACT.Square).then_inc(s.raw_sq, 1)
            act.wait_ge(s.sums, 1)
            for b, width in ((0, Q_LORA), (1, KV_LORA), (2, ROPE)):
                nc.scalar.activation(m.r4[:, b, :], m.psum[:, 4 + b, :], ACT.Sqrt, bias=m.const("eps"),
                                     scale=1.0 / width).then_inc(s.roots, 1)
            act.wait_ge(s.normed, 1)
            nc.scalar.activation(m.lat_h[:, :, :], m.lat[:, 0:3, :], ACT.Copy).then_inc(s.lat_high, 1)

        @block.tensor
        def _(pe):
            norm_pe(nc, pe, m, s)
            unit_products(nc, pe, ring, 0, m.Hs, m.psum, k_ready=h_tiles(pe, s))
            unit_products(nc, pe, ring, 1, m.Hs, m.psum)
            pe.wait_ge(s.raw_sq, 1)
            nc.tensor.matmul(m.psum[:, 4, :], m.const("ones"), m.sq4[:, 0, :], start=True, stop=False)
            nc.tensor.matmul(m.psum[:, 4, :], m.const("ones"), m.sq4[:, 1, :], start=False, stop=True)
            nc.tensor.matmul(m.psum[:, 5, :], m.const("ones"), m.sq4[:, 2, :], start=True, stop=True)
            nc.tensor.matmul(m.psum[:, 6, :], m.const("ones64"), m.sq4[:, 3, :], start=True, stop=True)\
                .then_inc(s.sums, 1)
            pe.wait_ge(s.rot_in, 1)
            nc.tensor.matmul(m.psum[:, 0, :], m.const("rot"), m.lat[:, 3, :], start=True, stop=True)\
                .then_inc(s.rot_out, 1)

        @block.vector
        def _(dve):
            link = Link(dve, s.v)
            norm_dve(nc, dve, m, s, link, m.X, m.gain[:, 0, 0, :])
            angles = Link(dve, s.angles_v)
            angles(nc.vector.tensor_scalar(t0, t1, m.const("inv_freq"), None, ALU.mult))
            for table, quarter in ((m.sin, 0.0), (m.cos, math.pi / 2)):
                angles(nc.vector.tensor_scalar(t1, t0, 1.0 / (2 * math.pi), quarter / (2 * math.pi),
                                             ALU.mult, ALU.add))
                angles(nc.vector.tensor_scalar(t1, t1, ROUND_MAGIC, None, ALU.add))
                angles(nc.vector.tensor_scalar(t1, t1, ROUND_MAGIC, None, ALU.subtract))
                angles(nc.vector.scalar_tensor_tensor(t2, t1, -TWO_PI_A, t0, ALU.mult, ALU.add))
                if quarter:
                    angles(nc.vector.tensor_scalar(t2, t2, quarter, None, ALU.add))
                angles(nc.vector.scalar_tensor_tensor(t2, t1, -TWO_PI_B, t2, ALU.mult, ALU.add))
                angles(nc.vector.scalar_tensor_tensor(t2, t1, -TWO_PI_C, t2, ALU.mult, ALU.add))
                nc.vector.tensor_scalar(table[:, :], t2, PI_DOWN, -PI_DOWN, ALU.min, ALU.max)\
                    .then_inc(s.tables, 1)
            dve.wait_ge(s.roots, 3)
            link(nc.vector.reciprocal(m.r4[:, 0:3, :], m.r4[:, 0:3, :]))
            for t, root, g in ((0, 0, m.param("q_a_g", 1, 0)), (1, 0, m.param("q_a_g", 1, 1)),
                               (2, 1, m.param("kv_a_g", 1))):
                last = nc.vector.scalar_tensor_tensor(m.lat[:, t, :], m.lat[:, t, :], g, m.r4[:, root, :],
                                                      ALU.mult, ALU.mult)
            last.then_inc(s.normed, 1)
            nc.vector.scalar_tensor_tensor(m.lat[:, 3, :], m.lat[:, 3, :], m.param("k_pe_g", 1), m.r4[:, 2, :],
                                           ALU.mult, ALU.mult).then_inc(s.rot_in, 1)
            dve.wait_ge(s.rot_in, 1)
            dve.wait_ge(s.tables_done, 2)
            link(nc.vector.tensor_tensor(m.k_pe[:, :], m.lat[:, 3, :], m.cos[:, :], ALU.mult))
            dve.wait_ge(s.rot_out, 1)
            link(nc.vector.tensor_tensor(m.sq4[:, 0, :], m.psum[:, 0, :], m.sin[:, :], ALU.mult))
            nc.vector.tensor_tensor(m.k_pe[:, :], m.k_pe[:, :], m.sq4[:, 0, :], ALU.add)
            dve.wait_ge(s.lat_high, 1)
            low_part(nc, m.lat_l[:, :, :], m.lat[:, 0:3, :], m.lat_h[:, :, :])

        @block.gpsimd
        def _(pool):
            ring.make_lows(pool, n)
        ring.first += n


def phase_heads(nc, m, ph, ring, d, following):
    with ExitStack() as ctx:
        block, s, stale = ph.open(ctx, "raw", "copied", "sq", "sums", "roots", "inv", "spread", "normed", "v", "rot",
                                  "rotated", "vraw", "vcopied", "here", *BESIDE_SEMS)
        W = on_chip(nc, ctx, "mod_weights", [P, 2, UNIT], F32)
        mod_units = d.ada_w[MOD_FIRST:MOD_FIRST + MOD_HEADS, :, :]
        dest = [m.qn[:, 0:4, :], m.qn[:, 4:8, :], m.qp[:, :, :], m.kn[:, 0:4, :], m.kn[:, 4:8, :]]
        gains = ["q_nope_g", "q_nope_g", "q_pe_g", "k_nope_g", "k_nope_g"]
        PE_BATCH = 2
        rows = m.root[0:NORM_ROWS[-1], :]
        pe_rows = on_chip(nc, ctx, "pe_rows", [NORM_ROWS[-1], 4 * P], F32)
        order = (PE_BATCH, 0, 1, 3, 4)

        @block.sync
        def _(sp):
            sp.sem_clear(stale)
            sp.dma_start(pe_rows[:, :], d.pe_rows).then_inc(s.here, 16)
            ring.stream(sp, d.mla_w_heads, 3, following)
            sp.wait_ge(s.here, 16)

        @block.gpsimd
        def _(pool):
            ring.make_lows(pool, 3)

        @block.tensor
        def _(pe):
            def raw(b):
                if b in (0, 2, 3):
                    unit[:] = ring.parts(pe, {0: 0, 2: 1, 3: 2}[b])
                if b >= 1:
                    pe.wait_ge(s.copied, b)
                for j in range(4):
                    if b <= PE_BATCH:
                        col = (j if b == PE_BATCH else 4 * b + j) * P
                        for k in range(2):
                            mm = split_matmul(nc, m.psum[:, j, :], [w[:, k * D + col:k * D + col + P] for w in unit],
                                              [x[:, k, :] for x in (m.lat_h, m.lat_l)], k == 0, k == 1)
                    else:
                        col = (4 * (b - 3) + j) * P
                        mm = split_matmul(nc, m.psum[:, j, :], [w[:, col:col + P] for w in unit],
                                          [x[:, 2, :] for x in (m.lat_h, m.lat_l)], True, True)
                mm.then_inc(s.raw, 1)

            def sums(b):
                pe.wait_ge(s.sq, b + 1)
                for j in range(4):
                    pick = m.const("pick_two" if b == PE_BATCH else "pick_one")
                    end = NORM_ROWS[-1]
                    row = NORM_ROWS[b] + (2 * j if b == PE_BATCH else j)
                    mm = nc.tensor.matmul(m.psum[0:end, 7, :], pick[:, end - 1 - row:2 * end - 1 - row],
                                          m.sq8[:, b % 2, j, :], start=(b == 0 and j == 0), stop=(b == 4 and j == 3))
                    if j == 0 and b in (0, 1):
                        mm.then_inc(ring.used, 1)
                mm.then_inc(s.sums, 1)

            def values(half):
                for t in range(TT):
                    mm = split_matmul(nc, m.psum[:, t, :], [x[:, 2, t * P:(t + 1) * P] for x in (m.lat_h, m.lat_l)],
                                      [w[:, D + half * 512:D + half * 512 + 512] for w in unit], True, True)
                mm.then_inc(s.vraw, 1)

            def spread(b, bank):
                for j in range(4):
                    row = NORM_ROWS[b] + j
                    if b == PE_BATCH:
                        sel = pe_rows[:, j * P:(j + 1) * P]
                    else:
                        sel = m.const("ident")[0:NORM_ROWS[-1], row:row + 1].broadcast_to([NORM_ROWS[-1], P])
                    mm = nc.tensor.matmul(m.psum[:, bank + j, :], sel, rows, start=True, stop=True)
                    if b == 0 and j == 0:
                        mm.then_inc(ring.used, 1)
                mm.then_inc(s.spread, 1)

            unit = [None, None]
            raw(0)
            for b in range(5):
                if b < 4:
                    raw(b + 1)
                sums(b)
            pe.wait_ge(s.copied, 5)
            values(0)
            pe.wait_ge(s.inv, 1)
            pe.wait_ge(s.here, 16)
            spread(PE_BATCH, 4)
            pe.wait_ge(s.vcopied, 1)
            values(1)
            pe.wait_ge(s.normed, 1)
            spread(0, 4)
            pe.wait_ge(s.vcopied, 2)
            spread(1, 0)
            pe.wait_ge(s.normed, 2)
            for j in range(4):
                mm = nc.tensor.matmul(m.psum[:, 4 + j, :], m.const("rot"), m.qp[:, j, :], start=True, stop=True)
            mm.then_inc(s.rot, 1)
            pe.wait_ge(s.normed, 3)
            spread(3, 0)
            pe.wait_ge(s.rotated, 4)
            spread(4, 4)

        @block.scalar
        def _(act):
            ring.make_high(act, 1)
            for k in range(2):
                load_beside(act, s, W, mod_units, k)
            for b in range(5):
                act.wait_ge(s.copied, b + 1)
                if b >= 2:
                    act.wait_ge(s.sums, b - 1)
                nc.scalar.activation(m.sq8[:, b % 2, :, :], dest[b], ACT.Square).then_inc(s.sq, 1)
                if 2 <= b + 1 < MOD_HEADS:
                    load_beside(act, s, W, mod_units, b + 1)
                if b in (1, 2):
                    ring.make_high(act, b + 1)
            act.wait_ge(s.sums, 5)
            nc.scalar.activation(rows, m.psum[0:NORM_ROWS[-1], 7, :], ACT.Sqrt,
                                 bias=m.const("eps")[0:NORM_ROWS[-1], :]).then_inc(s.roots, 1)
            for half in range(2):
                act.wait_ge(s.vraw, half + 1)
                nc.scalar.activation(m.vt[:, :, half * 512:half * 512 + 512], m.psum[:, 0:4, :],
                                     ACT.Copy).then_inc(s.vcopied, 1)

        @block.vector
        def _(dve):
            link = Link(dve, s.v)
            modulate_beside(nc, dve, m, s, W, 0, 2 * MOD_FIRST)
            for b in range(5):
                dve.wait_ge(s.raw, b + 1)
                nc.vector.tensor_copy(dest[b], m.psum[:, 0:4, :]).then_inc(s.copied, 1)
                if b + 1 < MOD_HEADS:
                    modulate_beside(nc, dve, m, s, W, b + 1, 2 * (MOD_FIRST + b + 1))
            dve.wait_ge(s.mod_read, MOD_HEADS)
            modulation_gains(nc, link, m, 0, 2 * KC, 3 * KC)
            dve.wait_ge(s.roots, 1)
            nc.vector.reciprocal(rows, rows).then_inc(s.inv, 1)
            dve.wait_ge(s.copied, 5)
            for n, b in enumerate(order):
                dve.wait_ge(s.spread, n + 1)
                bank = (4, 4, 0, 0, 4)[n]
                nc.vector.scalar_tensor_tensor(flat(dest[b]), flat(dest[b]), m.param(gains[b], 1),
                                               flat(m.psum[:, bank:bank + 4, :]), ALU.mult, ALU.mult).then_inc(s.normed, 1)
                if n == 2:
                    dve.wait_ge(s.normed, 1)
                    dve.wait_ge(s.rot, 1)
                    for j in range(4):
                        nc.vector.tensor_tensor(m.sq8[:, 0, j, :], m.psum[:, 4 + j, :], m.sin[:, :], ALU.mult)\
                            .then_inc(s.rotated, 1)
                        link(nc.vector.tensor_tensor(m.qp[:, j, :], m.qp[:, j, :], m.cos[:, :], ALU.mult))
                    dve.wait_ge(s.rotated, 4)
                    nc.vector.tensor_tensor(m.qp[:, :, :], m.qp[:, :, :], m.sq8[:, 0, :, :], ALU.add)
        ring.first += 3


def phase_attention(nc, m, ph, ring, d):
    scale = QK_HEAD ** -0.5
    steps = HEADS * TT
    with ExitStack() as ctx:
        block, s, stale = ph.open(ctx, "scores", "v", "neg", "exped", "rsum", "probs", "flipped", "pt_ready", "pv", "out_high", "out_low")
        E = on_chip(nc, ctx, "probs", [P, 3, S], F32)
        pt = on_chip(nc, ctx, "probs_t", [P, 2, TT, S], F32)
        top = on_chip(nc, ctx, "top", [P, steps], F32)
        neg = on_chip(nc, ctx, "neg", [P, steps], F32)
        tot = on_chip(nc, ctx, "tot", [P, steps], F32)
        inv = on_chip(nc, ctx, "inv", [P, steps], F32)

        @block.sync
        def _(sp):
            sp.sem_clear(stale)

        @block.tensor
        def _(pe):
            def scores(i):
                h, q = divmod(i, TT)
                if i >= 3:
                    pe.wait_ge(s.exped, i - 2)
                half = ROPE * (h % 2)
                nc.tensor.matmul(m.psum[:, i % 3, :], m.qn[:, h, q * P:(q + 1) * P], m.kn[:, h, :],
                                 start=True, stop=False)
                nc.tensor.matmul(m.psum[:, i % 3, :], m.qp[half:half + ROPE, h // 2, q * P:(q + 1) * P],
                                 m.k_pe[half:half + ROPE, :], start=False, stop=True).then_inc(s.scores, 1)

            def flip(i):
                pe.wait_ge(s.probs, i + 1)
                if i >= 2:
                    pe.wait_ge(s.pt_ready, i - 1)
                for kt in range(TT):
                    mm = nc.tensor.transpose(m.psum[:, 3 + i % 2, kt * P:(kt + 1) * P],
                                             E[:, i % 3, kt * P:(kt + 1) * P], m.const("ident"))
                mm.then_inc(s.flipped, 1)

            def values(h):
                pe.wait_ge(s.pt_ready, TT * (h + 1))
                if h >= 2:
                    pe.wait_ge(s.out_low, h - 1)
                for kt in range(TT):
                    mm = nc.tensor.matmul(m.psum[:, 5 + h % 2, :], m.vt[:, kt, h * P:(h + 1) * P],
                                          pt[:, h % 2, kt, :], start=(kt == 0), stop=(kt == TT - 1))
                mm.then_inc(s.pv, 1)

            for i in range(steps + 3):
                if i < steps:
                    scores(i)
                if 2 <= i < steps + 2:
                    flip(i - 2)
                if i >= 6 and (i - 6) % TT == 0:
                    values((i - 6) // TT)

        @block.vector
        def _(dve):
            link = Link(dve, s.v)

            def out(h):
                dve.wait_ge(s.out_high, h + 1)
                low_part(nc, m.Hl[:, h, :], m.psum[:, 5 + h % 2, :], m.Hh[:, h, :]).then_inc(s.out_low, 1)

            for i in range(steps + 2):
                if i < steps:
                    dve.wait_ge(s.scores, i + 1)
                    link(nc.vector.tensor_reduce(top[:, i:i + 1], m.psum[:, i % 3, :], AX.X, ALU.max))
                    nc.vector.tensor_scalar(neg[:, i:i + 1], top[:, i:i + 1], -scale, None, ALU.mult).then_inc(s.neg, 1)
                if 1 <= i <= steps:
                    dve.wait_ge(s.exped, i)
                    nc.vector.reciprocal(inv[:, i - 1:i], tot[:, i - 1:i]).then_inc(s.rsum, 1)
                if i >= 2:
                    j = i - 2
                    h, q = divmod(j, TT)
                    dve.wait_ge(s.flipped, j + 1)
                    if h >= 2:
                        dve.wait_ge(s.pv, h - 1)
                    nc.vector.tensor_copy(pt[:, h % 2, :, q * P:(q + 1) * P],
                                          m.psum[:, 3 + j % 2, :].rearrange("p (k n) -> p k n", k=TT)).then_inc(s.pt_ready, 1)
                if i >= 9 and (i - 9) % TT == 0:
                    out((i - 9) // TT)
            out(HEADS - 1)

        @block.scalar
        def _(act):
            def out(h):
                act.wait_ge(s.pv, h + 1)
                nc.scalar.activation(m.Hh[:, h, :], m.psum[:, 5 + h % 2, :], ACT.Copy).then_inc(s.out_high, 1)

            for i in range(steps + 1):
                if i < steps:
                    act.wait_ge(s.neg, i + 1)
                    if i >= 3:
                        act.wait_ge(s.flipped, i - 2)
                    nc.scalar.activation(E[:, i % 3, :], m.psum[:, i % 3, :], ACT.Exp, bias=neg[:, i:i + 1],
                                         scale=scale, accum_out=tot[:, i:i + 1]).then_inc(s.exped, 1)
                if i >= 1:
                    act.wait_ge(s.rsum, i)
                    nc.scalar.activation(E[:, (i - 1) % 3, :], E[:, (i - 1) % 3, :], ACT.Copy,
                                         scale=inv[:, i - 1:i]).then_inc(s.probs, 1)
                if i >= 8 and (i - 8) % TT == 0:
                    out((i - 8) // TT)
            out(HEADS - 1)


def phase_residual(nc, m, ph, ring, w, gate, following, z=None, mod_units=None):
    n = 4
    with ExitStack() as ctx:
        block, s, stale = ph.open(ctx, "read_out", "h_high", "h_ready", "v", *BESIDE_SEMS)
        if mod_units is not None:
            W = on_chip(nc, ctx, "mod_weights", [P, 2, UNIT], F32)

        @block.sync
        def _(sp):
            sp.sem_clear(stale)
            ring.stream(sp, w, n, following)

        @block.gpsimd
        def _(pool):
            ring.make_lows(pool, n, following is not None)

        @block.tensor
        def _(pe):
            streamed_products(nc, pe, ring, n, m.Hs, m.psum, s.read_out, k_ready=None if z is None else h_tiles(pe, s))

        @block.scalar
        def _(act):
            if z is not None:
                for c in range(KC):
                    nc.scalar.activation(m.Hh[:, c, :], z[:, c, :], ACT.Copy).then_inc(s.h_high, 1)
            ring.make_high(act, 1)
            if mod_units is not None:
                for k in range(2):
                    load_beside(act, s, W, mod_units, k)
            for u in range(n):
                if mod_units is not None:
                    for k in (2 * u + 2, 2 * u + 3):
                        load_beside(act, s, W, mod_units, k)
                if u < n - 1:
                    ring.make_high(act, u + 2)

        @block.vector
        def _(dve):
            def modulate(k):
                if mod_units is not None:
                    modulate_beside(nc, dve, m, s, W, k, MOD_TILES - 2 * MOD_REST + 2 * k)

            for k in range(2):
                modulate(k)
            if z is not None:
                for c in range(KC):
                    dve.wait_ge(s.h_high, c + 1)
                    low_part(nc, m.Hl[:, c, :], z[:, c, :], m.Hh[:, c, :]).then_inc(s.h_ready, 1)
            for u in range(n):
                ring.products(dve, u)
                for j in range(2):
                    t = 2 * u + j
                    x, y = m.X[:, t, :], m.psum[:, t, :]
                    if z is not None:
                        x = x.rearrange("p (n two) -> p two n", two=2)
                        y = y.rearrange("p (two n) -> p two n", two=2)
                    nc.vector.scalar_tensor_tensor(x, y, gate[:, t:t + 1], x, ALU.mult, ALU.add)
                for k in (2 * u + 2, 2 * u + 3):
                    modulate(k)
            if mod_units is not None:
                dve.wait_ge(s.mod_read, MOD_REST)
                modulation_gains(nc, Link(dve, s.v), m, 0, 3 * KC, MOD_TILES)
        ring.first += n


def phase_moe(nc, m, ph, ring, layer, shift, gain, w, gate, following, modulation=None):
    per = 3 * PER_GROUP
    extra = MOD_UNITS // GROUPS
    with ExitStack() as ctx:
        block, s, stale = ph.open(ctx, *NORM_SEMS, "logits", "v", "m1", "e1", "m2", "e2", "diag", "spread", "spread_read",
                                  "gates_out", "ups_out", "weighted", "a_high", "a_ready", "downs_out", "gains_v",
                                  "mod_read", "mod_kept", "mod_loaded_0", "mod_loaded_1")
        L = on_chip(nc, ctx, "logits", [P, TT, GROUPS + EXPERTS], F32)
        G = on_chip(nc, ctx, "group", [P, 4, TT, GROUPS], F32)
        C = on_chip(nc, ctx, "column", [P, 6, TT], F32)
        EL = on_chip(nc, ctx, "chosen", [P, 4, TT, PER_GROUP], F32)
        T16 = on_chip(nc, ctx, "masked", [P, 2, TT, GROUPS, PER_GROUP], F32)
        T = on_chip(nc, ctx, "diagonals_then_silu", [P, 2, 2, S], F32)
        dg = T[:, :, :, :].rearrange("p a b (t n) -> p (a b) t n", t=TT)
        Ah = on_chip(nc, ctx, "acts_high", [P, 2 * PER_GROUP, S], F32R)
        Al = on_chip(nc, ctx, "acts_low", [P, 2 * PER_GROUP, S], F32R)
        if modulation is None:
            m.F = on_chip(nc, ctx, "norm_tiles", [P, 4, S], F32)
        else:
            W = on_chip(nc, ctx, "mod_weights", [P, 2, UNIT], F32)
            m.F = W[:, 1, :].rearrange("p (c n) -> p c n", c=4)
            sums = on_chip(nc, ctx, "mod_sums", [P, 2 * extra], F32)
            mod_loaded = (s.mod_loaded_0, s.mod_loaded_1)

        def wide(col, n=4):
            return col.unsqueeze(2).broadcast_to([P, TT, n])

        @block.sync
        def _(sp):
            sp.sem_clear(stale)
            ring.stream(sp, w, per * GROUPS, following)

        @block.gpsimd
        def _(pool):
            ring.make_lows(pool, per * GROUPS, following is not None)

        @block.scalar
        def _(act):
            norm_act(nc, act, m, s, m.X, shift=shift, ring=ring)
            act.wait_ge(s.m1, 1)
            nc.scalar.activation(G[:, 1, :, :], G[:, 1, :, :], ACT.Exp).then_inc(s.e1, 1)
            act.wait_ge(s.m2, 1)
            nc.scalar.activation(EL[:, 1, :, :], EL[:, 1, :, :], ACT.Exp).then_inc(s.e2, 1)
            ring.make_high(act, 2)
            for e in range(EXPERTS):
                act.wait_ge(s.spread, e + 1)
                nc.scalar.activation(m.cb[:, e, :], m.psum[:, 4 + e % 4, :], ACT.Copy).then_inc(s.spread_read, 1)
            if modulation is not None:
                act.sem_inc(s.mod_read, 2)

            def group(g, o):
                def load_modulation(k):
                    if modulation is None:
                        return
                    act.wait_ge(s.mod_read, g * extra + (extra * o + k + 1))
                    unit = extra * o + k
                    src = modulation[bass.ds(g * extra + unit, 1), :, :].rearrange("a p n -> (a p) n") if o \
                        else modulation[unit, :, :]
                    act.dma_start(W[:, k % 2, :], src).then_inc(mod_loaded[k % 2], 16)

                if o:
                    ring.make_high(act, per * o + 1, g, per)
                for j in range(PER_GROUP):
                    load_modulation(j)
                    ring.products(act, per * o + 2 * j, g, per)
                    if j >= 2:
                        act.wait_ge(s.a_ready, g * 4 + (4 * o + j - 1))
                    b = 4 * j % BANKS
                    nc.scalar.activation(T[:, j % 2, :, :], m.psum[:, b:b + 2, :], ACT.Silu).then_inc(s.gates_out, 1)
                    if o or j:
                        ring.make_high(act, per * o + 2 * j + 2, g, per)
                    act.wait_ge(s.weighted, g * 4 + (4 * o + j + 1))
                    nc.scalar.activation(Ah[:, 2 * j:2 * j + 2, :], T[:, j % 2, :, :], ACT.Copy).then_inc(s.a_high, 1)
                    ring.make_high(act, per * o + 2 * j + 3, g, per)
                for u in range(8, per):
                    if u < per - 1:
                        ring.make_high(act, per * o + u + 2, g, per)
                    if u in (8, 10):
                        load_modulation(u // 2)

            group(0, 0)
            with act.Fori(0, GROUPS - 1) as g:
                group(g, 1)

        @block.tensor
        def _(pe):
            norm_pe(nc, pe, m, s)
            for k in range(KC):
                pe.wait_ge(s.h_ready, k + 1)
                for t in range(TT):
                    mm = split_matmul(nc, m.psum[:, 4 + t, 0:GROUPS + EXPERTS],
                                      [x[:, k, t * P:(t + 1) * P] for x in m.Hs],
                                      [x[:, layer, k, :] for x in (m.WRh, m.WRl)], k == 0, k == KC - 1)
            mm.then_inc(s.logits, 1)

            def spread_weights():
                for e in range(EXPERTS):
                    pe.wait_ge(s.diag, e + 1)
                    if e >= 4:
                        pe.wait_ge(s.spread_read, e - 3)
                    nc.tensor.matmul(m.psum[:, 4 + e % 4, :], m.const("ones"), dg[:, e % 4, :, :].rearrange("p t n -> p (t n)"),
                                     start=True, stop=True).then_inc(s.spread, 1)
                pe.wait_ge(s.spread_read, EXPERTS)

            pe.sem_inc(s.downs_out, 4)

            def group(g, o):
                for u in range(per):
                    if u < 4:
                        pe.wait_ge(s.downs_out, g * 4 + (4 * o + u + 1))
                    elif u % 2 == 0:
                        pe.wait_ge(s.gates_out, g * 4 + (4 * o + u // 2 - 1))
                    else:
                        pe.wait_ge(s.ups_out, g * 4 + (4 * o + u // 2 - 1))
                    unit_products(nc, pe, ring, per * o + u, m.Hs if u < 8 else (Ah, Al), m.psum, turn=g, per=per,
                                  k_ready=(lambda k: pe.wait_ge(s.a_ready, g * 4 + (4 * o + k // 2 + 1))) if u == 8 else None)
                    if u == 1 and not o:
                        spread_weights()

            group(0, 0)
            with pe.Fori(0, GROUPS - 1) as g:
                group(g, 1)

        @block.vector
        def _(dve):
            link = Link(dve, s.v)
            tt, red = nc.vector.tensor_tensor, nc.vector.tensor_reduce
            norm_dve(nc, dve, m, s, link, m.X, gain)

            def first_of(out, values, largest, scratch):
                link(tt(scratch, values, wide(largest), ALU.is_equal))
                link(tt(scratch, scratch, m.priority[:, :, :], ALU.mult))
                link(red(C[:, 5, :], scratch, AX.X, ALU.max))
                link(tt(out, scratch, wide(C[:, 5, :]), ALU.is_equal))

            dve.wait_ge(s.logits, 1)
            link(tt(L[:, :, :], m.psum[:, 4:8, 0:GROUPS + EXPERTS],
                    m.RB[:, layer, :].unsqueeze(1).broadcast_to([P, TT, 20]), ALU.add))
            lg = L[:, :, 0:GROUPS]
            le = L[:, :, GROUPS:].rearrange("p t (g e) -> p t g e", g=GROUPS)
            link(red(C[:, 0, :], lg, AX.X, ALU.max))
            tt(G[:, 1, :, :], lg, wide(C[:, 0, :]), ALU.subtract).then_inc(s.m1, 1)
            dve.wait_ge(s.e1, 1)
            link(red(C[:, 1, :], G[:, 1, :, :], AX.X, ALU.add))
            link(nc.vector.reciprocal(C[:, 1, :], C[:, 1, :]))
            link(tt(G[:, 1, :, :], G[:, 1, :, :], wide(C[:, 1, :]), ALU.mult))
            link(red(C[:, 2, :], G[:, 1, :, :], AX.X, ALU.max))
            first_of(G[:, 2, :, :], G[:, 1, :, :], C[:, 2, :], G[:, 3, :, :])
            chosen_g = G[:, 2, :, :]
            for t in range(TT):
                link(tt(T16[:, 0, t, :, :], le[:, t, :, :], chosen_g[:, t, :].unsqueeze(2).broadcast_to([P, GROUPS, PER_GROUP]),
                        ALU.mult))
            for t in range(TT):
                link(red(EL[:, 0, t, :], T16[:, 0, t, :, :].rearrange("p g e -> p e g"), AX.X, ALU.add))
            link(red(C[:, 0, :], EL[:, 0, :, :], AX.X, ALU.max))
            tt(EL[:, 1, :, :], EL[:, 0, :, :], wide(C[:, 0, :]), ALU.subtract).then_inc(s.m2, 1)
            dve.wait_ge(s.e2, 1)
            link(red(C[:, 0, :], EL[:, 1, :, :], AX.X, ALU.add))
            link(nc.vector.reciprocal(C[:, 0, :], C[:, 0, :]))
            link(tt(EL[:, 1, :, :], EL[:, 1, :, :], wide(C[:, 0, :]), ALU.mult))
            link(red(C[:, 0, :], EL[:, 1, :, :], AX.X, ALU.max))
            first_of(EL[:, 2, :, :], EL[:, 1, :, :], C[:, 0, :], EL[:, 0, :, :])
            link(nc.vector.scalar_tensor_tensor(EL[:, 0, :, :], EL[:, 2, :, :], -2.0, EL[:, 1, :, :], ALU.mult, ALU.add))
            link(red(C[:, 1, :], EL[:, 0, :, :], AX.X, ALU.max))
            first_of(EL[:, 3, :, :], EL[:, 0, :, :], C[:, 1, :], EL[:, 1, :, :])
            link(tt(C[:, 3, :], C[:, 0, :], C[:, 1, :], ALU.add))
            link(nc.vector.reciprocal(C[:, 3, :], C[:, 3, :]))
            link(tt(C[:, 3, :], C[:, 3, :], C[:, 2, :], ALU.mult))
            link(tt(C[:, 0, :], C[:, 0, :], C[:, 3, :], ALU.mult))
            link(tt(C[:, 1, :], C[:, 1, :], C[:, 3, :], ALU.mult))
            link(tt(EL[:, 2, :, :], EL[:, 2, :, :], wide(C[:, 0, :]), ALU.mult))
            link(tt(EL[:, 3, :, :], EL[:, 3, :, :], wide(C[:, 1, :]), ALU.mult))
            link(tt(EL[:, 2, :, :], EL[:, 2, :, :], EL[:, 3, :, :], ALU.add))
            for t in range(TT):
                link(tt(T16[:, 1, t, :, :], chosen_g[:, t, :].unsqueeze(2).broadcast_to([P, GROUPS, PER_GROUP]),
                        EL[:, 2, t, :].unsqueeze(1).broadcast_to([P, GROUPS, PER_GROUP]), ALU.mult))
            for e in range(EXPERTS):
                if e >= 4:
                    dve.wait_ge(s.spread, e - 3)
                w = T16[:, 1, :, e // PER_GROUP, e % PER_GROUP]
                tt(dg[:, e % 4, :, :], m.const("ident").unsqueeze(1).broadcast_to([P, TT, P]), wide(w, P), ALU.mult)\
                    .then_inc(s.diag, 1)
            dve.wait_ge(s.spread_read, EXPERTS)
            if modulation is not None:
                dve.sem_inc(s.mod_kept, 1)
            with dve.Fori(0, GROUPS) as g:
                def modulate(k):
                    if modulation is None:
                        return
                    dve.wait_ge(mod_loaded[k % 2], g * (8 * extra) + 16 * (k // 2 + 1))
                    if k == 0:
                        dve.wait_ge(s.mod_kept, g + 1)
                    modulation_unit(nc, m, W[:, k % 2, :], sums, 2 * k).then_inc(s.mod_read, 1)

                for j in range(PER_GROUP):
                    ring.products(dve, 2 * j + 1, g, per)
                    dve.wait_ge(s.gates_out, g * 4 + (j + 1))
                    b = (4 * j + 2) % BANKS
                    t = T[:, j % 2, :, :]
                    mm = nc.vector.tensor_tensor(t, t, m.psum[:, b:b + 2, :], ALU.mult)
                    mm.then_inc(s.ups_out, 1)
                    dve.wait_ge(s.ups_out, g * 4 + (j + 1))
                    nc.vector.tensor_tensor(t, t, m.cb[:, bass.ds(g * PER_GROUP + j, 1), :].broadcast_to([P, 2, S]),
                                            ALU.mult).then_inc(s.weighted, 1)
                    dve.wait_ge(s.a_high, g * 4 + (j + 1))
                    low_part(nc, Al[:, 2 * j:2 * j + 2, :], t, Ah[:, 2 * j:2 * j + 2, :]).then_inc(s.a_ready, 1)
                    if j < 3:
                        modulate(j)
                for u in range(4):
                    ring.products(dve, 8 + u, g, per)
                    for j in range(2):
                        t = 2 * u + j
                        last = nc.vector.scalar_tensor_tensor(m.X[:, t, :], m.psum[:, t, :], gate[:, t:t + 1],
                                                              m.X[:, t, :], ALU.mult, ALU.add)
                    last.then_inc(s.downs_out, 1)
                    if u < 3:
                        modulate(3 + u)
                if modulation is not None:
                    dve.wait_ge(s.mod_read, g * extra + (extra + 2))
                    nc.vector.tensor_copy(m.mod[:, bass.ds(g * (2 * extra) + MOD_TILES, 2 * extra)],
                                          sums[:, :]).then_inc(s.mod_kept, 1)
            if modulation is not None:
                dve.wait_ge(s.mod_kept, GROUPS + 1)
                modulation_gains(nc, Link(dve, s.gains_v), m, 1)
        ring.first += per * GROUPS


def phase_hyena_in(nc, m, ph, ring, d, following):
    n = 12
    with ExitStack() as ctx:
        block, s, stale = ph.open(ctx, *NORM_SEMS, "v", "read_out", "conv", "pads", "here", "tables", "fv",
                                  "layer_sum", "arg", "sine")
        zT = on_chip(nc, ctx, "zT", [FILTER_EMB, S], F32)
        w1 = on_chip(nc, ctx, "w1", [FILTER_EMB, FILTER_WIDTH], F32)
        w23 = on_chip(nc, ctx, "w23", [FILTER_WIDTH, 2, FILTER_WIDTH], F32)
        a = on_chip(nc, ctx, "arg", [FILTER_WIDTH, S], F32)
        whole = on_chip(nc, ctx, "whole", [FILTER_WIDTH, S], F32)
        U = on_chip(nc, ctx, "padded", [P, 2, 2, S + 2], F32)
        W = on_chip(nc, ctx, "conv", [P, 2, S], F32)

        @block.sync
        def _(sp):
            sp.sem_clear(stale)
            for dst, src in ((zT[:, :], d.zT), (w1[:, :], d.hy_f_w1), (w23[:, 0, :], d.hy_f_w2), (w23[:, 1, :], d.hy_f_w3)):
                sp.dma_start(dst, src).then_inc(s.here, 16)
            sp.dma_start(m.fwd[:, :, :, :], d.dft_fwd).then_inc(s.tables, 16)
            sp.dma_start(m.inv[:, :, :, :], d.dft_inv).then_inc(s.tables, 16)
            ring.stream(sp, d.hy_w_in, n, following)
            sp.wait_ge(s.tables, 32)

        @block.gpsimd
        def _(pool):
            nc.gpsimd.memset(U[:, :, :, :], 0.0).then_inc(s.pads, 1)
            ring.make_lows(pool, n)

        @block.tensor
        def _(pe):
            norm_pe(nc, pe, m, s)
            pe.wait_ge(s.here, 64)
            nc.tensor.matmul(m.psum[0:FILTER_WIDTH, 6, :], w1[:, :], zT[:, :], start=True, stop=True)\
                .then_inc(s.layer_sum, 1)
            pe.wait_ge(s.root, 1)

            def filter_layer(u):
                if u < 2:
                    pe.wait_ge(s.sine, u + 1)
                    nc.tensor.matmul(m.psum[0:FILTER_WIDTH, 6, :], w23[:, u, :], m.hdn[:, :], start=True, stop=True)\
                        .then_inc(s.layer_sum, 1)
                if u == 2:
                    pe.wait_ge(s.arg, 3)
            streamed_products(nc, pe, ring, n, m.Hs, m.psum, s.read_out, k_ready=h_tiles(pe, s), after=filter_layer)

        @block.scalar
        def _(act):
            norm_act(nc, act, m, s, m.X, shift=m.mod[:, 48:48 + KC], ring=ring)
            act.wait_ge(s.pads, 1)
            act.sem_inc(s.conv, 4)

            def body(u, turn):
                ring.products(act, u, turn)
                act.wait_ge(s.conv, turn * 8 + (2 * u + 2))
                for j in range(2):
                    b = (2 * u + j) % BANKS
                    last = nc.scalar.activation(
                        U[:, u % 2, j, 1:S + 1], m.psum[:, b, :], ACT.Identity,
                        bias=m.PT[:, bass.ds(turn * 8 + (PCOL["hy_b_in"] + 2 * u + j), 1)])
                last.then_inc(s.read_out, 1)
                if u < n - 1:
                    ring.make_high(act, u + 2, turn)

            def sine(layer):
                act.wait_ge(s.arg, layer + 1)
                nc.scalar.activation(m.hdn[:, :], a[:, :], ACT.Sin).then_inc(s.sine, 1)

            sine(0)
            over_units(act, n, body, first=2, after=lambda u: sine(u + 1))

        @block.vector
        def _(dve):
            def argument(layer):
                filters = Link(dve, s.fv, 6 * layer)
                dve.wait_ge(s.layer_sum, layer + 1)
                filters(nc.vector.tensor_scalar(a[:, :], m.psum[0:FILTER_WIDTH, 6, :], m.param("hy_fb", 1, layer)[0:FILTER_WIDTH, :],
                                                m.param("hy_ff", 1, layer)[0:FILTER_WIDTH, :], ALU.add, ALU.mult))
                filters(nc.vector.tensor_scalar(whole[:, :], a[:, :], 1.0 / (2 * math.pi), ROUND_MAGIC, ALU.mult, ALU.add))
                filters(nc.vector.tensor_scalar(whole[:, :], whole[:, :], ROUND_MAGIC, None, ALU.subtract))
                for part in (TWO_PI_A, TWO_PI_B, TWO_PI_C):
                    filters(nc.vector.scalar_tensor_tensor(a[:, :], whole[:, :], -part, a[:, :], ALU.mult, ALU.add))
                nc.vector.tensor_scalar(a[:, :], a[:, :], PI_DOWN, -PI_DOWN, ALU.min, ALU.max).then_inc(s.arg, 1)

            link = Link(dve, s.v)
            norm_dve(nc, dve, m, s, link, m.X, m.gain[:, 1, 0, :])
            argument(0)
            base = link.n

            def col(name, k):
                return m.PT[:, bass.ds(k + PCOL[name], 1)]

            def body(u, turn):
                dve.wait_ge(s.read_out, turn * TURN + (u + 1))
                chain = Link(dve, s.v, turn * 16 + (base + 4 * u))
                for j in range(2):
                    t = turn * 8 + (2 * u + j)
                    src = U[:, u % 2, j, :]
                    chain(nc.vector.tensor_scalar(W[:, j, :], src[:, 1:S + 1], col("hy_conv_w", t + 24),
                                                  col("hy_conv_b", t), ALU.mult, ALU.add))
                    chain(nc.vector.scalar_tensor_tensor(W[:, j, :], src[:, 0:S], col("hy_conv_w", t), W[:, j, :],
                                                         ALU.mult, ALU.add))
                    out = m.xv[:, bass.ds(t, 1), :].rearrange("p a (two n) -> p n (a two)", two=2)
                    nc.vector.scalar_tensor_tensor(
                        out, src[:, 2:S + 2].rearrange("p (n two) -> p n two", two=2), col("hy_conv_w", t + 48),
                        W[:, j, :].rearrange("p (n two) -> p n two", two=2), ALU.mult, ALU.add).then_inc(s.conv, 1)

            over_units(dve, n, body, first=2, after=lambda u: argument(u + 1))
        ring.first += n


def phase_long_convs(nc, m, ph, ring, d):
    N = 256
    per_order = D // N
    chunks = 2 * per_order
    with ExitStack() as ctx:
        block, s, stale = ph.open(ctx, "decay_0", "decay_1", "w4_0", "w4_1", "raw", "decayed", "absed", "added", "norms",
                                  "norms_out", "v", "ab", "z_flip", "z_out", "k_sums", "k_odd", "k_done", "u_sums",
                                  "u_odd", "u_done", "pairs", "inverse", "gated")

        def pair(name, shape):
            return [on_chip(nc, ctx, f"{name}_{b}", shape, F32) for b in range(2)]

        Fs, As = pair("filters_then_u", [P, 2, TT, N]), pair("ab_then_y", [P, 2, TT, N])
        Ks, Os = pair("k_spectrum", [P, 2, TT, N]), pair("decay_then_odd", [P, TT, N])
        vts = pair("z_token_major", [P, TT, N])
        slots = [m.psum[:, 4 * b:4 * b + 4, :].rearrange("p k (h n) -> p (k h) n", h=2) for b in range(2)]
        w4s = [K[0:FILTER_WIDTH, 0, 0:2, :] for K in Ks]
        rns, addeds = [K[:, 1, 0:2, :] for K in Ks], [K[:, 1, 2:4, :] for K in Ks]
        w4_here, decay_here = (s.w4_0, s.w4_1), (s.decay_0, s.decay_1)

        @block.sync
        def _(sp):
            sp.sem_clear(stale)
            for i in range(chunks):
                order, part = divmod(i, per_order)
                cols = slice(part * N, part * N + N)
                if i >= 2:
                    sp.wait_ge(s.pairs, 2 * (i - 1))
                sp.dma_start(w4s[i % 2], d.hy_f_w4[:, order, :, cols]).then_inc(w4_here[i % 2], 16)
                if i >= 2:
                    sp.wait_ge(s.gated, i - 1)
                sp.dma_start(Os[i % 2][:, :, :], d.decay[:, :, cols]).then_inc(decay_here[i % 2], 16)

        @block.tensor
        def _(pe):
            def filters(i):
                b, part = i % 2, i % per_order
                if i >= 2:
                    pe.wait_ge(s.gated, i - 1)
                pe.wait_ge(w4_here[b], 16 * (i // 2 + 1))
                for x in range(2):
                    for j in range(TT):
                        mm = nc.tensor.matmul(slots[b][:, 4 * x + j, :], m.hdn[:, j * P:(j + 1) * P], w4s[b][:, x, :],
                                              start=True, stop=True)
                    mm.then_inc(s.raw, 1)
                pe.wait_ge(s.decayed, 2 * i + 1)
                if i >= per_order:
                    pe.wait_ge(s.gated, i - per_order + 1)
                for j in range(TT):
                    for c in range(2):
                        mm = nc.tensor.transpose(slots[b][:, j, c * P:(c + 1) * P],
                                                 m.xv[:, 16 + 2 * part + c, j * P:(j + 1) * P], m.const("ident"))
                mm.then_inc(s.z_flip, 1)
                for x in range(2):
                    pe.wait_ge(s.added, 2 * i + x + 1)
                    nc.tensor.matmul(slots[b][:, 4 + x, :], m.const("ones"), addeds[b][:, x, :],
                                     start=True, stop=True).then_inc(s.norms, 1)

            def transform(i, src_cos, src_sin, done):
                for which, src in ((0, src_cos), (1, src_sin)):
                    for parity in range(2):
                        for kt in range(2):
                            for c in range(2):
                                j = 2 * parity + c
                                mm = nc.tensor.matmul(slots[i % 2][:, 4 * parity + 2 * which + kt, :],
                                                      m.fwd[:, which, j, kt * P:(kt + 1) * P], src[:, j, :],
                                                      start=(c == 0), stop=(c == 1))
                    mm.then_inc(done, 1)

            def z_spectrum(i):
                pe.wait_ge(s.z_out, i + 1)
                pe.wait_ge(s.norms_out, i + 1)
                transform(i, vts[i % 2], vts[i % 2], s.u_sums)

            def filter_spectrum(i):
                pe.wait_ge(s.ab, i + 1)
                pe.wait_ge(s.u_done, 2 * i + 2)
                transform(i, As[i % 2][:, 0, :, :], As[i % 2][:, 1, :, :], s.k_sums)

            def inverse(i):
                b = i % 2
                for parity in range(2):
                    pe.wait_ge(s.pairs, 2 * i + parity + 1)
                    for c in range(2):
                        for n in range(4):
                            mm = nc.tensor.matmul(m.psum[:, 4 * b + c, parity * N:(parity + 1) * N],
                                                  Fs[b][:, parity, n, c * P:(c + 1) * P], m.inv[:, parity, n, :],
                                                  start=(n == 0), stop=(n == 3))
                        if parity:
                            mm.then_inc(s.inverse, 1)

            for i in range(chunks + 1):
                if i < chunks:
                    filters(i)
                    z_spectrum(i)
                if i:
                    inverse(i - 1)
                if i < chunks:
                    filter_spectrum(i)

        @block.scalar
        def _(act):
            for i in range(chunks):
                b = i % 2
                for x in range(2):
                    act.wait_ge(s.decayed, 2 * i + x + 1)
                    nc.scalar.activation(As[b][:, x, :, :], Fs[b][:, x, :, :], ACT.Abs).then_inc(s.absed, 1)
                act.wait_ge(s.z_flip, i + 1)
                nc.scalar.activation(vts[b][:, :, :], slots[b][:, 0:4, :], ACT.Copy).then_inc(s.z_out, 1)
                for sums, odd in ((s.u_sums, s.u_odd), (s.k_sums, s.k_odd)):
                    for w in range(2):
                        act.wait_ge(sums, 2 * i + w + 1)
                        nc.scalar.activation(Os[b][:, 2 * w:2 * w + 2, :], slots[b][:, 4 + 2 * w:6 + 2 * w, :], ACT.Copy)\
                            .then_inc(odd, 1)

        @block.vector
        def _(dve):
            link = Link(dve, s.v)
            tt = nc.vector.tensor_tensor

            def butterflies(i, out, which, done):
                at = 2 * which
                even, odd = slots[i % 2][:, at:at + 2, :], Os[i % 2][:, at:at + 2, :]
                tt(out[:, which, 0:2, :], even, odd, ALU.add)
                mirror = (odd, even) if which else (even, odd)
                return tt(out[:, which, 2:4, :], mirror[0], mirror[1], ALU.subtract).then_inc(done, 1)

            def decays(i):
                b = i % 2
                F, A = Fs[b], As[b]
                dve.wait_ge(decay_here[b], 16 * (i // 2 + 1))
                for x in range(2):
                    dve.wait_ge(s.raw, 2 * i + x + 1)
                    tt(F[:, x, :, :], slots[b][:, 4 * x:4 * x + 4, :], Os[b][:, :, :], ALU.mult).then_inc(s.decayed, 1)
                if i:
                    multiply_real(i - 1)
                for x in range(2):
                    dve.wait_ge(s.absed, 2 * i + x + 1)
                    link(tt(A[:, x, 0:2, :], A[:, x, 0:2, :], A[:, x, 2:4, :], ALU.add))
                    tt(addeds[b][:, x, :], A[:, x, 0, :], A[:, x, 1, :], ALU.add).then_inc(s.added, 1)
                if i:
                    multiply_imaginary(i - 1, 0)
                dve.wait_ge(s.norms, 2 * i + 2)
                nc.vector.tensor_scalar(rns[b], slots[b][:, 4:6, :], EPS, None, ALU.add).then_inc(s.norms_out, 1)

            def normalise(i):
                b = i % 2
                F, A = Fs[b], As[b]
                dve.wait_ge(s.norms_out, i + 1)
                link(nc.vector.reciprocal(rns[b], rns[b]))
                for x in range(2):
                    link(tt(F[:, x, :, :], F[:, x, :, :], rns[b][:, x, :].unsqueeze(1).broadcast_to([P, TT, N]), ALU.mult))
                link(nc.vector.memset(F[0:1, 1, 0, :], 0.0))
                tt(A[:, 0, :, :], F[:, 0, :, :], F[:, 1, :, :], ALU.add)
                tt(A[:, 1, :, :], F[:, 0, :, :], F[:, 1, :, :], ALU.subtract).then_inc(s.ab, 1)
                dve.wait_ge(s.ab, i + 1)
                for w in range(2):
                    dve.wait_ge(s.u_odd, 2 * i + w + 1)
                    butterflies(i, F, w, s.u_done)

            def multiply_real(i):
                F, A, K, O = (x[i % 2] for x in (Fs, As, Ks, Os))
                dve.wait_ge(s.k_done, 2 * i + 2)
                link(tt(A[:, 0, :, :], F[:, 0, :, :], K[:, 0, :, :], ALU.mult))
                link(tt(O[:, :, :], F[:, 1, :, :], K[:, 1, :, :], ALU.mult))
                link(tt(A[:, 0, :, :], A[:, 0, :, :], O[:, :, :], ALU.subtract))

            def multiply_imaginary(i, part):
                F, A, K, O = (x[i % 2] for x in (Fs, As, Ks, Os))
                if part == 0:
                    link(tt(A[:, 1, :, :], F[:, 0, :, :], K[:, 1, :, :], ALU.mult))
                    return
                link(tt(O[:, :, :], F[:, 1, :, :], K[:, 0, :, :], ALU.mult))
                link(tt(A[:, 1, :, :], A[:, 1, :, :], O[:, :, :], ALU.add))

            def spectrum_pairs(i):
                F, A = Fs[i % 2], As[i % 2]
                tt(F[:, 0, 0:2, :], A[:, 0, 0:2, :], A[:, 0, 2:4, :], ALU.add)
                tt(F[:, 0, 2:4, :], A[:, 1, 0:2, :], A[:, 1, 2:4, :], ALU.subtract).then_inc(s.pairs, 1)
                tt(F[:, 1, 0:2, :], A[:, 0, 0:2, :], A[:, 0, 2:4, :], ALU.subtract)
                tt(F[:, 1, 2:4, :], A[:, 1, 0:2, :], A[:, 1, 2:4, :], ALU.add).then_inc(s.pairs, 1)

            def gate(i):
                order, part = divmod(i, per_order)
                for c in range(2):
                    t = 2 * part + c
                    dve.wait_ge(s.inverse, 2 * i + c + 1)
                    y = Os[i % 2][:, 2 * c:2 * c + 2, :].rearrange("p k n -> p (k n)")
                    link(nc.vector.scalar_tensor_tensor(y, m.xv[:, 16 + t, :], m.param("hy_filt_bias", 1, 8 * order + t),
                                                        m.psum[:, 4 * (i % 2) + c, :], ALU.mult, ALU.add))
                    last = tt(m.xv[:, 16 + t, :], y, m.xv[:, 8 * order + t, :], ALU.mult)
                last.then_inc(s.gated, 1)

            for i in range(chunks + 1):
                if i < chunks:
                    decays(i)
                if i == chunks:
                    multiply_real(i - 1)
                    multiply_imaginary(i - 1, 0)
                if i:
                    multiply_imaginary(i - 1, 1)
                    spectrum_pairs(i - 1)
                if i < chunks:
                    normalise(i)
                if i:
                    gate(i - 1)
                if i < chunks:
                    for w in range(2):
                        dve.wait_ge(s.k_odd, 2 * i + w + 1)
                        butterflies(i, Ks[i % 2], w, s.k_done)


def phase_project(nc, m, ph, ring, d, layer, following):
    n = 16
    with ExitStack() as ctx:
        block, s, stale = ph.open(ctx, *NORM_SEMS, "v", "read_out")
        m.F = on_chip(nc, ctx, "norm_tiles", [P, 4, S], F32)

        @block.sync
        def _(sp):
            sp.sem_clear(stale)
            ring.stream(sp, d.w_proj[layer], n, following)

        @block.gpsimd
        def _(pool):
            ring.make_lows(pool, n)

        @block.tensor
        def _(pe):
            norm_pe(nc, pe, m, s)
            pe.wait_ge(s.root, 1)
            streamed_products(nc, pe, ring, 14, m.Hs, m.psum, s.read_out, k_ready=h_tiles(pe, s))
            for u in (14, 15):
                w = [x.rearrange("p (k m) -> p k m", k=KC) for x in ring.parts(pe, u)]
                pe.wait_ge(s.read_out, 14)
                for t in range(TT):
                    for k in range(KC):
                        mm = split_matmul(nc, m.psum[:, 4 * (u - 14) + t, 0:256], [x[:, k, t * P:(t + 1) * P] for x in m.Hs],
                                          [x[:, k, :] for x in w], k == 0, k == KC - 1)
                mm.then_inc(ring.used, 1)

        @block.scalar
        def _(act):
            norm_act(nc, act, m, s, m.X, ring=ring)
            for u in range(14):
                ring.products(act, u)
                func = ACT.Silu if u in (2, 3) else ACT.Sigmoid if u >= 12 else ACT.Copy
                b = 2 * u % BANKS
                nc.scalar.activation(m.raw[:, 2 * u:2 * u + 2, :], m.psum[:, b:b + 2, :], func).then_inc(s.read_out, 1)
                ring.make_high(act, u + 2)
            for u in (14, 15):
                ring.products(act, u)
                nc.scalar.activation(m.vr[:, :, 256 * (u - 14):256 * (u - 13)],
                                     m.psum[:, 4 * (u - 14):4 * (u - 14) + 4, 0:256], ACT.Copy)
                if u < n - 1:
                    ring.make_high(act, u + 2)

        @block.vector
        def _(dve):
            link = Link(dve, s.v)
            norm_dve(nc, dve, m, s, link, m.X, m.param("mix_pre", KC, layer * KC))
        ring.first += n


RAW_Q, RAW_K, RAW_G, RAW_SB, RAW_SC, RAW_SX, RAW_CA, RAW_CB = 0, 2, 4, 8, 12, 16, 20, 24


def phase_retention(nc, m, ph, ring, d, layer):
    with ExitStack() as ctx:
        block, s, stale = ph.open(ctx, "here", "rotary", "rot", "qk", "v", "scores", "decayed", "outs", "copied", "means", "centred",
                                  "squares", "variances", "root", "inv", "spread")
        middle = NORM_ROWS[-1] - 1
        rows = m.root[0:RET_HEADS, :]
        dec = on_chip(nc, ctx, "ret_decay", [P, RET_HEADS, S], F32)
        ST = on_chip(nc, ctx, "scores", [P, 2, TT, S], F32)
        OR = on_chip(nc, ctx, "head_out", [P, RET_HEADS, S], F32)
        sb, sc, sx = (m.raw[:, k:k + 4, :] for k in (RAW_SB, RAW_SC, RAW_SX))
        c_sw = layer * SC_K * 4
        tab = OR[:, 0:2, :]
        qk = m.raw[:, RAW_Q:RAW_K + 2, :]

        @block.sync
        def _(sp):
            sp.sem_clear(stale)
            sp.dma_start(tab[:, :, :], d.ret_rotary).then_inc(s.rotary, 16)
            sp.dma_start(dec[:, :, :], d.ret_decay).then_inc(s.here, 16)
            sp.wait_ge(s.here, 16)

        @block.tensor
        def _(pe):
            for j in range(4):
                mm = nc.tensor.matmul(m.psum[:, j, :], m.const("rot"), qk[:, j, :], start=True, stop=True)
            mm.then_inc(s.rot, 1)
            pe.wait_ge(s.qk, 1)
            for h in range(RET_HEADS):
                side, t = slice(64 * (h % 2), 64 * (h % 2) + 64), h // 2
                if h:
                    pe.wait_ge(s.decayed, TT * h)
                for i in range(TT):
                    nc.tensor.matmul(m.psum[:, 4 + i, 0:S - i * P], m.raw[side, RAW_K + t, i * P:(i + 1) * P],
                                     m.raw[side, RAW_Q + t, i * P:S], start=True, stop=True).then_inc(s.scores, 1)
                for i in range(TT):
                    pe.wait_ge(s.decayed, TT * h + i + 1)
                    mm = nc.tensor.matmul(m.psum[:, h, i * P:S], m.vr[:, i, h * P:(h + 1) * P],
                                          ST[:, h % 2, i, 0:S - i * P], start=(i == 0), stop=(i == TT - 1))
                mm.then_inc(s.outs, 1)
            pe.wait_ge(s.copied, RET_HEADS)
            for h in range(RET_HEADS):
                mm = nc.tensor.matmul(m.psum[:, h, :], m.const("ones"), OR[:, h, :], start=True, stop=True)
            mm.then_inc(s.means, 1)
            pe.wait_ge(s.squares, 1)
            for h in range(RET_HEADS):
                mm = nc.tensor.matmul(m.psum[0:RET_HEADS, 4, :], m.const("pick_one")[:, middle - h:middle - h + RET_HEADS],
                                      ST[:, 0, h, :], start=(h == 0), stop=(h == RET_HEADS - 1))
            mm.then_inc(s.variances, 1)
            pe.wait_ge(s.inv, 1)
            for h in range(RET_HEADS):
                mm = nc.tensor.matmul(m.psum[:, h, :], m.const("ident")[0:RET_HEADS, h:h + 1].broadcast_to([RET_HEADS, P]),
                                      rows, start=True, stop=True)
            mm.then_inc(s.spread, 1)

        @block.vector
        def _(dve):
            link = Link(dve, s.v)
            tt = nc.vector.tensor_tensor
            wide = lambda x: x.unsqueeze(1).broadcast_to([P, 4, S])
            link(tt(sx, sc, sx, ALU.mult))
            for j in range(4):
                last = nc.vector.tensor_scalar(sc[:, j, :], sx[:, j, :], m.param("sc_w", 1, c_sw + 8 + j), None, ALU.mult)
            link(last)
            dve.wait_ge(s.rotary, 16)
            dve.wait_ge(s.rot, 1)
            tt(ST[:, 0, :, :], m.psum[:, 0:4, :], wide(tab[:, 1, :]), ALU.mult)
            link(tt(qk, qk, wide(tab[:, 0, :]), ALU.mult))
            tt(qk, qk, ST[:, 0, :, :], ALU.add).then_inc(s.qk, 1)
            dve.wait_ge(s.qk, 1)
            dve.wait_ge(s.here, 16)
            for h in range(RET_HEADS):
                for i in range(TT):
                    dve.wait_ge(s.scores, TT * h + i + 1)
                    if h >= 2 and i == 0:
                        dve.wait_ge(s.outs, h - 1)
                    tt(ST[:, h % 2, i, 0:S - i * P], m.psum[:, 4 + i, 0:S - i * P], dec[:, h, 0:S - i * P], ALU.mult)\
                        .then_inc(s.decayed, 1)
            for k in (1, 0):
                lag = SC_K - 1 - k
                for j in range(4):
                    last = nc.vector.scalar_tensor_tensor(sc[:, j, lag:], sx[:, j, 0:S - lag], m.param("sc_w", 1, c_sw + 4 * k + j),
                                                          sc[:, j, lag:], ALU.mult, ALU.add)
                link(last)
            dve.wait_ge(s.means, 1)
            nc.vector.scalar_tensor_tensor(flat(OR[:, :, :]), flat(m.psum[:, 0:4, :]), -1.0 / RET_V, flat(OR[:, :, :]),
                                           ALU.mult, ALU.add).then_inc(s.centred, 1)
            tt(sb, sb, sc, ALU.mult)
            dve.wait_ge(s.root, 1)
            nc.vector.reciprocal(rows, rows).then_inc(s.inv, 1)
            dve.wait_ge(s.spread, 1)
            link(tt(OR[:, :, :], OR[:, :, :], m.psum[:, 0:4, :], ALU.mult))
            tt(m.raw[:, RAW_G:RAW_G + 4, :], m.raw[:, RAW_G:RAW_G + 4, :], OR[:, :, :], ALU.mult)

        @block.scalar
        def _(act):
            for h in range(RET_HEADS):
                act.wait_ge(s.outs, h + 1)
                nc.scalar.activation(OR[:, h, :], m.psum[:, h, :], ACT.Copy).then_inc(s.copied, 1)
            act.wait_ge(s.centred, 1)
            nc.scalar.activation(ST[:, 0, :, :], OR[:, :, :], ACT.Square).then_inc(s.squares, 1)
            act.wait_ge(s.variances, 1)
            nc.scalar.activation(rows, m.psum[0:RET_HEADS, 4, :], ACT.Sqrt,
                                 bias=m.const("eps")[0:RET_HEADS, :]).then_inc(s.root, 1)


def flat(x):
    return x.rearrange("p t n -> p (t n)")


def phase_branches(nc, m, ph, ring, d, layer, following):
    steps = 6
    n = 3 * steps
    with ExitStack() as ctx:
        block, s, stale = ph.open(ctx, "pads", "glu", "v", "sigmoids", "merged", "b_value", "b_high", "b_ready",
                                  "conv", "means", "means_out", "centred", "squares", "variances", "root", "scaled")
        GP = on_chip(nc, ctx, "long_in", [P, 4, S + CF_K - 1], F32)
        Bh = on_chip(nc, ctx, "branch_high", [P, 4, S], F32R)
        Bl = on_chip(nc, ctx, "branch_low", [P, 4, S], F32R)
        sg, sb, sc, sx, ca, cb = (m.raw[:, k:k + 4, :] for k in (RAW_G, RAW_SB, RAW_SC, RAW_SX, RAW_CA, RAW_CB))
        gate = cb
        branch = (sg, sb, ca)
        c_cw = PCOL["cf_w"] + layer * CF_K * 4
        chunk = (CF_K - 1) // 3

        @block.sync
        def _(sp):
            sp.sem_clear(stale)
            ring.stream(sp, d.w_branches[layer], n, following)

        @block.gpsimd
        def _(pool):
            nc.gpsimd.memset(GP[:, :, 0:CF_K - 1], 0.0).then_inc(s.pads, 1)
            ring.make_lows(pool, n)

        @block.tensor
        def _(pe):
            for i in range(steps):
                for j in range(2):
                    if i:
                        pe.wait_ge(s.sigmoids, 2 * (i - 1) + j + 1)
                    unit_products(nc, pe, ring, 3 * i + j, m.Hs, m.psum, banks=(2 * j, 2 * j + 1))
                    if i == 3 and j == 1:
                        pe.wait_ge(s.conv, 1)
                        pe.wait_ge(s.merged, 3)
                        for c in range(4):
                            mm = nc.tensor.matmul(m.psum[:, 4, :], m.const("ones"), ca[:, c, :], start=(c == 0), stop=(c == 3))
                        mm.then_inc(s.means, 1)
                    if i == 4 and j == 0:
                        pe.wait_ge(s.squares, 1)
                        pe.wait_ge(s.merged, 4)
                        for c in range(4):
                            mm = nc.tensor.matmul(m.psum[:, 5, :], m.const("ones"), sc[:, c, :], start=(c == 0), stop=(c == 3))
                        mm.then_inc(s.variances, 1)
                if i % 2 == 0:
                    pe.wait_ge(s.b_ready, i // 2 + 1)
                if i:
                    pe.wait_ge(s.merged, i)
                if i == 3:
                    pe.wait_ge(s.means_out, 1)
                if i == 4:
                    pe.wait_ge(s.root, 1)
                unit_products(nc, pe, ring, 3 * i + 2, (Bh, Bl), m.psum, kc=4, tiles=4, banks=(4, 5, 6, 7))

        @block.scalar
        def _(act):
            def high(b):
                act.wait_ge(s.b_value, b + 1)
                if b:
                    ring.products(act, 6 * b - 1)
                nc.scalar.activation(Bh[:, :, :], branch[b], ACT.Copy).then_inc(s.b_high, 1)

            high(0)
            ring.make_high(act, 1)
            act.wait_ge(s.glu, 1)
            for i in range(steps):
                for j in range(2):
                    u = 3 * i + j
                    ring.products(act, u)
                    if i and j == 0:
                        act.wait_ge(s.merged, i)
                    nc.scalar.activation(gate[:, 2 * j:2 * j + 2, :], m.psum[:, 2 * j:2 * j + 2, :], ACT.Sigmoid)\
                        .then_inc(s.sigmoids, 1)
                    ring.make_high(act, u + 2)
                    if i == 4 and j == 0:
                        act.wait_ge(s.variances, 1)
                        nc.scalar.activation(m.root[:, :], m.psum[:, 5, :], ACT.Sqrt, bias=m.const("eps"), scale=1.0 / MIX)\
                            .then_inc(s.root, 1)
                        act.wait_ge(s.scaled, 1)
                        for c in range(4):
                            nc.scalar.activation(ca[:, c, :], ca[:, c, :], ACT.Silu, scale=m.param("cf_g", 1, 4 * layer + c),
                                                 bias=m.param("cf_lb", 1, 4 * layer + c)).then_inc(s.b_value, 1)
                        act.wait_ge(s.b_value, 6)
                        ring.products(act, 11)
                        nc.scalar.activation(Bh[:, :, :], ca, ACT.Copy).then_inc(s.b_high, 1)
                if i == 1:
                    ring.products(act, 5)
                    high(1)
                if i == 3:
                    act.wait_ge(s.centred, 1)
                    nc.scalar.activation(sc, ca, ACT.Square).then_inc(s.squares, 1)
                if i < steps - 1:
                    ring.make_high(act, 3 * i + 4)

        @block.vector
        def _(dve):
            link = Link(dve, s.v)
            tt, stt = nc.vector.tensor_tensor, nc.vector.scalar_tensor_tensor
            col = lambda c: m.PT[:, bass.ds(c, 1)]

            def low(b):
                dve.wait_ge(s.b_high, b + 1)
                low_part(nc, Bl[:, :, :], branch[b], Bh[:, :, :]).then_inc(s.b_ready, 1)

            def merge(i):
                dve.wait_ge(s.sigmoids, 2 * i + 2)
                ring.products(dve, 3 * i + 2)
                out = m.merged[:, 4 * (i % 2):4 * (i % 2) + 4, :]
                if i < 2:
                    tt(out, gate, m.psum[:, 4:8, :], ALU.mult).then_inc(s.merged, 1)
                else:
                    link(tt(gate, gate, m.psum[:, 4:8, :], ALU.mult))
                    tt(out, out, gate, ALU.add).then_inc(s.merged, 1)

            def taps(first):
                base = link.n
                with dve.Fori(0, chunk) as k:
                    for j in range(4):
                        dve.wait_ge(s.v, k * 4 + (base + j - 3))
                        stt(ca[:, j, :], GP[:, j, bass.ds(k + first, S)], col(k * 4 + (c_cw + 4 * first + j)),
                            ca[:, j, :], ALU.mult, ALU.add).then_inc(s.v, 1)
                link.n += 4 * chunk
                dve.wait_ge(s.v, link.n)

            nc.vector.memset(m.conv_end[:, :], 0.0).then_inc(s.b_value, 2)
            dve.wait_ge(s.pads, 1)
            link(tt(GP[:, :, CF_K - 1:], ca, cb, ALU.mult))
            nc.vector.memset(m.conv_end[:, :], 0.0).then_inc(s.glu, 1)
            low(0)
            for j in range(4):
                link(nc.vector.tensor_scalar(ca[:, j, :], GP[:, j, CF_K - 1:], col(c_cw + 120 + j),
                                             m.param("cf_b", 1, 4 * layer + j), ALU.mult, ALU.add))
            taps(0)
            for i in range(steps):
                if i == 3:
                    dve.wait_ge(s.means, 1)
                    nc.vector.tensor_scalar(m.root[:, :], m.psum[:, 4, :], -1.0 / MIX, None, ALU.mult)\
                        .then_inc(s.means_out, 1)
                    dve.wait_ge(s.means_out, 1)
                    tt(ca, ca, m.root[:, :].unsqueeze(1).broadcast_to([P, 4, S]), ALU.add).then_inc(s.centred, 1)
                merge(i)
                if i == 1:
                    low(1)
                if i < 2:
                    taps((i + 1) * chunk)
                if i == 1:
                    nc.vector.memset(m.conv_end[:, :], 0.0).then_inc(s.conv, 1)
                if i == 3:
                    dve.wait_ge(s.root, 1)
                    link(nc.vector.reciprocal(m.root[:, :], m.root[:, :]))
                    tt(ca, ca, m.root[:, :].unsqueeze(1).broadcast_to([P, 4, S]), ALU.mult).then_inc(s.scaled, 1)
                    low(2)
        ring.first += n


POST_SEMS = ("y_squared", "y_added", "y_sum", "y_root")


def post_norm_pe(nc, pe, m, s, squares):
    pe.wait_ge(s.y_added, KC - 1)
    nc.tensor.matmul(m.psum[:, 0, :], m.const("ones"), squares[:, 0, :], start=True, stop=True).then_inc(s.y_sum, 1)


def post_norm_tile(nc, m, s, c, y, squares, gain):
    nc.scalar.activation(y[:, c, :], m.psum[:, c, :], ACT.Copy, scale=gain[:, c:c + 1])
    nc.scalar.activation(squares[:, c, :], m.psum[:, c, :], ACT.Square).then_inc(s.y_squared, 1)


def post_norm_root(nc, act, m, s):
    act.wait_ge(s.y_sum, 1)
    nc.scalar.activation(m.root[:, :], m.psum[:, 0, :], ACT.Sqrt, bias=m.const("eps"), scale=1.0 / D).then_inc(s.y_root, 1)


def post_norm_dve(nc, dve, m, s, y, squares):
    link = Link(dve, s.v)
    for c in range(1, KC):
        dve.wait_ge(s.y_squared, c + 1)
        if c >= 2:
            dve.wait_ge(s.y_added, c - 1)
        nc.vector.tensor_tensor(squares[:, 0, :], squares[:, 0, :], squares[:, c, :], ALU.add).then_inc(s.y_added, 1)
    dve.wait_ge(s.y_root, 1)
    link(nc.vector.reciprocal(m.root[:, :], m.root[:, :]))
    link(nc.vector.tensor_tensor(y, y, m.root[:, :].unsqueeze(1).broadcast_to([P, KC, S]), ALU.mult))
    nc.vector.tensor_tensor(m.X[:, :, :], m.X[:, :, :], y, ALU.add)


def phase_mix_out(nc, m, ph, ring, d, layer, following):
    n = 4
    with ExitStack() as ctx:
        block, s, stale = ph.open(ctx, *POST_SEMS, "v", "h_high", "h_ready")

        @block.sync
        def _(sp):
            sp.sem_clear(stale)
            ring.stream(sp, d.w_o_2[layer], n, following)

        @block.gpsimd
        def _(pool):
            ring.make_lows(pool, n, following is not None)

        @block.tensor
        def _(pe):
            for u in range(n):
                unit_products(nc, pe, ring, u, m.Hs, m.psum, k_ready=h_tiles(pe, s) if u == 0 else None)
            post_norm_pe(nc, pe, m, s, m.raw)

        @block.scalar
        def _(act):
            for c in range(KC):
                nc.scalar.activation(m.Hh[:, c, :], m.merged[:, c, :], ACT.Copy).then_inc(s.h_high, 1)
            ring.make_high(act, 1)
            act.wait_ge(s.h_ready, KC)
            for u in range(n):
                ring.products(act, u)
                for c in (2 * u, 2 * u + 1):
                    post_norm_tile(nc, m, s, c, m.merged, m.raw, m.param("mix_post", KC, layer * KC))
                if u < n - 1:
                    ring.make_high(act, u + 2)
            post_norm_root(nc, act, m, s)

        @block.vector
        def _(dve):
            for c in range(KC):
                dve.wait_ge(s.h_high, c + 1)
                low_part(nc, m.Hl[:, c, :], m.merged[:, c, :], m.Hh[:, c, :]).then_inc(s.h_ready, 1)
            post_norm_dve(nc, dve, m, s, m.merged[:, :, :], m.raw)
        ring.first += n


def phase_ffn_up(nc, m, ph, ring, d, layer, following):
    n = FF_TILES
    with ExitStack() as ctx:
        block, s, stale = ph.open(ctx, *NORM_SEMS, "v", "last_tap", "read_out", "silu", "f_value", "f_high", "f_low")
        T = m.F[:, :, :].rearrange("p (a j) n -> p a j n", a=2)
        w0 = PCOL["ffn_w"] + layer * FFN_K * 2 * FF_TILES

        def tile_of(x, u, turn):
            return x[:, bass.ds(turn * TURN + u, 1), :].rearrange("p a n -> p (a n)")

        @block.sync
        def _(sp):
            sp.sem_clear(stale)
            ring.stream(sp, d.w_up[layer], n, following)

        @block.gpsimd
        def _(pool):
            ring.make_lows(pool, n)

        @block.tensor
        def _(pe):
            norm_pe(nc, pe, m, s)
            pe.wait_ge(s.root, 1)
            streamed_products(nc, pe, ring, n, m.Hs, m.psum, s.read_out, k_ready=h_tiles(pe, s))

        def tap(u, turn, j, k):
            return m.PT[:, bass.ds(turn * TURN + (w0 + k * 2 * FF_TILES + j * FF_TILES + u), 1)]

        @block.scalar
        def _(act):
            norm_act(nc, act, m, s, m.X, ring=ring)
            act.sem_inc(s.f_low, 2)

            def body(u, turn):
                ring.products(act, u, turn)
                act.wait_ge(s.f_low, turn * TURN + (u + 1))
                for j in range(2):
                    b = (2 * u + j) % BANKS
                    last = nc.scalar.activation(T[:, u % 2, j, :], m.psum[:, b, :], ACT.Copy, scale=tap(u, turn, j, 2))
                last.then_inc(s.last_tap, 1)
                if u < n - 1:
                    ring.make_high(act, u + 2, turn)
                act.wait_ge(s.read_out, turn * TURN + (u + 1))
                nc.scalar.activation(T[:, u % 2, 0, :], T[:, u % 2, 0, :], ACT.Silu).then_inc(s.silu, 1)
                act.wait_ge(s.f_value, turn * TURN + (u + 1))
                nc.scalar.activation(tile_of(m.ffs[0], u, turn), T[:, u % 2, 1, :], ACT.Copy).then_inc(s.f_high, 1)
            over_units(act, n, body)

        @block.vector
        def _(dve):
            link = Link(dve, s.v)
            norm_dve(nc, dve, m, s, link, m.X, m.param("ffn_pre", KC, layer * KC))
            base = link.n

            def body(u, turn):
                dve.wait_ge(s.last_tap, turn * TURN + (u + 1))
                chain = Link(dve, s.v, turn * TURN + (base + u))
                t = T[:, u % 2, :, :]
                for k in (1, 0):
                    for j in range(2):
                        b = (2 * u + j) % BANKS
                        lag = FFN_K - 1 - k
                        last = nc.vector.scalar_tensor_tensor(t[:, j, lag:], m.psum[:, b, 0:S - lag], tap(u, turn, j, k),
                                                              t[:, j, lag:], ALU.mult, ALU.add)
                    if k:
                        chain(last)
                last.then_inc(s.read_out, 1)
                dve.wait_ge(s.silu, turn * TURN + (u + 1))
                nc.vector.tensor_tensor(t[:, 1, :], t[:, 0, :], t[:, 1, :], ALU.mult).then_inc(s.f_value, 1)
                dve.wait_ge(s.f_high, turn * TURN + (u + 1))
                low_part(nc, tile_of(m.ffs[1], u, turn), t[:, 1, :], tile_of(m.ffs[0], u, turn)).then_inc(s.f_low, 1)
            over_units(dve, n, body)
        ring.first += n


def phase_ffn_down(nc, m, ph, ring, d, layer, following):
    n = FF_TILES // 2
    with ExitStack() as ctx:
        block, s, stale = ph.open(ctx, *POST_SEMS, "v", "tile_done")
        y = on_chip(nc, ctx, "y", [P, KC, S], F32)
        squares = on_chip(nc, ctx, "y_squares", [P, KC, S], F32)

        @block.sync
        def _(sp):
            sp.sem_clear(stale)
            ring.stream(sp, d.w_down[layer], n, following)

        @block.gpsimd
        def _(pool):
            ring.make_lows(pool, n, following is not None)

        @block.tensor
        def _(pe):
            def unit(u, turn):
                w = [x.rearrange("p (k m) -> p k m", k=2) for x in ring.parts(pe, u, turn)]
                rhs = [[x[:, bass.ds(turn * 2 * TURN + (2 * u + k), 1), :].rearrange("p a n -> p (a n)") for x in m.ffs]
                       for k in range(2)]
                order = [(k, t) for k in range(2) for t in range(KC)]
                if u == n - 1:
                    order = [(k, t) for t in range(KC) for k in range(2)]
                for k, t in order:
                    mm = split_matmul(nc, m.psum[:, t, :], [x[:, k, t * P:(t + 1) * P] for x in w], rhs[k],
                                      u == 0 and k == 0, u == n - 1 and k == 1)
                    if u == n - 1 and k == 1 and t < KC - 1:
                        mm.then_inc(s.tile_done, 1)
                mm.then_inc(ring.used, 1)

            unit(0, 0)
            turns = (n - 2) // TURN
            with pe.Fori(0, turns) as i:
                for k in range(TURN):
                    unit(1 + k, i)
            for u in range(1 + turns * TURN, n):
                unit(u, 0)
            post_norm_pe(nc, pe, m, s, squares)

        @block.scalar
        def _(act):
            ring.make_high(act, 1)
            over_units(act, n - 1 if following is not None else n - 2, lambda u, turn: ring.make_high(act, u + 2, turn))
            for c in range(KC):
                if c < KC - 1:
                    act.wait_ge(s.tile_done, c + 1)
                else:
                    ring.products(act, n - 1)
                post_norm_tile(nc, m, s, c, y, squares, m.param("ffn_post", KC, layer * KC))
            post_norm_root(nc, act, m, s)

        @block.vector
        def _(dve):
            post_norm_dve(nc, dve, m, s, y[:, :, :], squares)
        ring.first += n


def phase_store(nc, m, ph, ring, d):
    with ExitStack() as ctx:
        block, s, stale = ph.open(ctx, "stored")

        @block.sync
        def _(sp):
            sp.dma_start(d.out, m.X[:, :, :]).then_inc(s.stored, 16)
            sp.wait_ge(s.stored, 16)


def build(nc, d, upto=99):
    with ExitStack() as whole:
        def sb(ctx, name, shape, dtype=F32):
            return on_chip(nc, ctx, name, shape, dtype)

        m = Memory()
        m.X = sb(whole, "x", [P, KC, S])
        m.PT = sb(whole, "params", [P, PCOLS])
        m.CT = sb(whole, "consts", [P, CCOLS])
        m.WRh = sb(whole, "router_high", [P, DEPTH, KC, GROUPS + EXPERTS], F32R)
        m.WRl = sb(whole, "router_low", [P, DEPTH, KC, GROUPS + EXPERTS], F32R)
        m.RB = sb(whole, "router_b", [P, DEPTH, GROUPS + EXPERTS])
        m.mod = sb(whole, "mod", [P, DEPTH * 48])
        m.gain = sb(whole, "gain", [P, DEPTH, 2, KC])
        m.root = sb(whole, "root", [P, S])
        m.priority = sb(whole, "priority", [P, TT, 4])
        m.conv_end = sb(whole, "conv_end", [P, 1])
        m.psum = whole.enter_context(nc.psum_tensor("psum", [P, BANKS, S], F32))
        ring = Ring(nc, whole)
        ph = Phases(nc)
        m.const = lambda name: m.CT[:, CCOL[name]:CCOL[name] + dict(CONST_TILES)[name]]
        m.param = lambda name, n, at=0: m.PT[:, PCOL[name] + at:PCOL[name] + at + n]

        def mod(layer, k):
            return m.mod[:, 48 * layer + KC * k:48 * layer + KC * (k + 1)]

        def operand(ctx, name, tiles):
            return sb(ctx, name + "_high", [P, tiles, S], F32R), sb(ctx, name + "_low", [P, tiles, S], F32R)

        def give_h(ctx):
            m.Hs = m.Hh, m.Hl = operand(ctx, "h", KC)

        def moe(layer, following, modulation=None):
            with ExitStack() as part:
                give_h(part)
                m.cb = sb(part, "expert_weights", [P, EXPERTS, S])
                phase_moe(nc, m, ph, ring, layer, mod(layer, 3), m.gain[:, layer, 1, :], d.moe[layer], mod(layer, 5),
                          following, modulation)

        def finish():
            phase_store(nc, m, ph, ring, d)

        with ExitStack() as early:
            m.c_act = sb(early, "c_act", [P, D])
            with ExitStack() as part:
                m.sin, m.cos = sb(part, "rope_sin", [P, S]), sb(part, "rope_cos", [P, S])
                m.k_pe = sb(part, "k_pe", [P, S])
                m.qn, m.kn = sb(part, "q_nope", [P, HEADS, S]), sb(part, "k_nope", [P, HEADS, S])
                m.qp, m.vt = sb(part, "q_pe", [P, 4, S]), sb(part, "v_tok", [P, TT, D])
                phase_load(nc, m, ph, ring, d)
                with ExitStack() as inner:
                    m.lat = sb(inner, "latents", [P, 4, S])
                    m.lat_h, m.lat_l = operand(inner, "latents", 3)
                    with ExitStack() as narrow:
                        give_h(narrow)
                        m.F = m.sq4 = sb(narrow, "norm_tiles", [P, 4, S])
                        m.r4 = sb(narrow, "r4", [P, 3, S])
                        phase_latents(nc, m, ph, ring, d, d.mla_w_heads)
                    m.sq8 = sb(inner, "sq8", [P, 2, 4, S])
                    phase_heads(nc, m, ph, ring, d, d.mla_w_o)
                give_h(part)
                phase_attention(nc, m, ph, ring, d)
                phase_residual(nc, m, ph, ring, d.mla_w_o, mod(0, 2), d.moe[0],
                               mod_units=d.ada_w[MOD_UNITS - MOD_REST:MOD_UNITS, :, :])
            if upto == 0:
                return finish()
            moe(0, d.hy_w_in, d.ada_w[MOD_UNITS:2 * MOD_UNITS, :, :])
        if upto == 1:
            return finish()
        with ExitStack() as part:
            m.xv = sb(part, "x1_x2_v", [P, 24, S])
            with ExitStack() as inner:
                m.hdn = sb(inner, "filter_hidden", [FILTER_WIDTH, S])
                m.fwd, m.inv = sb(inner, "dft_fwd", [P, 2, TT, 256]), sb(inner, "dft_inv", [P, 2, 4, 256])
                with ExitStack() as narrow:
                    give_h(narrow)
                    m.F = sb(narrow, "norm_tiles", [P, 4, S])
                    phase_hyena_in(nc, m, ph, ring, d, d.hy_w_out)
                phase_long_convs(nc, m, ph, ring, d)
            give_h(part)
            phase_residual(nc, m, ph, ring, d.hy_w_out, mod(1, 2), d.moe[1], z=m.xv[:, 16:24, :])
        if upto == 2:
            return finish()
        moe(1, d.w_proj[0])
        if upto == 3:
            return finish()
        for layer in range(DEPTH):
            with ExitStack() as part:
                give_h(part)
                m.raw = sb(part, "projections", [P, 28, S])
                with ExitStack() as inner:
                    m.vr = sb(inner, "v_tok", [P, TT, MIX])
                    phase_project(nc, m, ph, ring, d, layer, d.w_branches[layer])
                    phase_retention(nc, m, ph, ring, d, layer)
                m.merged = sb(part, "merged", [P, KC, S])
                phase_branches(nc, m, ph, ring, d, layer, d.w_o_2[layer])
                phase_mix_out(nc, m, ph, ring, d, layer, d.w_up[layer])
            if upto == 4 + 2 * layer:
                return finish()
            with ExitStack() as part:
                m.ffs = operand(part, "ff", FF_TILES)
                with ExitStack() as inner:
                    give_h(inner)
                    m.F = sb(inner, "norm_tiles", [P, 4, S])
                    phase_ffn_up(nc, m, ph, ring, d, layer, d.w_down[layer])
                phase_ffn_down(nc, m, ph, ring, d, layer, d.w_proj[1] if layer == 0 else None)
            if upto == 5 + 2 * layer:
                return finish()
        finish()


def table_consts():
    f = np.float32
    parts = {"ident": np.eye(P), "ones": np.ones((P, P)), "ones64": np.kron(np.eye(2), np.ones((64, 64)))}
    rot = np.zeros((P, P))
    for b in (0, 64):
        for j in range(32):
            rot[b + 32 + j, b + j] = -1
            rot[b + j, b + 32 + j] = 1
    parts["rot"] = rot
    middle = NORM_ROWS[-1] - 1
    parts["pick_one"], parts["pick_two"] = np.zeros((P, 2 * middle + 1)), np.zeros((P, 2 * middle + 1))
    pe_rows = np.zeros((NORM_ROWS[-1], 4 * P))
    pe_rows[NORM_ROWS[2] + np.arange(4 * P) // ROPE, np.arange(4 * P)] = 1
    parts["pick_one"][:, middle] = 1.0 / NOPE
    parts["pick_two"][:ROPE, middle] = parts["pick_two"][ROPE:, middle + 1] = 1.0 / ROPE
    parts["inv_freq"] = (f(1) / (f(10000.0) ** (np.arange(0, 64, 2, dtype=f) / f(64))))[np.arange(P) % 32][:, None]
    parts["eps"] = np.full((P, 1), EPS)
    parts["zero"] = np.zeros((P, 1))
    consts = np.concatenate([parts[name].astype(f) for name, _ in CONST_TILES], axis=1)

    order = np.concatenate([np.arange(0, S, 2), np.arange(1, S, 2)])
    t = np.linspace(0.0, 1.0, S, dtype=f)[:, None]
    w = (f(2.0 * math.pi) * np.arange(S, dtype=f)[:, None] / f(S)).astype(f)
    fr = np.linspace(1e-4, 15, 16, dtype=f)[None, :]
    z = np.concatenate([t, np.cos(fr * w), -np.sin(fr * w)], axis=-1).astype(f)
    deltas = np.abs(np.linspace(math.log(0.3) / 1e-2, math.log(1.5) / 1e-2, D, dtype=f))
    decay = np.exp(-t * deltas).astype(f)[order].reshape(TT, P, D).transpose(1, 0, 2)
    k = np.arange(256)
    angle = math.pi * (2 * k[None, :] + 1) * order[:, None] / 1024.0
    fwd = np.stack([np.cos(angle), np.sin(angle)]).reshape(2, TT, P, 256).transpose(2, 0, 1, 3)
    back = np.stack([np.cos(angle).T, np.sin(angle).T]) / 512.0
    inv = back.reshape(2, 2, P, 2, 256).transpose(2, 3, 0, 1, 4).reshape(P, 2, 4, 256)

    gamma = 1.0 - np.exp2(-5.0 - np.arange(RET_HEADS))
    lag = np.arange(S)[None, :] - np.arange(P)[:, None]
    ret = np.where(lag[:, None, :] >= 0, gamma[None, :, None] ** np.maximum(lag, 0)[:, None, :], 0.0) / 8.0
    inv_r = f(10000.0) ** (-np.arange(32, dtype=f) / f(32))
    ang = (np.arange(S, dtype=f)[None, :] * inv_r[np.arange(P) % 32][:, None]).astype(f)
    rotary = np.stack([np.cos(ang), np.sin(ang)], axis=1)
    return {name: np.ascontiguousarray(a, dtype=f) for name, a in
            (("consts", consts), ("pe_rows", pe_rows), ("zT", z[order].T), ("decay", decay), ("dft_fwd", fwd), ("dft_inv", inv),
             ("ret_decay", ret), ("ret_rotary", rotary))}


def feature_tiles(a):
    return a.reshape(-1, P).T


def padded_rows(a):
    return np.concatenate([a.T, np.zeros_like(a.T)], axis=0)


def units(w, cols=256):
    k, n = w.shape[0] // P, w.shape[1] // cols
    return w.reshape(k, P, n, cols).transpose(2, 1, 0, 3).reshape(n, P, k * cols)


def layout(i):
    a = {k: np.asarray(v) for k, v in i.items()}
    out = table_consts()
    out["x"] = a["x"][0].T.reshape(KC, P, S).transpose(1, 0, 2)
    out["positions"] = np.broadcast_to(a["positions"].reshape(1, S), (P, S))
    twice = lambda v: np.concatenate([v, v])
    hy = lambda name: a[name][0]
    params = {
        "ada_b": a["ada_b"], "norm_mix_g": a["norm_mix_g"], "norm_ffn_g": a["norm_ffn_g"],
        "q_a_g": a["mla_q_a_g"], "kv_a_g": a["mla_kv_a_g"],
        "q_nope_g": a["mla_q_norm_g"][0, :NOPE], "q_pe_g": twice(a["mla_q_norm_g"][0, NOPE:]),
        "k_nope_g": a["mla_k_norm_g"][0, :NOPE], "k_pe_g": twice(a["mla_k_norm_g"][0, NOPE:]),
        "hy_b_in": hy("hy_b_in"), "hy_conv_w": hy("hy_conv_w"), "hy_conv_b": hy("hy_conv_b"),
        "hy_filt_bias": hy("hy_filt_bias"),
        "mix_pre": a["norm_mix_pre_2"], "mix_post": a["norm_mix_post_2"],
        "ffn_pre": a["norm_ffn_pre_2"], "ffn_post": a["norm_ffn_post_2"],
        "sc_w": a["sc_conv_w_2"], "cf_w": a["cf_conv_w_2"], "cf_b": a["cf_conv_b_2"],
        "cf_g": a["cf_ln_g_2"], "cf_lb": a["cf_ln_b_2"], "ffn_w": a["ffn_conv_w_2"],
    }
    cols = {name: feature_tiles(v) for name, v in params.items()}
    cols["hy_fb"] = padded_rows(np.concatenate([a["hy_f_b1"], a["hy_f_b2"], a["hy_f_b3"]]))
    cols["hy_ff"] = padded_rows(np.concatenate([a["hy_f_freq1"], a["hy_f_freq2"], a["hy_f_freq3"]]))
    out["params"] = np.concatenate([cols[name] for name, _ in PARAM_TILES], axis=1)
    assert out["params"].shape == (P, PCOLS)
    wr = np.concatenate([a["moe_wg"], a["moe_we"]], axis=2)
    out["router_w"] = wr.reshape(DEPTH, KC, P, GROUPS + EXPERTS).transpose(2, 0, 1, 3)
    out["router_b"] = np.broadcast_to(np.concatenate([a["moe_bg"], a["moe_be"]], axis=1)[None], (P, DEPTH, 20))

    out["c"] = np.broadcast_to(a["c"].reshape(1, D), (P, D))
    out["ada_w"] = a["ada_w"].transpose(0, 2, 1).reshape(DEPTH * 24, 2, P, D).transpose(0, 2, 1, 3).reshape(-1, P, 2 * D)
    wd = a["mla_w_down"][0]
    out["mla_w_down"] = units(np.concatenate([wd, wd[:, -ROPE:]], axis=1))
    uq = a["mla_w_uq"][0].reshape(Q_LORA, HEADS, QK_HEAD)
    uq = np.concatenate([uq[:, :, :NOPE].reshape(Q_LORA, -1), uq[:, :, NOPE:].reshape(Q_LORA, -1)], axis=1)
    uq = np.concatenate([uq, np.zeros((Q_LORA, 512), uq.dtype)], axis=1)
    ukv = a["mla_w_ukv"][0].reshape(KV_LORA, HEADS, NOPE + V_HEAD)
    ukv = np.concatenate([ukv[:, :, :NOPE].reshape(KV_LORA, -1), ukv[:, :, NOPE:].reshape(KV_LORA, -1)], axis=1)
    out["mla_w_heads"] = np.concatenate([units(uq, 1024), ukv[None]])
    out["mla_w_o"] = units(a["mla_w_o"][0])
    for l in range(DEPTH):
        g = []
        for k in range(GROUPS):
            for e in range(k * PER_GROUP, (k + 1) * PER_GROUP):
                g += [units(a["moe_w_gate"][l, e]), units(a["moe_w_up"][l, e])]
            g.append(units(a["moe_w_down"][l, k * PER_GROUP:(k + 1) * PER_GROUP].reshape(PER_GROUP * D_EXPERT, D)))
        out[f"moe_{l}"] = np.concatenate(g)
        w = a["w_in_2"][l]
        q, v, r, g = w[:, :512], w[:, 512:1024], w[:, 1024:4096], w[:, 4096:]
        out[f"w_proj_{l}"] = units(np.concatenate([q, r, v], axis=1))
        outs = [units(a[n][l], 512) for n in ("w_ret_out_2", "w_sc_out_2", "w_cf_out_2")]
        g = units(g)
        out[f"w_branches_{l}"] = np.concatenate(
            [x for i in range(6) for x in (g[2 * i:2 * i + 2], outs[i // 2][i % 2:i % 2 + 1])])
        out[f"w_o_2_{l}"] = units(a["w_o_2"][l])
        up = a["w_up_2"][l].reshape(D, 2, FF_TILES, P).transpose(0, 2, 1, 3).reshape(D, -1)
        out[f"w_up_{l}"] = units(up)
        dn = a["w_down_2"][l].reshape(FF_TILES // 2, 2, P, D)
        out[f"w_down_{l}"] = dn.transpose(0, 2, 1, 3).reshape(FF_TILES // 2, P, 2 * D)
    out["hy_w_in"] = units(hy("hy_w_in"))
    out["hy_w_out"] = units(hy("hy_w_out"))
    out["hy_f_w1"], out["hy_f_w2"], out["hy_f_w3"] = hy("hy_f_w1"), hy("hy_f_w2"), hy("hy_f_w3")
    out["hy_f_w4"] = hy("hy_f_w4").reshape(FILTER_WIDTH, 2, 2, D)
    return {k: np.ascontiguousarray(v) for k, v in out.items()}


def declare(nc, arrays):
    found = {}
    for name, v in arrays.items():
        ap = nc.dram_tensor("in_" + name, list(v.shape), mybir.dt.from_np(v.dtype), kind="ExternalInput").ap()
        if name[-2:] in ("_0", "_1"):
            found.setdefault(name[:-2], []).append(ap)
        else:
            found[name] = ap
    found["out"] = nc.dram_tensor("out_x", [P, KC, S], F32, kind="ExternalOutput").ap()
    return namedtuple("Dram", found)(*found.values())


def kernel(**inputs):
    import concourse.bacc as bacc
    from concourse.bass_utils import run_bass_kernel_spmd

    arrays = layout(inputs)
    nc = bacc.Bacc("TRN2", target_bir_lowering=False, num_devices=1)
    build(nc, declare(nc, arrays))
    r = run_bass_kernel_spmd(nc, [{"in_" + k: v for k, v in arrays.items()}], core_ids=[0])
    out = np.asarray(r.results[0]["out_x"])
    return np.ascontiguousarray(out.transpose(1, 0, 2).reshape(D, S).T)[None]
```
